# Optimizing a Trainium2 kernel written in Bass

```python
import math
import jax, jax.numpy as jnp
from jax import lax
import numpy as np

D_MODEL = 1024
BATCH = 1
SEQ = 1024
DEPTH = 1
DEC_BATCH = 8
DEC_SEQ = 1
PAST_LEN = 2048
PAGE_SIZE = 128

D_CONV = D_MODEL
CONV_WIDTH = 3
N_HEADS = 16
N_KV_HEADS = 4
HEAD_DIM = 64
GROUP = N_HEADS // N_KV_HEADS
WINDOW = 128
ATTN_BLOCK = WINDOW
Q_DIM = N_HEADS * HEAD_DIM
KV_DIM = N_KV_HEADS * HEAD_DIM
N_BUCKETS = 32
MAX_DISTANCE = 128
N_EXPERT_GROUPS = 4
EXPERTS_PER_GROUP = 8
N_EXPERTS = N_EXPERT_GROUPS * EXPERTS_PER_GROUP
TOP_K = 2
D_EXPERT = 512
MOE_BLOCK = 128
EPS = 1e-6
IN_OFFSETS = (D_CONV, 2 * D_CONV, 3 * D_CONV, 3 * D_CONV + Q_DIM, 3 * D_CONV + Q_DIM + KV_DIM,
              3 * D_CONV + Q_DIM + 2 * KV_DIM, 3 * D_CONV + Q_DIM + 2 * KV_DIM + D_MODEL)
D_IN = 3 * D_CONV + Q_DIM + 2 * KV_DIM + 2 * D_MODEL

kernel_name = "hybrid_conv_swa_hmoe_decode_step"

def rms_norm(x, g):
    xf = x.astype(jnp.float32)
    y = xf * lax.rsqrt(jnp.mean(xf * xf, axis=-1, keepdims=True) + EPS)
    return (y * g.astype(jnp.float32)).astype(x.dtype)

def t5_bucket(dist):
    n = jnp.maximum(dist, 0)
    max_exact = N_BUCKETS // 2
    nf = jnp.maximum(n, 1).astype(jnp.float32)
    large = max_exact + (jnp.log(nf / max_exact) / math.log(MAX_DISTANCE / max_exact)
                         * (N_BUCKETS - max_exact)).astype(jnp.int32)
    large = jnp.minimum(large, N_BUCKETS - 1)
    return jnp.where(n < max_exact, n, large)

def attend(q, k, v, q_pos, k_pos, rel_bias, sinks):
    lead = q.shape[:-3]
    tq = q.shape[-3]
    tk = k.shape[-3]
    qg = q.reshape(*lead, tq, N_KV_HEADS, GROUP, HEAD_DIM)
    s = jnp.einsum('...qkgd,...skd->...kgqs', qg, k,
                   preferred_element_type=jnp.float32) * (HEAD_DIM ** -0.5)
    dist = q_pos[..., :, None] - k_pos[..., None, :]
    valid = (dist >= 0) & (dist <= WINDOW) & (k_pos[..., None, :] >= 0)
    bias = rel_bias.astype(jnp.float32)[t5_bucket(dist)]
    bias = jnp.moveaxis(bias, -1, -3).reshape(*dist.shape[:-2], N_KV_HEADS, GROUP, tq, tk)
    s = jnp.where(valid[..., None, None, :, :], s + bias, -jnp.inf)
    sink = sinks.astype(jnp.float32).reshape(N_KV_HEADS, GROUP, 1, 1)
    m = jnp.maximum(jnp.max(s, axis=-1, keepdims=True), sink)
    p = jnp.exp(s - m)
    p = p / (jnp.sum(p, axis=-1, keepdims=True) + jnp.exp(sink - m))
    o = jnp.einsum('...kgqs,...skd->...qkgd', p.astype(v.dtype), v)
    return o.reshape(*lead, tq, Q_DIM)

def attn_prompt(q, k, v, rel_bias, sinks):
    b, s = q.shape[:2]
    nb = s // ATTN_BLOCK
    qb = q.reshape(b, nb, ATTN_BLOCK, N_HEADS, HEAD_DIM)

    def band(t):
        t = t.reshape(b, nb, ATTN_BLOCK, N_KV_HEADS, HEAD_DIM)
        prev = jnp.concatenate([jnp.zeros_like(t[:, :1]), t[:, :-1]], axis=1)
        return jnp.concatenate([prev, t], axis=2)

    pos = jnp.arange(s, dtype=jnp.int32).reshape(nb, ATTN_BLOCK)
    k_pos = jnp.concatenate([pos - ATTN_BLOCK, pos], axis=1)
    o = attend(qb, band(k), band(v), pos, k_pos, rel_bias, sinks)
    return o.reshape(b, s, Q_DIM)

def attn_sample(q, k, v, cache_k, cache_v, rel_bias, sinks):
    t = q.shape[1]
    w_buf = cache_k.shape[1]
    k_all = jnp.concatenate([cache_k.astype(k.dtype), k], axis=1)
    v_all = jnp.concatenate([cache_v.astype(v.dtype), v], axis=1)
    q_pos = PAST_LEN + jnp.arange(t, dtype=jnp.int32)
    k_pos = jnp.concatenate([PAST_LEN - w_buf + jnp.arange(w_buf, dtype=jnp.int32), q_pos])
    o = attend(q, k_all, v_all, q_pos, k_pos, rel_bias, sinks)
    return o, k_all[:, -w_buf:], v_all[:, -w_buf:]

def short_conv(u_ext, conv_w):
    t = u_ext.shape[1] - (CONV_WIDTH - 1)
    y = conv_w[0] * u_ext[:, 0:t]
    for j in range(1, CONV_WIDTH):
        y = y + conv_w[j] * u_ext[:, j:j + t]
    return y

def hier_moe(h, w_rg, b_rg, w_re, b_re, w_gate, w_up, w_down):
    lead = h.shape[:-1]
    x = h.reshape(-1, D_MODEL)
    m = x.shape[0]
    g_logits = (x @ w_rg).astype(jnp.float32) + b_rg.astype(jnp.float32)
    g_prob = jax.nn.softmax(g_logits, axis=-1)
    grp = jnp.argmax(g_logits, axis=-1)
    p_grp = jnp.take_along_axis(g_prob, grp[:, None], axis=-1)[:, 0]
    e_logits = ((x @ w_re).astype(jnp.float32) + b_re.astype(jnp.float32)).reshape(
        m, N_EXPERT_GROUPS, EXPERTS_PER_GROUP)
    e_in = jnp.take_along_axis(e_logits, grp[:, None, None], axis=1)[:, 0]
    top_val, top_idx = lax.top_k(e_in, TOP_K)
    w_top = jax.nn.softmax(top_val, axis=-1) * p_grp[:, None]
    expert = grp[:, None] * EXPERTS_PER_GROUP + top_idx
    a = m * TOP_K
    e_flat = expert.reshape(-1)
    t_flat = jnp.repeat(jnp.arange(m, dtype=jnp.int32), TOP_K)
    w_flat = w_top.reshape(-1)
    order = jnp.argsort(e_flat)
    e_s = e_flat[order]
    t_s = t_flat[order]
    counts = jnp.bincount(e_flat, length=N_EXPERTS)
    padded = ((counts + MOE_BLOCK - 1) // MOE_BLOCK) * MOE_BLOCK
    pad_end = jnp.cumsum(padded)
    pad_start = pad_end - padded
    start = jnp.cumsum(counts) - counts
    dest = pad_start[e_s] + (jnp.arange(a, dtype=jnp.int32) - start[e_s])
    n_blocks = -(-a // MOE_BLOCK) + N_EXPERTS
    xs = jnp.zeros((n_blocks * MOE_BLOCK, D_MODEL), x.dtype).at[dest].set(x[t_s])
    block_start = jnp.arange(n_blocks, dtype=jnp.int32) * MOE_BLOCK
    block_expert = jnp.minimum(jnp.searchsorted(pad_end, block_start, side='right'), N_EXPERTS - 1)

    def run_block(args):
        xb, e = args
        return (jax.nn.silu(xb @ w_gate[e]) * (xb @ w_up[e])) @ w_down[e]

    ys = lax.map(run_block, (xs.reshape(n_blocks, MOE_BLOCK, D_MODEL), block_expert))
    ys = ys.reshape(-1, D_MODEL)[dest] * w_flat[order][:, None].astype(x.dtype)
    out = jnp.zeros((m, D_MODEL), x.dtype).at[t_s].add(ys)
    return out.reshape(*lead, D_MODEL)

def decoder_layer(x, conv_hist, attn_fn, norm1_g, w_in, conv_w, w_conv_out, w_attn_out, w_o,
                  norm2_g, w_rg, b_rg, w_re, b_re, w_gate, w_up, w_down):
    b, t = x.shape[:2]
    h = rms_norm(x, norm1_g)
    z = h @ w_in
    cb, cc, ch, q, k, v, ga, gb = jnp.split(z, IN_OFFSETS, axis=-1)
    u_ext = jnp.concatenate([conv_hist.astype(z.dtype), cc * ch], axis=1)
    y_conv = (cb * short_conv(u_ext, conv_w)) @ w_conv_out
    o, k_state, v_state = attn_fn(q.reshape(b, t, N_HEADS, HEAD_DIM),
                                  k.reshape(b, t, N_KV_HEADS, HEAD_DIM),
                                  v.reshape(b, t, N_KV_HEADS, HEAD_DIM))
    y_attn = o @ w_attn_out
    mix = jax.nn.sigmoid(ga) * y_conv + jax.nn.sigmoid(gb) * y_attn
    x = x + mix @ w_o
    x = x + hier_moe(rms_norm(x, norm2_g), w_rg, b_rg, w_re, b_re, w_gate, w_up, w_down)
    return x, u_ext[:, -(CONV_WIDTH - 1):], k_state, v_state

def setup_inputs(seed: int = 0) -> dict:
    key = jax.random.key(seed)
    ks = jax.random.split(key, 24)
    f32 = jnp.float32
    win_buf = min(WINDOW, PAST_LEN)
    nrm = lambda k, shape, scale: jax.random.normal(k, shape, f32) * scale
    return {
        "x_prompt": nrm(ks[0], (BATCH, SEQ, D_MODEL), 1.0),
        "x_sample": nrm(ks[1], (DEC_BATCH, DEC_SEQ, D_MODEL), 1.0),
        "cache_conv": nrm(ks[2], (DEPTH, DEC_BATCH, CONV_WIDTH - 1, D_CONV), 1.0),
        "cache_k": nrm(ks[3], (DEPTH, DEC_BATCH, win_buf, N_KV_HEADS, HEAD_DIM), 1.0),
        "cache_v": nrm(ks[4], (DEPTH, DEC_BATCH, win_buf, N_KV_HEADS, HEAD_DIM), 1.0),
        "norm1_g": 1.0 + nrm(ks[5], (DEPTH, D_MODEL), 0.02),
        "w_in": nrm(ks[6], (DEPTH, D_MODEL, D_IN), D_MODEL ** -0.5),
        "conv_w": nrm(ks[7], (DEPTH, CONV_WIDTH, D_CONV), 0.5),
        "w_conv_out": nrm(ks[8], (DEPTH, D_CONV, D_MODEL), D_CONV ** -0.5),
        "w_attn_out": nrm(ks[9], (DEPTH, Q_DIM, D_MODEL), Q_DIM ** -0.5),
        "w_o": nrm(ks[10], (DEPTH, D_MODEL, D_MODEL), D_MODEL ** -0.5),
        "sinks": nrm(ks[11], (DEPTH, N_HEADS), 0.5),
        "rel_bias": nrm(ks[12], (N_BUCKETS, N_HEADS), 0.5),
        "norm2_g": 1.0 + nrm(ks[13], (DEPTH, D_MODEL), 0.02),
        "w_router_group": nrm(ks[14], (DEPTH, D_MODEL, N_EXPERT_GROUPS), D_MODEL ** -0.5),
        "b_router_group": nrm(ks[15], (DEPTH, N_EXPERT_GROUPS), 0.01),
        "w_router_expert": nrm(ks[16], (DEPTH, D_MODEL, N_EXPERTS), D_MODEL ** -0.5),
        "b_router_expert": nrm(ks[17], (DEPTH, N_EXPERTS), 0.01),
        "w_e_gate": nrm(ks[18], (DEPTH, N_EXPERTS, D_MODEL, D_EXPERT), D_MODEL ** -0.5),
        "w_e_up": nrm(ks[19], (DEPTH, N_EXPERTS, D_MODEL, D_EXPERT), D_MODEL ** -0.5),
        "w_e_down": nrm(ks[20], (DEPTH, N_EXPERTS, D_EXPERT, D_MODEL), D_EXPERT ** -0.5),
        "norm_f_g": 1.0 + nrm(ks[21], (D_MODEL,), 0.02),
    }

def reference(x_prompt, x_sample, cache_conv, cache_k, cache_v, norm1_g, w_in, conv_w,
              w_conv_out, w_attn_out, w_o, sinks, rel_bias, norm2_g, w_router_group,
              b_router_group, w_router_expert, b_router_expert, w_e_gate, w_e_up, w_e_down,
              norm_f_g):
    hp = x_prompt
    hs = x_sample
    win_p = min(WINDOW, x_prompt.shape[1])
    conv_p, kp_l, vp_l, conv_s, ks_l, vs_l = [], [], [], [], [], []
    for l in range(DEPTH):
        weights = (norm1_g[l], w_in[l], conv_w[l], w_conv_out[l], w_attn_out[l], w_o[l],
                   norm2_g[l], w_router_group[l], b_router_group[l], w_router_expert[l],
                   b_router_expert[l], w_e_gate[l], w_e_up[l], w_e_down[l])
        sink_l = sinks[l]

        def prompt_attn(q, k, v, sink_l=sink_l):
            return attn_prompt(q, k, v, rel_bias, sink_l), k[:, -win_p:], v[:, -win_p:]

        def sample_attn(q, k, v, sink_l=sink_l, l=l):
            return attn_sample(q, k, v, cache_k[l], cache_v[l], rel_bias, sink_l)

        zero_hist = jnp.zeros((hp.shape[0], CONV_WIDTH - 1, D_CONV), hp.dtype)
        hp, c_p, k_p, v_p = decoder_layer(hp, zero_hist, prompt_attn, *weights)
        hs, c_s, k_s, v_s = decoder_layer(hs, cache_conv[l], sample_attn, *weights)
        conv_p.append(c_p); kp_l.append(k_p); vp_l.append(v_p)
        conv_s.append(c_s); ks_l.append(k_s); vs_l.append(v_s)
    y_prompt = rms_norm(hp, norm_f_g)
    y_sample = rms_norm(hs, norm_f_g)
    conv_state_prompt = jnp.stack(conv_p)
    k_win_prompt = jnp.stack(kp_l)
    v_win_prompt = jnp.stack(vp_l)
    conv_state_sample = jnp.stack(conv_s)
    k_win_sample = jnp.stack(ks_l)
    v_win_sample = jnp.stack(vs_l)
    return (y_prompt, y_sample, conv_state_prompt, k_win_prompt, v_win_prompt,
            conv_state_sample, k_win_sample, v_win_sample)


_drawn_inputs = setup_inputs


def setup_inputs(seed=0):
    import zlib

    import numpy as np

    out = dict(_drawn_inputs(seed))
    spreads = {}
    factors = {'sinks': 8.0, 'b_router_group': 64.0, 'b_router_expert': 4.234, 'norm_f_g': 7.55}
    for name, (base, spread) in spreads.items():
        noise = np.random.default_rng([zlib.crc32(name.encode()), seed]).standard_normal(out[name].shape)
        drawn = base * np.exp(spread * noise) if base else spread * noise
        out[name] = __import__('jax').numpy.asarray(drawn.astype(out[name].dtype))
    for name, factor in factors.items():
        out[name] = (out[name] * factor).astype(out[name].dtype)
    return out
```

```python
from contextlib import ExitStack

import numpy as np
import concourse.bass as bass
from concourse import mybir

F32 = mybir.dt.float32
F32R = mybir.dt.float32r
U32 = mybir.dt.uint32
ALU = mybir.AluOpType
ACT = mybir.ActivationFunctionType
AX = mybir.AxisListType

P = 128
D = 1024
KT = D // P
S = 1024
B8 = 8
T = S + B8
NT = 9
CH = T // 3
HEADS, KV, HD, WIN = 16, 4, 64, 128
NBUCKET, MAXD = 32, 128
NE, NG, EG, FE = 32, 4, 8, 512
EPS = 1e-6
SCALE = HD ** -0.5
MASKED = -1e30
COL_CB, COL_CC, COL_CH, COL_Q, COL_K, COL_V, COL_GA, COL_GB = 0, 1024, 2048, 3072, 4096, 4352, 4608, 5632
SKEW = 384
NBUF = 383
UNITS_A, UNITS_V, UNITS_B, UNITS_C = 10, 2, 24, 32
LISTROWS = 9 * P
OVF = 16
NOROW = 4096
C_ID, C_SLT, C_ONE, C_MB, C_HM, C_IO, C_TOK, C_I16, C_B128, C_PIX, C_END = (
    0, 128, 256, 257, 265, 281, 313, 331, 347, 355, 356)


def bucket(n):
    if n < NBUCKET // 2:
        return n
    big = 16 + int(np.float32(np.log(np.float32(n) / np.float32(16))) / np.float32(np.log(8.0)) * np.float32(16))
    return min(big, NBUCKET - 1)


def constants():
    c = np.zeros((P, C_END), np.float32)
    p = np.arange(P)
    c[:, C_ID:C_ID + P] = np.eye(P)
    c[:, C_SLT:C_SLT + P] = p[:, None] < p[None, :]
    c[:, C_ONE] = 1
    c[:, C_MB:C_MB + 8] = (p[:, None] // 4) % 8 == np.arange(8)
    c[:, C_HM:C_HM + 16] = (p[:, None] // 32) * 4 + p[:, None] % 4 == np.arange(16)
    c[:, C_IO:C_IO + 32] = np.arange(32)
    for t in range(NT):
        for k in range(2):
            c[:, C_TOK + 2 * t + k] = k * T + P * t + p
    c[:, C_I16:C_I16 + OVF] = np.arange(OVF)
    c[:, C_B128:C_B128 + 8] = P * np.arange(1, 9)
    c[:, C_PIX] = p
    hot = np.zeros((NBUCKET + 1, 512 + 1), np.float32)
    for u in range(NBUF):
        d = 255 - u
        if 0 <= d <= WIN:
            hot[bucket(d), u] = 1 / SCALE
        else:
            hot[NBUCKET, u] = MASKED
    for j in range(129):
        hot[bucket(128 - j), SKEW + j] = 1 / SCALE
    return c, hot


class Steps:

    def __init__(self, engine, sem):
        self.engine, self.sem, self.n = engine, sem, 0

    def after(self, instruction):
        instruction.then_inc(self.sem, 1)
        self.n = self.n + 1
        self.engine.wait_ge(self.sem, self.n)


def program(nc, x_prompt, x_sample, cache_conv, cache_k, cache_v, norm1_g, w_in, conv_w, w_conv_out,
            w_attn_out, w_o, sinks, rel_bias, norm2_g, w_router_group, b_router_group,
            w_router_expert, b_router_expert, w_e_gate, w_e_up, w_e_down, norm_f_g, table, onehot,
            y_prompt, y_sample, conv_state_prompt, k_win_prompt, v_win_prompt,
            conv_state_sample, k_win_sample, v_win_sample):
    a_dram = nc.dram_tensor("a_spill", (P, KT, T), F32).ap()
    skew = nc.dram_tensor("bias_skew", (HEADS, P * SKEW), F32).ap()
    xn_dram = nc.dram_tensor("normed_rows", (T, D), F32).ap()
    y_dram = nc.dram_tensor("expert_rows", (2 * T, D), F32).ap()
    list_dram = nc.dram_tensor("token_lists", (LISTROWS * NE, 1), U32).ap()

    with ExitStack() as ctx:
        base = 16512

        def at(name, offset, shape, dt=F32):
            return nc.alloc_sbuf_tensor_at(name, [P] + shape if shape[0] != "rows" else shape[1:], dt, offset=base + offset)

        def sem(name):
            return ctx.enter_context(nc.semaphore(name))

        W8 = KT * T * 4
        R3, R4, R5, RING, SMALL = 2 * W8, 3 * W8, 3 * W8 + 33856, 4 * W8 + 33856, 4 * W8 + 33856 + 36864
        h_hi = at("h_hi", 0, [KT, T], F32R)
        h_lo = at("h_lo", W8, [KT, T], F32R)
        q_sb = at("q_sb", R3, [KT, T])
        o_lo = at("o_lo", R3, [KT, T], F32R)
        o_hi = at("o_hi", R4, [KT, T], F32R)
        a_raw = at("a_raw", R3, [KT, T])
        a_lo = at("a_lo", R3, [KT, T], F32R)
        a_hi = at("a_hi", R4, [KT, T], F32R)
        x_tok = at("x_tok", R3, [NT, D])
        k_sb = at("k_sb", R4, [2, T])
        v_sb = at("v_sb", R4 + 8256, [NT, 256])
        bias_sb = at("bias_sb", R4 + 8256 + 9216, [HEADS, 256])
        mix = at("mix", R5, [KT, T])
        junk = at("junk", R5, [D])
        bias_row = at("bias_row", R5 + 4096, [HEADS, SKEW])
        q_stage = at("q_stage", R5, [KT, P])
        k_stage = at("k_stage", R5 + 4096, [2, 2 * P])
        probs = at("probs", R5 + 6144, [2, 2, 256])
        probsT = at("probsT", R5 + 10240, [2, 4, P])
        o_tok = at("o_tok", R5 + 14336, [D])
        u_sb = at("u_sb", R5 + 18432, [T + 2])
        y_sb = at("y_sb", R5 + 22592, [T])
        kc = at("kc", R5, [B8, 256])
        vc = at("vc", R5 + 8192, [B8, 256])
        kcT = at("kcT", R5 + 16384, [B8, 2, P])
        sT = at("sT", R5 + 24576, [P])
        s_rows = at("s_rows", R5 + 25088, [P])
        pT = at("pT", R5 + 25600, [P])
        k_out = at("k_out", R5 + 26112, [2, 256])
        u_out = at("u_out", R5 + 28160, [D])
        pn8 = at("pn8", R5 + 32256, [8])
        pn8T = at("pn8T", R5 + 32288, [P])

        w_raw = [at(f"w_raw{i}", RING + 4096 * i, [KT, P]) for i in range(3)]
        w_hi = at("w_hi", RING + 12288, [3, KT, P], F32R)
        w_lo = at("w_lo", RING + 24576, [3, KT, P], F32R)
        cur = [SMALL]

        def small(name, shape, dt=F32):
            n = 4
            for s in shape:
                n *= s
            cur[0] += -cur[0] % 32
            t = at(name, cur[0], shape, dt)
            cur[0] += n
            return t

        tab = small("tab", [C_END])
        cols32 = small("cols32", [32])
        g1 = cols32[:, 0:KT]
        carrier = small("carrier", [1])
        ssq = small("ssq", [NT])
        rms = small("rms", [NT])
        eps = small("eps", [1])
        GATE = cur[0] + -cur[0] % 32
        gate = small("gate", [T])
        SHARED = cur[0]
        sinkb = small("sinkb", [HEADS])
        sink8 = small("sink8", [HEADS])
        sinkc = small("sinkc", [1])
        relb = small("relb", [HEADS])
        bs8 = small("bs8", [129])
        histT = small("histT", [KT, 2, B8])
        ustate = small("ustate", [KT, 10])
        maxs = small("maxs", [HEADS])
        negm = small("negm", [HEADS])
        sinkd = small("sinkd", [HEADS])
        den = small("den", [HEADS])
        esink = small("esink", [HEADS])
        rden = small("rden", [HEADS])
        sc = small("sc", [16])
        tmp8 = small("tmp8", [KT, B8])
        relc = at("relc", R5 + 32000, [P])
        hot = at("hot", R5 + 28672, [513])
        hist_rows = at("hist_rows", R4 + 8256, [D])
        rows32 = at("rows32", R4 + 12352, [P])
        q_new = small("q_new", [2, 32])
        wo_raw = at("wo_raw", 0, [KT, D])
        wo_lo = at("wo_lo", 0, [KT, D], F32R)
        wo_hi = at("wo_hi", W8, [KT, D], F32R)
        mix_hi = at("mix_hi", R3, [2, KT, P], F32R)
        mix_lo = at("mix_lo", R3 + 8192, [2, KT, P], F32R)
        x2 = at("x2", R3 + 16384, [NT, D])
        x_in = at("x_in", R3 + 53248, [2, D])
        h2T = at("h2T", R3 + 61440, [KT, P])
        xn = at("xn", RING + 32768, [D])
        g2b = at("g2b", GATE, [D])
        list_init = at("list_init", GATE, [LISTROWS * NE // P], U32)
        wr = at("wr", R3 + 65536, [KT, 36])
        cur[0] = SHARED
        rb = small("rb", [36])
        lg = small("lg", [40])
        top_g = small("top_g", [8])
        idx_g = small("idx_g", [8], U32)
        grp = small("grp", [2])
        oh4 = small("oh4", [4])
        prod = small("prod", [8, 4])
        e8 = small("e8", [8])
        top_e = small("top_e", [8])
        idx_e = small("idx_e", [8], U32)
        idx_f = small("idx_f", [2])
        picked = small("picked", [2, 2])
        hots = small("hots", [2, 2, NE])
        picks = small("picks", [2, NE])
        seen = small("seen", [NE])
        rank2 = small("rank2", [2])
        adr_f = small("adr_f", [2])
        adr = small("adr", [2 * NT], U32)
        tok_u = small("tok_u", [2 * NT], U32)
        gl = small("gl", [NT, 4])
        tv = small("tv", [NT, 2])
        wts = small("wts", [NT, 2])
        wsum = small("wsum", [NT])
        cnt = small("cnt", [4])
        ov_a = small("ov_a", [3, OVF])
        ov_b = small("ov_b", [2 * OVF + 1])
        ov_t = small("ov_t", [2 * OVF + 1], U32)
        lst = small("lst", [NE], U32)
        lst_f = small("lst_f", [NE])
        lst_g = small("lst_g", [NE])
        gidx = small("gidx", [NE], U32)
        gcol = small("gcol", [2], U32)
        idle_in, idle_out = small("idle_in", [1]), small("idle_out", [2])
        scol = small("scol", [1], U32)
        e_raw = [at(f"e_raw{i}", RING + 8192 * i if i < 4 else 8192 * (i - 4), [2048]) for i in range(12)]
        e_lo = [at(f"e_lo{i}", RING + 8192 * i if i < 4 else 8192 * (i - 4), [2048], F32R) for i in range(12)]
        e_hi = at("e_hi", R5, [4, 2048], F32R)
        xT_hi = at("xT_hi", R3, [2, KT, P], F32R)
        xT_lo = at("xT_lo", R3 + 8192, [2, KT, P], F32R)
        xg = at("xg", R3 + 53248, [2, D])
        sg = at("sg", R3 + 61440, [FE])
        act_sb = at("act_sb", R3 + 63488, [FE])
        aT_hi = at("aT_hi", RING + 32768, [4, P], F32R)
        aT_lo = at("aT_lo", RING + 34816, [4, P], F32R)
        y_out = at("y_out", GATE, [D])
        v_gate = at("v_gate", 0, [KT, FE])
        v_up = at("v_up", 16384, [KT, FE])
        v_down = at("v_down", 32768, [4, D])
        v_xT = at("v_xT", R3, [KT, P])
        v_aT = at("v_aT", R3 + 4096, [4, P])
        f_y = [at(f"f_y{k}", 8192 * k, [2, D]) for k in range(2)]
        f_out = at("f_out", 16384, [2, D])
        gfb = at("gfb", 24576, [D])
        f_junk = at("f_junk", 28672, [D])
        assert base + cur[0] <= 229344, cur[0]

        bank = [ctx.enter_context(nc.psum_tensor(f"bank{i}", [P, 512], F32)) for i in range(8)]
        DN, SCB, PTB, OB, OTB = bank[0:3], bank[3:5], bank[5], bank[6], bank[7]
        ident = tab[:, C_ID:C_ID + P]

        relb_ones = sem("relb_ones")
        consts_loaded = sem("consts_loaded")
        x_loaded = [sem(f"x_loaded{g}") for g in range(3)]
        squares_done, sqrt_done, x_scaled = sem("squares_done"), sem("sqrt_done"), sem("x_scaled")
        xT_ready, h_hi_done, h_lo_done = sem("xT_ready"), sem("h_hi_done"), sem("h_lo_done")
        bias_psum, bias_row_done, skew_written, bias_loaded = sem("bias_psum"), sem("bias_row_done"), sem("skew_written"), sem("bias_loaded")
        relc_done, start_psum, start_copied, halo_zero = sem("relc_done"), sem("start_psum"), sem("start_copied"), sem("halo_zero")
        raw_loaded = [sem(f"raw_loaded{i}") for i in range(3)]
        hi_ready, lo_ready = sem("hi_ready"), sem("lo_ready")
        chunk_done, chunk_out, gate_out = sem("chunk_done"), sem("chunk_out"), sem("gate_out")
        staged, scores_ready, max_ready, probs_ready = sem("staged"), sem("scores_ready"), sem("max_ready"), sem("probs_ready")
        probs_turned, probsT_ready, pv_done, o_normed = sem("probs_turned"), sem("probsT_ready"), sem("pv_done"), sem("o_normed")
        o_turned, o_stored = sem("o_turned"), sem("o_stored")
        a_spilled = sem("a_spilled")
        dve_step, act_step = sem("dve_step"), sem("act_step")
        cache_loaded, states_out, v_out = sem("cache_loaded"), sem("states_out"), sem("v_out")
        kcT_psum, kcT_copied, sT_psum, sT_copied = sem("kcT_psum"), sem("kcT_copied"), sem("sT_psum"), sem("sT_copied")
        s_psum, s_max, s_exp, s_normed = sem("s_psum"), sem("s_max"), sem("s_exp"), sem("s_normed")
        pT_psum, pT_copied, so_psum, so_stored = sem("pT_psum"), sem("pT_copied"), sem("so_psum"), sem("so_stored")
        win_psum, win_copied, q_new_done = sem("win_psum"), sem("win_copied"), sem("q_new_done")
        o_hi_done, o_lo_done, a_loaded, a_hi_done, a_lo_done = sem("o_hi_done"), sem("o_lo_done"), sem("a_loaded"), sem("a_hi_done"), sem("a_lo_done")

        wo_loaded = [sem(f"wo_loaded{i}") for i in range(4)]
        wo_hi_done, wo_lo_done = sem("wo_hi_done"), sem("wo_lo_done")
        router_loaded, list_filled, list_blank = sem("router_loaded"), sem("list_filled"), sem("list_blank")
        x_again = [sem(f"x_again{i}") for i in range(2)]
        mix_hi_done, mix_lo_done, proj_done, x2_done = sem("mix_hi_done"), sem("mix_lo_done"), sem("proj_done"), sem("x2_done")
        sq2_done, root2_done, xn_done, xn_written = sem("sq2_done"), sem("root2_done"), sem("xn_done"), sem("xn_written")
        xnT_psum, h2T_done, logits_done, picks_done = sem("xnT_psum"), sem("h2T_done"), sem("logits_done"), sem("picks_done")
        rank_done, seen_done, adr_done, listed = sem("rank_done"), sem("seen_done"), sem("adr_done"), sem("listed")
        ov_psum, ov_sbuf, list_loaded, gidx_done = sem("ov_psum"), sem("ov_sbuf"), sem("list_loaded"), sem("gidx_done")
        wexp_done, wsum_done = sem("wexp_done"), sem("wsum_done")
        e_loaded = [sem(f"e_loaded{i}") for i in range(12)]
        e_hi_done, e_lo_done, e_used = sem("e_hi_done"), sem("e_lo_done"), sem("e_used")
        silu_done, act_done = sem("silu_done"), sem("act_done")
        aT_psum, aT_hi_done, aT_lo_done = sem("aT_psum"), sem("aT_hi_done"), sem("aT_lo_done")
        xT_psum, xT_hi_done, xT_lo_done = sem("xT_psum"), sem("xT_hi_done"), sem("xT_lo_done")
        y_psum, y_stored, col_done, scattered = sem("y_psum"), sem("y_stored"), sem("col_done"), sem("scattered")
        idle_ready, idled, v_free = sem("idle_ready"), sem("idled"), sem("v_free")
        gathered = [sem(f"gathered{i}") for i in range(2)]
        v_loaded, v_col, v_idx, v_gathered, v_xpsum, v_xT_done = (sem("v_loaded"), sem("v_col"), sem("v_idx"), sem("v_gathered"),
                                                                  sem("v_xpsum"), sem("v_xT_done"))
        v_gu, v_silu, v_act, v_apsum, v_aT_done, v_ypsum, v_y, v_scattered = (
            sem("v_gu"), sem("v_silu"), sem("v_act"), sem("v_apsum"), sem("v_aT_done"), sem("v_ypsum"), sem("v_y"), sem("v_scattered"))
        rows_written, gf_loaded, f_sum, f_sq, f_root, f_done, f_stored = (
            sem("rows_written"), sem("gf_loaded"), sem("f_sum"), sem("f_sq"), sem("f_root"), sem("f_done"),
            [sem(f"f_stored{i}") for i in range(2)])
        f_loaded = [sem(f"f_loaded{i}") for i in range(2)]

        block = ctx.enter_context(nc.Block())

        def e_chunk(s):
            c, e = s
            if c < 4:
                w = (w_e_gate if c < 2 else w_e_up)[0].rearrange("e (k p) f -> e p k f", p=P)
                return w, e, slice(4 * (c % 2), 4 * (c % 2) + 4)
            return w_e_down[0].rearrange("e (k p) f -> e p k f", p=P), e - 1, slice(2 * (c % 2), 2 * (c % 2) + 2)
        w_in_t = w_in[0].rearrange("(k p) f -> p k f", p=P)
        w_ao_t = w_attn_out[0].rearrange("(k p) f -> p k f", p=P)
        w_co_t = w_conv_out[0].rearrange("(k p) f -> p k f", p=P)
        N_CONSTS = 11
        U_V, U_B, U_C = UNITS_A, UNITS_A + UNITS_V, UNITS_A + UNITS_V + UNITS_B

        @block.sync
        def _(sp):
            def load(slot, parts):
                for dst, src in parts:
                    sp.dma_start(dst, src).then_inc(raw_loaded[slot], 32 // len(parts))

            def cols(slot, w, col, wait=None):
                if wait is not None:
                    sp.wait_ge(lo_ready, wait)
                w = w.rearrange("p k (n f) -> p k n f", f=P)
                load(slot, [(w_raw[slot][:, 4 * h:4 * h + 4, :], w[:, 4 * h:4 * h + 4, bass.ds(col, 1), :].rearrange("p k n f -> p k (n f)")) for h in range(2)])

            for g in range(2):
                sp.dma_start(x_tok[:, 4 * g:4 * g + 4, :],
                             x_prompt[0, 512 * g:512 * g + 512, :].rearrange("(t p) d -> p t d", p=P)).then_inc(x_loaded[g], 16)
            sp.dma_start(x_tok[0:B8, 8, :], x_sample[:, 0, :]).then_inc(x_loaded[2], 16)
            def q_unit(t, j, slot, wait):
                col = [COL_Q + t * 512 + j * 64 + 256 * h for h in range(2)]
                col = [x if isinstance(x, int) else sp.snap(x) for x in col]
                if wait is not None:
                    sp.wait_ge(lo_ready, wait)
                load(slot, [(w_raw[slot][:, :, 64 * h:64 * h + 64],
                             w_in_t[:, :, bass.ds(col[h], 64)]) for h in range(2)])

            def a_units(t, first):
                u = t * 5
                for j in range(4):
                    q_unit(t, j, j % 3, None if first and j < 3 else u + j - 1)
                cols(1, w_in_t, COL_K // P + t, u + 3)

            a_units(0, True)
            a_units(1, False)
            for v in range(2):
                cols(v, w_in_t, COL_V // P + v, U_V + v - 1)
            with sp.Fori(0, KT) as j:
                for s, col in enumerate((COL_CC, COL_CH, COL_CB)):
                    cols(s, w_in_t, j + col // P, j * 3 + (U_B + s - 1))
            with sp.Fori(0, KT) as j:
                cols(0, w_in_t, j + COL_GB // P, j * 2 + (U_C - 1))
                cols(1, w_ao_t, j, j * 2 + U_C)
            sp.wait_ge(chunk_done, 111 + 48)
            sp.dma_start(a_raw[:, :, :], a_dram).then_inc(a_loaded, 16)
            with sp.Fori(0, KT) as j:
                cols(0, w_in_t, j + COL_GA // P, j * 2 + (U_C + 15))
                cols(1, w_co_t, j, j * 2 + (U_C + 16))
            sp.wait_ge(chunk_done, 111 + 6 * 15 + 3)
            wo_t = w_o[0].rearrange("(k p) f -> p k f", p=P)
            for i in range(4):
                sp.dma_start(wo_raw[:, 2 * i:2 * i + 2, :], wo_t[:, 2 * i:2 * i + 2, :]).then_inc(wo_loaded[i], 16)
            sp.wait_ge(chunk_done, 111 + 96)

            def load_x(n, slot, first):
                if not first:
                    sp.wait_ge(sq2_done, n - 1)
                sp.dma_start(x_in[:, slot, :], x_prompt[0, bass.ds(n * P, P), :]).then_inc(x_again[slot], 16)

            def load_chunk(slot, c, e, wait):
                if wait is not None:
                    sp.wait_ge(e_used, wait)
                w, ex, ks = e_chunk((c, e))
                n = ks.stop - ks.start
                sp.dma_start(e_raw[slot][:, :].rearrange("p (k f) -> p k f", k=n),
                             w[bass.ds(ex, 1), :, ks, :].rearrange("e p k f -> p (e k) f")).then_inc(e_loaded[slot], 16)

            load_x(0, 0, True)
            load_x(1, 1, True)
            sp.wait_ge(chunk_out, 159)
            for s in range(4):
                load_chunk(s, s, 0, None)
            with sp.Fori(1, 4) as i:
                for b in range(2):
                    load_x(i * 2 + b, b, False)
            sp.wait_ge(sq2_done, 7)
            sp.dma_start(x_in[0:B8, 0, :], x_sample[:, 0, :]).then_inc(x_again[0], 16)
            sp.wait_ge(proj_done, NT)
            for s in range(4, 12):
                load_chunk(s, (s - 4) % 6, 1 + (s - 4) // 6, None)

            def load_round(i, final):
                for c in range(12):
                    s = 8 + c
                    cc, de = s % 6, s // 6
                    if final and c >= 10:
                        cc, de = cc + 4, de
                    load_chunk(c, cc, i * 2 + (1 + de), i * 12 + (1 + c))

            with sp.Fori(0, 14) as i:
                load_round(i, False)
            load_round(14, True)

            sp.wait_ge(e_used, 192)
            sp.wait_ge(ov_sbuf, 3)
            n_ov = sp.value_load(ov_t[0:1, 2 * OVF:2 * OVF + 1], min_val=0, max_val=OVF)
            with sp.Fori(0, OVF) as i:
                with sp.If(i < n_ov):
                    ex = sp.value_load(ov_t[0:1, bass.ds(i, 1)], min_val=0, max_val=NE - 1)
                    sp.wait_ge(v_free, i + 1)
                    for dst, w in ((v_gate, w_e_gate), (v_up, w_e_up), (v_down, w_e_down)):
                        sp.dma_start(dst[:, :, :], w[0][bass.ds(ex, 1)].rearrange("e (k p) f -> p (e k) f", p=P)).then_inc(v_loaded, 16)

            sp.wait_ge(rows_written, 1)
            sp.dma_start(gfb[:, :], norm_f_g.partition_broadcast(P)).then_inc(gf_loaded, 16)

            def load_y(n, slot, rows, first):
                if not first:
                    sp.wait_ge(f_sum, n - 1)
                for k in range(2):
                    sp.dma_start(f_y[k][0:rows, slot, :], y_dram[bass.ds(n * P + k * T, rows), :]).then_inc(f_loaded[slot], 16)

            def store_y(n, slot, rows):
                sp.wait_ge(f_done, n + 1)
                dst = y_prompt[0, bass.ds(n * P, P), :] if rows == P else y_sample[:, 0, :]
                sp.dma_start(dst, f_out[0:rows, slot, :]).then_inc(f_stored[slot], 16)

            load_y(0, 0, P, True)
            load_y(1, 1, P, True)
            with sp.Fori(0, 3) as i:
                for b in range(2):
                    load_y(i * 2 + (b + 2), b, P, False)
                    store_y(i * 2 + b, b, P)
            load_y(8, 0, B8, False)
            store_y(6, 0, P)
            store_y(7, 1, P)
            store_y(8, 0, B8)
            sp.wait_ge(f_stored[0], 16 * 5)
            sp.wait_ge(f_stored[1], 16 * 4)
            sp.wait_ge(states_out, 16 * 7)

        @block.gpsimd
        def _(pool):
            pool.dma_start(tab[:, :], table).then_inc(consts_loaded, 16)
            pool.dma_start(hot[0:33, :], onehot).then_inc(consts_loaded, 16)
            pool.dma_start(rows32[0:8, :], norm1_g[0].rearrange("(k p) -> k p", p=P)).then_inc(consts_loaded, 16)
            pool.dma_start(rows32[8:32, :], conv_w[0].rearrange("j (k p) -> (j k) p", p=P)).then_inc(consts_loaded, 48)
            pool.dma_start(sinkb[:, :], sinks[0].partition_broadcast(P)).then_inc(consts_loaded, 16)
            pool.dma_start(hist_rows[0:16, :], cache_conv[0].rearrange("b r d -> (b r) d")).then_inc(consts_loaded, 16)
            pool.wait_ge(relb_ones, 1)
            pool.dma_start(relb[0:32, :], rel_bias).then_inc(consts_loaded, 48)
            pool.wait_ge(list_filled, 1)
            pool.dma_start(list_dram.rearrange("(p q) o -> p (q o)", p=P), list_init[:, :]).then_inc(list_blank, 16)
            for h in range(HEADS):
                pool.wait_ge(bias_row_done, h + 1)
                pool.dma_start(skew[h].rearrange("(p q) -> p q", q=SKEW), bias_row[:, h, :]).then_inc(skew_written, 16)
            pool.wait_ge(skew_written, 16 * HEADS)
            pool.dma_start(bias_sb[:, :, :], skew[:, 127:127 + P * NBUF].rearrange("h (p q) -> p h q", q=NBUF)[:, :, 0:256]).then_inc(bias_loaded, 16)

            def stage(b, first):
                if not first:
                    pool.wait_ge(scores_ready, b * 8)
                if first:
                    pool.tensor_copy(k_stage[:, :, P:2 * P], k_sb[:, :, 0:P]).then_inc(staged, 1)
                else:
                    pool.tensor_copy(k_stage[:, :, :], k_sb[:, :, bass.ds(b * P - P, 2 * P)]).then_inc(staged, 1)
                pool.tensor_copy(q_stage[:, :, :], q_sb[:, :, bass.ds(b * P, P)]).then_inc(staged, 1)

            def spill(j):
                pool.wait_ge(chunk_out, j * 9 + 48)
                pool.dma_start(a_dram[:, bass.ds(j, 1), :], y_sb[:, :].unsqueeze(1)).then_inc(a_spilled, 16)

            pool.wait_ge(chunk_out, 3 * UNITS_A)
            pool.wait_ge(bias_loaded, 16)
            stage(0, True)
            with pool.Fori(0, KT - 1) as j:
                stage(j + 1, False)
                spill(j)
            spill(KT - 1)

            pool.wait_ge(o_stored, 16)
            pool.wait_ge(a_spilled, 16 * KT)
            pool.dma_start(kc[:, :, :], cache_k[0].rearrange("b s g d -> s b (g d)")).then_inc(cache_loaded, 16)
            pool.dma_start(vc[:, :, :], cache_v[0].rearrange("b s g d -> s b (g d)")).then_inc(cache_loaded, 16)
            flat = lambda x: x.rearrange("b s g d -> b s (g d)")
            pool.dma_start(flat(k_win_sample[0])[:, 0:WIN - 1, :], flat(cache_k[0])[:, 1:WIN, :]).then_inc(states_out, 16)
            pool.dma_start(flat(v_win_sample[0])[:, 0:WIN - 1, :], flat(cache_v[0])[:, 1:WIN, :]).then_inc(states_out, 16)
            pool.dma_start(conv_state_sample[0, :, 0, :], cache_conv[0, :, 1, :]).then_inc(states_out, 16)
            pool.dma_start(flat(v_win_prompt[0])[0], v_sb[:, 7, :]).then_inc(v_out, 16)
            pool.dma_start(flat(v_win_sample[0])[:, WIN - 1, :], v_sb[0:B8, 8, :]).then_inc(v_out, 16)
            pool.wait_ge(win_copied, 4)
            pool.dma_start(flat(k_win_prompt[0])[0], k_out[:, 0, :]).then_inc(states_out, 16)
            pool.dma_start(flat(k_win_sample[0])[:, WIN - 1, :], k_out[0:B8, 1, :]).then_inc(states_out, 16)
            pool.dma_start(conv_state_prompt[0, 0], u_out[0:2, :]).then_inc(states_out, 16)
            pool.dma_start(conv_state_sample[0, :, 1, :], u_out[2:10, :]).then_inc(states_out, 16)
            pool.wait_ge(states_out, 16 * 7)
            pool.wait_ge(v_out, 32)
            pool.wait_ge(chunk_out, 159)
            pool.dma_start(wr[:, :, 0:NG], w_router_group[0].rearrange("(k p) g -> p k g", p=P)).then_inc(router_loaded, 16)
            pool.dma_start(wr[:, :, NG:NG + NE], w_router_expert[0].rearrange("(k p) g -> p k g", p=P)).then_inc(router_loaded, 16)
            pool.dma_start(rb[:, 0:NG], b_router_group[0].partition_broadcast(P)).then_inc(router_loaded, 16)
            pool.dma_start(rb[:, NG:NG + NE], b_router_expert[0].partition_broadcast(P)).then_inc(router_loaded, 16)
            pool.dma_start(g2b[:, :], norm2_g[0].partition_broadcast(P)).then_inc(router_loaded, 16)
            pool.wait_ge(list_blank, 16)

            def write_xn(n, rows):
                pool.wait_ge(xn_done, n + 1)
                pool.dma_start(xn_dram[P * n:P * n + rows, :], xn[0:rows, :]).then_inc(xn_written, 16)

            def enter_lists(n, rows):
                pool.wait_ge(adr_done, n + 1)
                for k in range(2):
                    pool.indirect_dma_start(out=list_dram, out_offset=bass.IndirectOffsetOnAxis(ap=adr[0:rows, 2 * n + k:2 * n + k + 1], axis=0),
                                            in_=tok_u[0:rows, 2 * n + k:2 * n + k + 1], in_offset=None,
                                            bounds_check=LISTROWS * NE - 1, oob_is_err=False).then_inc(listed, 16)

            for n in range(NT + 2):
                if n >= 2:
                    enter_lists(n - 2, P if n < 10 else B8)
                if n < NT:
                    write_xn(n, P if n < 8 else B8)
            pool.wait_ge(listed, 32 * NT)
            pool.wait_ge(xn_written, 16 * NT)
            pool.dma_start(lst[:, :], list_dram[0:P * NE, :].rearrange("(r e) o -> r (e o)", e=NE)).then_inc(list_loaded, 16)
            pool.wait_ge(gidx_done, 1)

            pool.memset(idle_in[:, :], 0.0).then_inc(idle_ready, 1)
            pool.wait_ge(idle_ready, 1)

            def gather(e, par, first):
                if not first:
                    pool.wait_ge(xT_psum, e - 1)
                pool.tensor_copy(gcol[:, par:par + 1], gidx[:, bass.ds(e, 1)]).then_inc(col_done, 1)
                return par

            def carry(k=0):
                return pool.tensor_tensor(idle_out[:, k:k + 1], idle_in[:, :], idle_in[:, :], ALU.add)

            def gather_rows(par):
                pool.indirect_dma_start(out=xg[:, par, :], out_offset=None, in_=xn_dram,
                                        in_offset=bass.IndirectOffsetOnAxis(ap=gcol[:, par:par + 1], axis=0),
                                        bounds_check=T - 1, oob_is_err=False).then_inc(gathered[par], 16)

            def scatter_rows():
                pool.indirect_dma_start(out=y_dram, out_offset=bass.IndirectOffsetOnAxis(ap=scol[:, 0:1], axis=0),
                                        in_=y_out[:, :], in_offset=None, bounds_check=2 * T - 1, oob_is_err=False).then_inc(scattered, 16)

            for e in range(2):
                gather(e, e, True)
                pool.wait_ge(col_done, e + 1)
                gather_rows(e)

            def step_e(e, par, more):
                if more:
                    gather(e + 2, par, False)
                    pool.wait_ge(col_done, e * 2 + 3)
                    carry()
                    gather_rows(par)
                    pool.wait_ge(y_stored, e + 1)
                    pool.tensor_copy(scol[:, 0:1], lst[:, bass.ds(e, 1)]).then_inc(col_done, 1)
                    pool.wait_ge(col_done, e * 2 + 4)
                    carry()
                else:
                    pool.wait_ge(y_stored, e + 1)
                    pool.tensor_copy(scol[:, 0:1], lst[:, bass.ds(e, 1)]).then_inc(col_done, 1)
                    pool.wait_ge(col_done, e + 33)
                scatter_rows()

            with pool.Fori(0, 15) as i:
                for b in range(2):
                    step_e(i * 2 + b, b, True)
            step_e(30, 0, False)
            step_e(31, 1, False)
            pool.wait_ge(scattered, 16 * NE)

            pool.wait_ge(ov_sbuf, 3)
            pool.sem_inc(v_free, 1)
            n_ov = pool.value_load(ov_t[0:1, 2 * OVF:2 * OVF + 1], min_val=0, max_val=OVF)
            with pool.Fori(0, OVF) as i:
                with pool.If(i < n_ov):
                    ex = pool.value_load(ov_t[0:1, bass.ds(i, 1)], min_val=0, max_val=NE - 1)
                    bk = pool.value_load(ov_t[0:1, bass.ds(i + OVF, 1)], min_val=1, max_val=8)
                    pool.dma_start(scol[:, 0:1], list_dram[bass.ds(bk * (P * NE), P * NE), :].rearrange("(r e) o -> r (e o)", e=NE)[:, bass.ds(ex, 1)],
                                   allow_slow_non_contiguous=True).then_inc(v_col, 16)
                    pool.wait_ge(v_idx, i + 1)
                    carry().then_inc(idled, 1)
                    pool.indirect_dma_start(out=xg[:, 0, :], out_offset=None, in_=xn_dram,
                                            in_offset=bass.IndirectOffsetOnAxis(ap=gcol[:, 0:1], axis=0),
                                            bounds_check=T - 1, oob_is_err=False).then_inc(v_gathered, 16)
                    pool.wait_ge(v_y, i + 1)
                    carry(1).then_inc(idled, 1)
                    pool.indirect_dma_start(out=y_dram, out_offset=bass.IndirectOffsetOnAxis(ap=scol[:, 0:1], axis=0),
                                            in_=y_out[:, :], in_offset=None, bounds_check=2 * T - 1, oob_is_err=False).then_inc(v_scattered, 16)
                    pool.wait_ge(idled, i * 2 + 2)
                    pool.wait_ge(v_scattered, i * 16 + 16)
                    pool.sem_inc(v_free, 1)
            pool.drain().then_inc(rows_written, 1)

        def ce(u):
            return (u - U_B) * 3 + 42

        @block.tensor
        def _(pe):
            def split_product(out, pairs):
                for i, ((xh, xl), (wh, wl)) in enumerate(pairs):
                    pe.matmul(out, wh, xh, start=i == 0, stop=False)
                    pe.matmul(out, wh, xl, start=False, stop=False)
                    mm = pe.matmul(out, wl, xh, start=False, stop=i == len(pairs) - 1)
                return mm

            def unit_chunk(slot, xh, xl, c):
                cols = slice(CH * c, CH * c + CH)
                split_product(DN[c][:, 0:CH], [((xh[:, k, cols], xl[:, k, cols]), (w_hi[:, slot, k, :], w_lo[:, slot, k, :]))
                                               for k in range(KT)]).then_inc(chunk_done, 1)

            pe.wait_ge(consts_loaded, 16 * N_CONSTS)
            for h in range(HEADS):
                if h >= 4:
                    pe.wait_ge(bias_row_done, h - 3)
                pe.matmul(bank[h % 4][:, 0:SKEW], relb[0:33, h:h + 1].to_broadcast([33, P]), hot[0:33, 0:SKEW],
                          start=True, stop=True).then_inc(bias_psum, 1)
            pe.wait_ge(relc_done, 1)
            pe.matmul(bank[4][:, 0:129], relc[0:33, :], hot[0:33, SKEW:SKEW + 129], start=True, stop=True).then_inc(start_psum, 1)
            for k in range(KT):
                mm = pe.transpose(bank[5][:, 16 * k:16 * k + 16], hist_rows[0:16, P * k:P * k + P], ident[0:16, 0:16])
            pe.transpose(bank[5][:, P:P + 32], rows32[0:32, :], ident[0:32, 0:32]).then_inc(start_psum, 1)
            pe.wait_ge(bias_row_done, HEADS)
            pe.wait_ge(start_copied, 2)
            for g in range(2):
                pe.wait_ge(x_scaled, 4 * g + 4)
                for k in range(KT):
                    if g:
                        pe.wait_ge(h_lo_done, k + 1)
                    for i in range(4):
                        mm = pe.transpose(bank[k][:, P * i:P * i + P], x_tok[:, 4 * g + i, P * k:P * k + P], ident)
                    mm.then_inc(xT_ready, 1)
            pe.wait_ge(x_scaled, 9)
            pe.wait_ge(h_lo_done, 9)
            for k in range(KT):
                mm = pe.transpose(bank[0][:, B8 * k:B8 * k + B8], x_tok[0:B8, 8, P * k:P * k + P], ident[0:B8, 0:B8])
            mm.then_inc(xT_ready, 1)

            pe.wait_ge(h_lo_done, 17)

            def units_a(t, first):
                for i in range(5):
                    u = t * 5 + i
                    pe.wait_ge(lo_ready, u + 1)
                    for c in range(3):
                        if not (first and i == 0):
                            pe.wait_ge(chunk_out, u * 3 + (c - 2))
                        unit_chunk((0, 1, 2, 0, 1)[i], h_hi, h_lo, c)

            units_a(0, True)
            with pe.Fori(1, 2) as t:
                units_a(t, False)
            pe.wait_ge(lo_ready, U_V + 2)
            for n in range(NT):
                rows = P if n < 8 else B8
                pe.wait_ge(chunk_out, 30 + n - 2)
                out = DN[n % 3][0:rows, 0:256].rearrange("p (a f) -> p a f", a=2)
                for k in range(KT):
                    xh, xl = h_hi[:, k, P * n:P * n + rows], h_lo[:, k, P * n:P * n + rows]
                    pe.matmul(out, xh, w_hi[:, 0:2, k, :], start=k == 0, stop=False)
                    pe.matmul(out, xh, w_lo[:, 0:2, k, :], start=False, stop=False)
                    mm = pe.matmul(out, xl, w_hi[:, 0:2, k, :], start=False, stop=k == KT - 1)
                mm.then_inc(chunk_done, 1)

            def scores(st, b, first):
                g, off = st // 2, P if first else 0
                half, tile = 64 * (g % 2), 4 * (g // 2) + 2 * (st % 2)
                if st == 0:
                    pe.wait_ge(staged, b * 2 + 2)
                if not (first and st < 2):
                    pe.wait_ge(max_ready, b * 8 + (st - 1))
                for h in range(2):
                    mm = pe.matmul(SCB[st % 2][:, 256 * h + off:256 * h + 256], q_stage[half:half + 64, tile + h, :],
                                   k_stage[half:half + 64, g // 2, off:256], start=True, stop=True)
                mm.then_inc(scores_ready, 1)

            def turn_probs(st, b, first):
                pe.wait_ge(probs_ready, b * 8 + (st + 1))
                if not (first and st == 0):
                    pe.wait_ge(probsT_ready, b * 8 + st)
                for h in range(2):
                    for kt in range(1 if first else 0, 2):
                        mm = pe.transpose(PTB[:, P * (2 * h + kt):P * (2 * h + kt) + P],
                                          probs[:, st % 2, h, P * kt:P * kt + P], ident)
                mm.then_inc(probs_turned, 1)

            def values(st, b, first):
                g, a = st // 2, st % 2
                pe.wait_ge(probsT_ready, b * 8 + (st + 1))
                if st % 4 == 0 and not (first and st == 0):
                    pe.wait_ge(o_normed, b * 2 + st // 4)
                for h in range(2):
                    col = HD * (4 * (g % 2) + 2 * a + h)
                    if first:
                        mm = pe.matmul(OB[:, col:col + HD], probsT[:, st % 2, 2 * h + 1, :],
                                       v_sb[:, 0, HD * g:HD * g + HD], start=True, stop=True)
                        continue
                    for kt in range(2):
                        v = v_sb[:, bass.ds(b - 1 + kt, 1), HD * g:HD * g + HD].rearrange("p a f -> p (a f)")
                        mm = pe.matmul(OB[:, col:col + HD], probsT[:, st % 2, 2 * h + kt, :], v,
                                       start=kt == 0, stop=kt == 1)
                mm.then_inc(pv_done, 1)

            def turn_o(hf, b, first):
                pe.wait_ge(o_normed, b * 2 + (hf + 1))
                if not (first and hf == 0):
                    pe.wait_ge(o_stored, b * 2 + hf)
                for i in range(4):
                    mm = pe.transpose(OTB[:, P * i:P * i + P], o_tok[:, 512 * hf + P * i:512 * hf + P * i + P], ident)
                mm.then_inc(o_turned, 1)

            def step_b(j, first):
                for i in range(9):
                    s, c = i // 3, i % 3
                    if i > 0:
                        turn_probs(i - 1, j, first)
                    if i == 5:
                        turn_o(0, j, first)
                    if i < 8:
                        scores(i, j, first)
                    if c == 0:
                        pe.wait_ge(lo_ready, j * 3 + (U_B + s + 1))
                    pe.wait_ge(chunk_out, j * 9 + (39 + i - 2))
                    cols = slice(CH * c, CH * c + CH)
                    for k in range(KT):
                        if k == 4 and i > 0:
                            values(i - 1, j, first)
                        pe.matmul(DN[c][:, 0:CH], w_hi[:, s, k, :], h_hi[:, k, cols], start=k == 0, stop=False)
                        pe.matmul(DN[c][:, 0:CH], w_hi[:, s, k, :], h_lo[:, k, cols], start=False, stop=False)
                        mm = pe.matmul(DN[c][:, 0:CH], w_lo[:, s, k, :], h_hi[:, k, cols], start=False, stop=k == KT - 1)
                    mm.then_inc(chunk_done, 1)
                turn_o(1, j, first)

            step_b(0, True)
            with pe.Fori(1, KT) as j:
                step_b(j, False)

            pe.wait_ge(chunk_out, 111)
            for t in range(2):
                mm = pe.transpose(bank[0][:, P * t:P * t + P], k_sb[:, t, S - P:S], ident)
            mm.then_inc(win_psum, 1)
            for t in range(2):
                mm = pe.transpose(bank[1][0:B8, P * t:P * t + P], k_sb[:, t, S:T], ident)
            mm.then_inc(win_psum, 1)
            pe.wait_ge(max_ready, 64)
            for half in range(2):
                for k in range(4):
                    mm = pe.transpose(bank[2 + half][0:10, P * k:P * k + P], ustate[:, 4 * half + k, :], ident)
                mm.then_inc(win_psum, 1)
            pe.wait_ge(probsT_ready, 64)
            pe.wait_ge(o_normed, 16)
            pe.wait_ge(o_stored, 16)
            pe.wait_ge(q_new_done, 1)
            for g in range(KV):
                half, t = 64 * (g % 2), g // 2
                mm = pe.matmul(bank[6][32 * g:32 * g + 32, 0:B8], q_new[half:half + 64, t, :], k_sb[half:half + 64, t, S:T], start=True, stop=True)
            mm.then_inc(s_psum, 1)
            pe.wait_ge(cache_loaded, 32)
            pe.wait_ge(win_copied, 4)
            for i in range(4):
                for b in range(2):
                    for t in range(2):
                        mm = pe.transpose(bank[i][:, P * (2 * b + t):P * (2 * b + t) + P], kc[:, 2 * i + b, P * t:P * t + P], ident)
                mm.then_inc(kcT_psum, 1)
            pe.wait_ge(kcT_copied, 4)
            for g in range(KV):
                half, t = 64 * (g % 2), g // 2
                for b in range(B8):
                    mm = pe.matmul(bank[4 - 4 * (g % 2)][:, 32 * g + 4 * b:32 * g + 4 * b + 4], kcT[half:half + 64, b, t, :],
                                   q_new[half:half + 64, t, 4 * b:4 * b + 4], start=True, stop=True)
            mm.then_inc(sT_psum, 1)
            pe.wait_ge(sT_copied, 1)
            pe.transpose(bank[5][:, 0:P], sT[:, :], ident).then_inc(s_psum, 1)
            pe.wait_ge(s_normed, 1)
            pe.transpose(bank[7][:, 0:P], s_rows[:, :], ident)
            pe.transpose(bank[7][0:B8, P:2 * P], pn8[:, :], ident).then_inc(pT_psum, 1)
            pe.wait_ge(pT_copied, 1)
            for g in range(KV):
                for rows in (slice(0, HD), slice(HD, P)):
                    pe.matmul(bank[4][rows, 32 * g:32 * g + 32], v_sb[0:B8, 8, HD * g:HD * g + HD],
                              pn8T[0:B8, 32 * g:32 * g + 32], start=True, stop=False)
                    for b in range(B8):
                        mm = pe.matmul(bank[4][rows, 32 * g + 4 * b:32 * g + 4 * b + 4], vc[:, b, HD * g:HD * g + HD],
                                       pT[:, 32 * g + 4 * b:32 * g + 4 * b + 4], start=False, stop=b == B8 - 1)
            mm.then_inc(so_psum, 1)

            def unit_c(jj, s, xh, xl):
                pe.wait_ge(lo_ready, jj * 2 + (U_C + s + 1))
                for c in range(3):
                    if s == 0:
                        pe.wait_ge(chunk_out, jj * 3 + (109 + c))
                    else:
                        pe.wait_ge(gate_out, jj * 3 + (c + 1))
                    unit_chunk(s, xh, xl, c)

            unit_c(0, 0, h_hi, h_lo)
            pe.wait_ge(o_lo_done, KT)
            unit_c(0, 1, o_hi, o_lo)
            with pe.Fori(1, KT) as j:
                unit_c(j, 0, h_hi, h_lo)
                unit_c(j, 1, o_hi, o_lo)
            unit_c(KT, 0, h_hi, h_lo)
            pe.wait_ge(a_lo_done, KT)
            unit_c(KT, 1, a_hi, a_lo)
            with pe.Fori(KT + 1, 2 * KT) as j:
                unit_c(j, 0, h_hi, h_lo)
                unit_c(j, 1, a_hi, a_lo)

            def rank(n, par, rows):
                pe.wait_ge(picks_done, n + 1)
                pe.wait_ge(seen_done, n + 1)
                pe.matmul(bank[7][0:rows, 0:NE], tab[0:rows, C_SLT:C_SLT + rows], picks[0:rows, par, :], start=True, stop=False)
                pe.matmul(bank[7][0:rows, 0:NE], tab[:, C_ONE:C_ONE + 1].to_broadcast([P, rows]), seen[:, :],
                          start=False, stop=True).then_inc(rank_done, 1)

            def turn_xn(n, rows):
                pe.wait_ge(xn_done, n + 1)
                for k in range(KT):
                    mm = pe.transpose(bank[4 + k // 4][:, P * (k % 4):P * (k % 4) + rows], xn[0:rows, P * k:P * k + P], ident[0:rows, 0:rows])
                mm.then_inc(xnT_psum, 1)

            def route(n, rows):
                pe.wait_ge(h2T_done, n + 1)
                for k in range(KT):
                    mm = pe.matmul(bank[6][0:rows, 0:36], h2T[:, k, 0:rows], wr[:, k, :], start=k == 0, stop=k == KT - 1)
                mm.then_inc(logits_done, 1)

            def step_d(n, par, rows, before=True, ranked=True):
                if ranked:
                    rank(n - 2, par, P)
                pe.wait_ge(mix_lo_done, n + 1)
                for k in range(KT):
                    if k == 4 and before:
                        turn_xn(n - 1, P)
                    if k == 7 and before:
                        route(n - 1, P)
                    out = [bank[2 * par + x][0:rows, :] for x in range(2)]
                    half = [slice(0, 512), slice(512, D)]
                    for x in range(2):
                        pe.matmul(out[x], mix_hi[:, par, k, 0:rows], wo_hi[:, k, half[x]], start=k == 0, stop=False)
                    for x in range(2):
                        pe.matmul(out[x], mix_hi[:, par, k, 0:rows], wo_lo[:, k, half[x]], start=False, stop=False)
                    for x in range(2):
                        mm = pe.matmul(out[x], mix_lo[:, par, k, 0:rows], wo_hi[:, k, half[x]], start=False, stop=k == KT - 1)
                mm.then_inc(proj_done, 1)

            pe.wait_ge(wo_lo_done, 4)
            pe.wait_ge(chunk_out, 159)
            pe.wait_ge(router_loaded, 80)
            step_d(0, 0, P, False, False)
            step_d(1, 1, P, True, False)
            with pe.Fori(1, 4) as i:
                for b in range(2):
                    step_d(i * 2 + b, b, P)
            step_d(8, 0, B8)
            rank(7, 1, P)
            turn_xn(8, B8)
            route(8, B8)
            rank(8, 0, B8)
            pe.wait_ge(seen_done, NT + 1)
            pe.matmul(bank[6][0:NE, 0:1], seen[:, :], tab[:, C_ONE:C_ONE + 1], start=True, stop=True).then_inc(ov_psum, 1)
            pe.wait_ge(ov_sbuf, 1)
            pe.matmul(bank[7][0:NE, 0:1], tab[0:NE, C_SLT:C_SLT + NE], cnt[0:NE, 1:2], start=True, stop=True).then_inc(ov_psum, 1)
            pe.wait_ge(ov_sbuf, 2)
            pe.matmul(bank[6][0:1, 0:2 * OVF + 1], tab[0:NE, C_ONE:C_ONE + 1], ov_b[0:NE, :], start=True, stop=True).then_inc(ov_psum, 1)

            def turn_x(par, e):
                pe.wait_ge(gathered[par], (e - par) * 8 + 16 if isinstance(e, int) else e * 8 + (16 - 8 * par))
                for k in range(KT):
                    mm = pe.transpose(bank[4 + k // 4][:, P * (k % 4):P * (k % 4) + P], xg[:, par, P * k:P * k + P], ident)
                mm.then_inc(xT_psum, 1)

            def chunk_gu(s, slot, c, par, out):
                pe.wait_ge(e_lo_done, s + 1)
                for k in range(4):
                    kk = 4 * (c % 2) + k
                    wh, wl = e_hi[:, slot % 4, 512 * k:512 * k + 512], e_lo[slot][:, 512 * k:512 * k + 512]
                    pe.matmul(out, xT_hi[:, par, kk, :], wh, start=kk == 0, stop=False)
                    pe.matmul(out, xT_hi[:, par, kk, :], wl, start=False, stop=False)
                    mm = pe.matmul(out, xT_lo[:, par, kk, :], wh, start=False, stop=kk == KT - 1)
                mm.then_inc(e_used, 1)

            def chunk_d(s, slot, c):
                pe.wait_ge(e_lo_done, s + 1)
                for k in range(2):
                    kk = 2 * (c % 2) + k
                    w_h, w_l = e_hi[:, slot % 4, :], e_lo[slot][:, :]
                    for a, w, st in ((aT_hi, w_h, kk == 0), (aT_hi, w_l, False), (aT_lo, w_h, False)):
                        for x in range(2):
                            mm = pe.matmul(bank[2 + x][:, :], a[:, kk, :], w[:, 1024 * k + 512 * x:1024 * k + 512 * x + 512],
                                           start=st, stop=kk == 3 and a is aT_lo)
                mm.then_inc(e_used, 1)

            def turn_act(e):
                pe.wait_ge(act_done, e + 1)
                if not isinstance(e, int) or e > 0:
                    pe.wait_ge(aT_lo_done, e)
                for k in range(4):
                    mm = pe.transpose(bank[6][:, P * k:P * k + P], act_sb[:, P * k:P * k + P], ident)
                mm.then_inc(aT_psum, 1)

            def step_e(e, par, s, slot, down, more):
                pe.wait_ge(xT_lo_done, e + 1)
                if down:
                    pe.wait_ge(silu_done, e)
                chunk_gu(s, slot, 0, par, bank[0][:, :])
                chunk_gu(s + 1, (slot + 1) % 12, 1, par, bank[0][:, :])
                if down:
                    turn_act(e - 1)
                chunk_gu(s + 2, (slot + 2) % 12, 2, par, bank[1][:, :])
                chunk_gu(s + 3, (slot + 3) % 12, 3, par, bank[1][:, :])
                if more:
                    turn_x(1 - par, e + 1)
                if down:
                    down_e(e - 1, s + 4, (slot + 4) % 12)

            def down_e(e, s, slot):
                pe.wait_ge(aT_lo_done, e + 1)
                if not isinstance(e, int) or e > 0:
                    pe.wait_ge(y_stored, e)
                chunk_d(s, slot, 0)
                chunk_d(s + 1, slot + 1, 1)

            turn_x(0, 0)
            step_e(0, 0, 0, 0, False, True)
            step_e(1, 1, 4, 4, True, True)
            with pe.Fori(1, 15) as i:
                for b in range(2):
                    step_e(i * 2 + b, b, i * 12 + (6 * b - 2), (6 * b - 2) % 12, True, True)
            step_e(30, 0, 178, 10, True, True)
            step_e(31, 1, 184, 4, True, False)
            turn_act(31)
            down_e(31, 190, 10)

            n_ov = pe.value_load(ov_t[0:1, 2 * OVF:2 * OVF + 1], min_val=0, max_val=OVF)
            with pe.Fori(0, OVF) as i:
                with pe.If(i < n_ov):
                    pe.wait_ge(v_gathered, i * 16 + 16)
                    for k in range(KT):
                        mm = pe.transpose(bank[4 + k // 4][:, P * (k % 4):P * (k % 4) + P], xg[:, 0, P * k:P * k + P], ident)
                    mm.then_inc(v_xpsum, 1)
                    pe.wait_ge(v_xT_done, i + 1)
                    pe.wait_ge(v_loaded, i * 48 + 48)
                    for x, w in enumerate((v_gate, v_up)):
                        for k in range(KT):
                            mm = pe.matmul(bank[x][:, :], v_xT[:, k, :], w[:, k, :], start=k == 0, stop=k == KT - 1)
                    mm.then_inc(v_gu, 1)
                    pe.wait_ge(v_act, i + 1)
                    for k in range(4):
                        mm = pe.transpose(bank[6][:, P * k:P * k + P], act_sb[:, P * k:P * k + P], ident)
                    mm.then_inc(v_apsum, 1)
                    pe.wait_ge(v_aT_done, i + 1)
                    for k in range(4):
                        for x in range(2):
                            mm = pe.matmul(bank[2 + x][:, :], v_aT[:, k, :], v_down[:, k, 512 * x:512 * x + 512], start=k == 0, stop=k == 3)
                    mm.then_inc(v_ypsum, 1)

        @block.scalar
        def _(act):
            A = nc.scalar
            step = Steps(act, act_step)

            def split_hi(u, slot, uses, freed):
                act.wait_ge(raw_loaded[slot], uses * 32)
                if freed is not None:
                    act.wait_ge(chunk_done, freed)
                A.activation(w_hi[:, slot, :, :], w_raw[slot][:, :, :], ACT.Copy).then_inc(hi_ready, 1)

            act.wait_ge(start_copied, 3)
            for g in range(3):
                act.wait_ge(x_loaded[g], 16)
                for n in range(4 * g, min(4 * g + 4, NT)):
                    rows = P if n < 8 else B8
                    step.after(A.activation(junk[0:rows, :], x_tok[0:rows, n, :], ACT.Square, accum_out=ssq[0:rows, n:n + 1]))
                rows, w = (P, 4) if g < 2 else (B8, 1)
                A.activation(rms[0:rows, 4 * g:4 * g + w], ssq[0:rows, 4 * g:4 * g + w], ACT.Sqrt, bias=eps[0:rows, 0:1],
                             scale=1.0 / D).then_inc(sqrt_done, 1)
                if g == 0:
                    split_hi(0, 0, 1, None)
            for g in range(2):
                for k in range(KT):
                    act.wait_ge(xT_ready, KT * g + k + 1)
                    A.activation(h_hi[:, k, 512 * g:512 * g + 512], bank[k][:, :], ACT.Copy, scale=g1[:, k:k + 1]).then_inc(h_hi_done, 1)

            def splits_a(t):
                split_hi(t * 5 + 1, 1, t * 2 + 1, None if isinstance(t, int) and t == 0 else t * 15)
                split_hi(t * 5 + 2, 2, t + 1, t * 15 + 3)
                split_hi(t * 5 + 3, 0, t * 2 + 2, t * 15 + 6)
                split_hi(t * 5 + 4, 1, t * 2 + 2, t * 15 + 9)
                split_hi(t * 5 + 5, 0, t * 2 + 3, t * 15 + 12)

            splits_a(0)
            with act.Fori(1, 2) as t:
                splits_a(t)
            split_hi(U_V + 1, 1, 5, 30)
            split_hi(U_B, 0, 6, 39)

            def store_o(hf, b):
                act.wait_ge(o_turned, b * 2 + (hf + 1))
                A.activation(q_sb[:, 4 * hf:4 * hf + 4, bass.ds(b * P, P)], OTB[:, :].rearrange("p (k t) -> p k t", k=4), ACT.Copy).then_inc(o_stored, 1)

            def step_b(j, first):
                for i in range(9):
                    if i > 0:
                        st = i - 1
                        act.wait_ge(probs_turned, j * 8 + (st + 1))
                        if not (first and st < 2):
                            act.wait_ge(pv_done, j * 8 + (st - 1))
                        if first:
                            for h in range(2):
                                ins = A.activation(probsT[:, st % 2, 2 * h + 1, :], PTB[:, P * (2 * h + 1):P * (2 * h + 2)], ACT.Copy)
                            ins.then_inc(probsT_ready, 1)
                        else:
                            A.activation(probsT[:, st % 2, :, :], PTB[:, :].rearrange("p (k t) -> p k t", k=4), ACT.Copy).then_inc(probsT_ready, 1)
                    if i == 5:
                        store_o(0, j)
                    if i < 8:
                        off = P if first else 0
                        act.wait_ge(max_ready, j * 8 + (i + 1))
                        for h in range(2):
                            head = 2 * i + h
                            pr = probs[:, i % 2, h, off:256]
                            A.activation(pr, pr, ACT.Exp, bias=negm[:, head:head + 1], scale=SCALE, accum_out=den[:, head:head + 1])
                        A.activation(esink[:, 2 * i:2 * i + 2], sinkd[:, 2 * i:2 * i + 2], ACT.Exp).then_inc(probs_ready, 1)
                    if i == 0:
                        split_hi(j * 3 + (U_B + 1), 1, j + 6, j * 9 + 39)
                    if i == 3:
                        split_hi(j * 3 + (U_B + 2), 2, j + 3, j * 9 + 42)
                    if i == 6:
                        split_hi(j * 3 + (U_B + 3), 0, j + 7, j * 9 + 45)
                store_o(1, j)

            step_b(0, True)
            with act.Fori(1, KT) as j:
                step_b(j, False)

            for i in range(4):
                act.wait_ge(kcT_psum, i + 1)
                A.activation(kcT[:, 2 * i:2 * i + 2, :, :], bank[i][:, :].rearrange("p (b t s) -> p b t s", b=2, t=2), ACT.Copy).then_inc(kcT_copied, 1)
            act.wait_ge(s_max, 1)
            A.activation(s_rows[:, :], s_rows[:, :], ACT.Exp, bias=sc[:, 1:2], scale=SCALE, accum_out=sc[:, 2:3])
            A.activation(sc[:, 3:4], sc[:, 0:1], ACT.Exp, bias=sc[:, 1:2], scale=SCALE)
            A.activation(sc[:, 4:5], sinkc[:, :], ACT.Exp, bias=sc[:, 1:2]).then_inc(s_exp, 1)

            act.wait_ge(so_stored, 1)
            act.wait_ge(v_out, 32)
            for k in range(KT):
                A.activation(o_hi[:, k, :], q_sb[:, k, :], ACT.Copy).then_inc(o_hi_done, 1)

            def step_c(jj, more):
                split_hi(jj * 2 + (U_C + 1), 1, jj + 14, jj * 6 + 111)
                for c in range(3):
                    act.wait_ge(chunk_done, jj * 6 + (111 + c + 1))
                    A.activation(gate[:, CH * c:CH * c + CH], DN[c][:, 0:CH], ACT.Sigmoid).then_inc(gate_out, 1)
                if more:
                    split_hi(jj * 2 + (U_C + 2), 0, jj + 15, jj * 6 + 114)

            with act.Fori(0, KT) as jj:
                step_c(jj, True)
            act.wait_ge(a_loaded, 16)
            for k in range(KT):
                A.activation(a_hi[:, k, :], a_raw[:, k, :], ACT.Copy).then_inc(a_hi_done, 1)
            with act.Fori(KT, 2 * KT - 1) as jj:
                step_c(jj, True)
            step_c(2 * KT - 1, False)

            for i in range(4):
                act.wait_ge(wo_loaded[i], 16)
                A.activation(wo_hi[:, 2 * i:2 * i + 2, :], wo_raw[:, 2 * i:2 * i + 2, :], ACT.Copy).then_inc(wo_hi_done, 1)
            act.wait_ge(chunk_out, 159)

            def mix_split(n, par, rows, first=False):
                if not first:
                    act.wait_ge(proj_done, n - 1)
                A.activation(mix_hi[:, par, :, 0:rows], mix[:, :, bass.ds(n * P, rows)], ACT.Copy).then_inc(mix_hi_done, 1)

            def turned(n, rows):
                act.wait_ge(xnT_psum, n + 1)
                for x in range(2):
                    ins = A.activation(h2T[:, 4 * x:4 * x + 4, 0:rows], bank[4 + x][:, :].rearrange("p (k t) -> p k t", k=4)[:, :, 0:rows], ACT.Copy)
                ins.then_inc(h2T_done, 1)

            def norm2(n, par, rows):
                act.wait_ge(x2_done, n + 1)
                src = x2[0:rows, bass.ds(n, 1), :].rearrange("p a d -> p (a d)")
                A.activation(x_in[0:rows, par, :], src, ACT.Square, accum_out=ssq[0:rows, 0:1]).then_inc(sq2_done, 1)
                act.wait_ge(sq2_done, n + 1)
                A.activation(rms[0:rows, 0:1], ssq[0:rows, 0:1], ACT.Sqrt, bias=eps[0:rows, 0:1], scale=1.0 / D).then_inc(root2_done, 1)

            mix_split(0, 0, P, True)
            mix_split(1, 1, P, True)
            norm2(0, 0, P)
            mix_split(2, 0, P)
            turned(0, P)
            norm2(1, 1, P)

            def pair_d(i, rows):
                mix_split(i * 2 + 1, 1, P)
                turned(i * 2 - 1, P)
                norm2(i * 2, 0, P)
                mix_split(i * 2 + 2, 0, rows)
                turned(i * 2, P)
                norm2(i * 2 + 1, 1, P)

            with act.Fori(1, 3) as i:
                pair_d(i, P)
            pair_d(3, B8)
            turned(7, P)
            norm2(8, 0, B8)
            turned(8, B8)

            def e_split(s, slot, uses):
                act.wait_ge(e_loaded[slot], uses)
                if not isinstance(s, int) or s >= 4:
                    act.wait_ge(e_used, s - 3)
                A.activation(e_hi[:, slot % 4, :], e_raw[slot][:, :], ACT.Copy).then_inc(e_hi_done, 1)

            def x_split(e, par):
                act.wait_ge(xT_psum, e + 1)
                for x in range(2):
                    ins = A.activation(xT_hi[:, par, 4 * x:4 * x + 4, :], bank[4 + x][:, :].rearrange("p (k t) -> p k t", k=4), ACT.Copy)
                ins.then_inc(xT_hi_done, 1)

            def a_split(e):
                act.wait_ge(aT_psum, e + 1)
                A.activation(aT_hi[:, :, :], bank[6][:, :].rearrange("p (k t) -> p k t", k=4), ACT.Copy).then_inc(aT_hi_done, 1)

            def store_rows(e, s_end, first=False):
                act.wait_ge(e_used, s_end)
                if not first:
                    act.wait_ge(scattered, e * 16)
                for x in range(2):
                    ins = A.activation(y_out[:, 512 * x:512 * x + 512], bank[2 + x][:, :], ACT.Copy)
                ins.then_inc(y_stored, 1)

            def step_e(e, par, s, base, uses, first=False):
                sp_ = lambda c: e_split(s + c, (base + c) % 12, uses + 16 * ((base + c) // 12 + 1))
                if not first:
                    store_rows(e - 2, s, first=isinstance(e, int) and e == 2)
                sp_(3)
                sp_(4)
                silu_e(e, s + 2)
                a_split(e - 1)
                sp_(5)
                sp_(6)
                sp_(7)
                if isinstance(e, int) and e == NE - 1:
                    return
                x_split(e + 1, 1 - par)
                sp_(8)

            def silu_e(e, s):
                act.wait_ge(e_used, s)
                if not isinstance(e, int) or e > 0:
                    act.wait_ge(act_done, e)
                A.activation(sg[:, :], bank[0][:, :], ACT.Silu).then_inc(silu_done, 1)

            act.wait_ge(wsum_done, 1)
            A.activation(gl[:, :, :], gl[:, :, :], ACT.Exp)
            A.activation(wts[:, :, 1], wts[:, :, 1], ACT.Exp).then_inc(wexp_done, 1)
            act.wait_ge(proj_done, NT)
            e_split(0, 0, 16)
            x_split(0, 0)
            for c in range(1, 5):
                e_split(c, c, 16)
            silu_e(0, 2)
            e_split(5, 5, 16)
            x_split(1, 1)
            e_split(6, 6, 16)
            step_e(1, 1, 4, 4, 0, first=True)
            step_e(2, 0, 10, 10, 0)
            with act.Fori(1, 15) as i:
                step_e(i * 2 + 1, 1, i * 12 + 4, 4, i * 16)
                step_e(i * 2 + 2, 0, i * 12 + 10, 10, i * 16)
            step_e(31, 1, 184, 4, 240)
            store_rows(30, 190)
            a_split(31)
            store_rows(31, 192)

            n_ov = act.value_load(ov_t[0:1, 2 * OVF:2 * OVF + 1], min_val=0, max_val=OVF)
            with act.Fori(0, OVF) as i:
                with act.If(i < n_ov):
                    act.wait_ge(v_gu, i + 1)
                    A.activation(sg[:, :], bank[0][:, :], ACT.Silu).then_inc(v_silu, 1)
                    act.wait_ge(v_ypsum, i + 1)
                    act.wait_ge(v_free, i + 1)
                    for x in range(2):
                        ins = A.activation(y_out[:, 512 * x:512 * x + 512], bank[2 + x][:, :], ACT.Copy)
                    ins.then_inc(v_y, 1)

            def root(n, par, rows):
                act.wait_ge(f_sum, n + 1)
                A.activation(f_junk[0:rows, :], f_out[0:rows, par, :], ACT.Square, accum_out=ssq[0:rows, par:par + 1]).then_inc(f_sq, 1)
                act.wait_ge(f_sq, n + 1)
                A.activation(rms[0:rows, par:par + 1], ssq[0:rows, par:par + 1], ACT.Sqrt, bias=eps[0:rows, 0:1], scale=1.0 / D).then_inc(f_root, 1)

            act.wait_ge(rows_written, 1)
            with act.Fori(0, 4) as i:
                for b in range(2):
                    root(i * 2 + b, b, P)
            root(8, 0, B8)

        @block.vector
        def _(dve):
            V = nc.vector
            step = Steps(dve, dve_step)

            def split_lo(u, slot):
                dve.wait_ge(hi_ready, u + 1)
                V.tensor_tensor(w_lo[:, slot, :, :], w_raw[slot][:, :, :], w_hi[:, slot, :, :].bitcast(F32), ALU.subtract).then_inc(lo_ready, 1)

            step.after(V.memset(relb[:, :], 1.0))
            V.memset(list_init[:, :], NOROW).then_inc(list_filled, 1)
            V.memset(eps[:, :], EPS)
            V.memset(ssq[:, :], 1.0).then_inc(relb_ones, 1)
            dve.wait_ge(consts_loaded, 16 * N_CONSTS)
            relc_v = relc[0:33, :].rearrange("p (g b j) -> p g b j", g=4, b=8)
            for b in range(B8):
                ins = V.tensor_copy(relc_v[:, :, b, :], relb[0:33, :].rearrange("p (g j) -> p g j", g=4))
            ins.then_inc(relc_done, 1)
            step.after(V.tensor_scalar(sink8[:, :], sinkb[:, :], 1 / SCALE, None, ALU.mult))
            step.after(V.tensor_tensor_reduce(tmp8[:, 0:2, :].rearrange("p a b -> p (a b)"), sinkb[:, :], tab[:, C_HM:C_HM + 16], 1.0, 0.0, ALU.mult, ALU.add, sinkc[:, :]))
            for h in range(HEADS):
                dve.wait_ge(bias_psum, h + 1)
                V.tensor_copy(bias_row[:, h, :], bank[h % 4][:, 0:SKEW]).then_inc(bias_row_done, 1)
            dve.wait_ge(start_psum, 1)
            V.tensor_copy(bs8[:, :], bank[4][:, 0:129]).then_inc(start_copied, 1)
            dve.wait_ge(start_psum, 2)
            V.tensor_copy(histT[:, :, :, :], bank[5][:, 0:P].rearrange("p (k b r) -> p k r b", k=KT, b=B8)).then_inc(start_copied, 1)
            V.tensor_copy(cols32[:, :], bank[5][:, P:P + 32]).then_inc(start_copied, 1)
            for g in range(3):
                rows, w = (P, 4) if g < 2 else (B8, 1)
                dve.wait_ge(sqrt_done, g + 1)
                r = rms[0:rows, 4 * g:4 * g + w]
                step.after(V.reciprocal(r, r))
                for n in range(4 * g, 4 * g + w):
                    V.tensor_scalar(x_tok[0:rows, n, :], x_tok[0:rows, n, :], rms[0:rows, n:n + 1], None, ALU.mult).then_inc(x_scaled, 1)
                if g == 0:
                    split_lo(0, 0)
            for g in range(2):
                for k in range(KT):
                    dve.wait_ge(h_hi_done, KT * g + k + 1)
                    cols = slice(512 * g, 512 * g + 512)
                    V.scalar_tensor_tensor(h_lo[:, k, cols], bank[k][:, :], g1[:, k:k + 1], h_hi[:, k, cols].bitcast(F32),
                                           ALU.mult, ALU.subtract).then_inc(h_lo_done, 1)
            dve.wait_ge(xT_ready, 17)
            step.after(V.tensor_tensor(tmp8[:, :, :], bank[0][:, 0:64].rearrange("p (k b) -> p k b", k=KT),
                                       g1[:, :].unsqueeze(2).to_broadcast([P, KT, B8]), ALU.mult))
            step.after(V.tensor_copy(h_hi[:, :, S:T], tmp8[:, :, :]))
            V.tensor_tensor(h_lo[:, :, S:T], tmp8[:, :, :], h_hi[:, :, S:T].bitcast(F32), ALU.subtract).then_inc(h_lo_done, 1)

            def units_a(t):
                for i in range(5):
                    split_lo(t * 5 + (i + 1), (1, 2, 0, 1, 0)[i])
                    for c in range(3):
                        dve.wait_ge(chunk_done, t * 15 + (3 * i + c + 1))
                        dst = q_sb[:, bass.ds(t * 4 + i, 1), CH * c:CH * c + CH] if i < 4 else k_sb[:, bass.ds(t, 1), CH * c:CH * c + CH]
                        V.tensor_copy(dst, DN[c][:, 0:CH].unsqueeze(1)).then_inc(chunk_out, 1)

            with dve.Fori(0, 2) as t:
                units_a(t)
            split_lo(U_V + 1, 1)
            for n in range(NT):
                rows = P if n < 8 else B8
                dve.wait_ge(chunk_done, 31 + n)
                V.tensor_copy(v_sb[0:rows, n, :], DN[n % 3][0:rows, 0:256]).then_inc(chunk_out, 1)
            split_lo(U_B, 0)
            dve.wait_ge(bias_loaded, 16)
            step.after(V.memset(u_sb[:, 0:2], 0.0))

            def norm_o(hf, b):
                dve.wait_ge(pv_done, b * 8 + (4 * hf + 4))
                heads = slice(8 * hf, 8 * hf + 8)
                step.after(V.tensor_tensor(rden[:, heads], den[:, heads], esink[:, heads], ALU.add))
                step.after(V.reciprocal(rden[:, heads], rden[:, heads]))
                V.tensor_tensor(o_tok[:, 512 * hf:512 * hf + 512].rearrange("p (h d) -> p h d", h=8),
                                OB[:, :].rearrange("p (h d) -> p h d", h=8),
                                rden[:, heads].unsqueeze(2).to_broadcast([P, 8, HD]), ALU.mult).then_inc(o_normed, 1)

            def step_b(j, first):
                n0 = step.n
                w = [cols32[:, bass.ds(j + (8 + 8 * i), 1)] for i in range(3)]
                for i in range(9):
                    c = i % 3
                    cols = slice(2 + CH * c, 2 + CH * c + CH)
                    if i < 8:
                        off = P if first else 0
                        dve.wait_ge(scores_ready, j * 8 + (i + 1))
                        if not (first and i < 2):
                            dve.wait_ge(probs_turned, j * 8 + (i - 1))
                        V.memset(carrier[:, :], 0.0)
                        for h in range(2):
                            head = 2 * i + h
                            ins = V.tensor_tensor_reduce(probs[:, i % 2, h, off:256], SCB[i % 2][:, 256 * h + off:256 * h + 256],
                                                         bias_sb[:, head, off:256], 1.0, sink8[:, head:head + 1],
                                                         ALU.add, ALU.max, maxs[:, head:head + 1])
                        step.after(ins)
                        pair = slice(2 * i, 2 * i + 2)
                        step.after(V.tensor_scalar(negm[:, pair], maxs[:, pair], -SCALE, None, ALU.mult))
                        V.tensor_tensor(sinkd[:, pair], sinkb[:, pair], negm[:, pair], ALU.add).then_inc(max_ready, 1)
                    if i == 6:
                        if not first:
                            dve.wait_ge(a_spilled, j * 16)
                        hist = [histT[:, bass.ds(j, 1), r, :].rearrange("p a b -> p (a b)") for r in range(2)]
                        V.tensor_copy(ustate[:, bass.ds(j, 1), :], u_sb[:, S:S + 10].unsqueeze(1))
                        V.tensor_scalar(y_sb[:, 0:S], u_sb[:, 0:S], w[0], None, ALU.mult)
                        step.after(V.tensor_scalar(y_sb[:, S:T], hist[0], w[0], None, ALU.mult))
                        V.scalar_tensor_tensor(y_sb[:, 0:S], u_sb[:, 1:S + 1], w[1], y_sb[:, 0:S], ALU.mult, ALU.add)
                        step.after(V.scalar_tensor_tensor(y_sb[:, S:T], hist[1], w[1], y_sb[:, S:T], ALU.mult, ALU.add))
                        step.after(V.scalar_tensor_tensor(y_sb[:, :], u_sb[:, 2:T + 2], w[2], y_sb[:, :], ALU.mult, ALU.add))
                    if i % 3 == 0:
                        split_lo(j * 3 + (U_B + i // 3 + 1), (i // 3 + 1) % 3)
                    if i == 4:
                        norm_o(0, j)
                    if i == 8:
                        norm_o(1, j)
                    dve.wait_ge(chunk_done, j * 9 + (39 + i + 1))
                    if i < 3:
                        V.tensor_copy(u_sb[:, cols], DN[c][:, 0:CH]).then_inc(chunk_out, 1)
                    elif i < 6:
                        dve.wait_ge(chunk_out, j * 9 + (39 + i - 2))
                        V.tensor_tensor(u_sb[:, cols], u_sb[:, cols], DN[c][:, 0:CH], ALU.mult).then_inc(chunk_out, 1)
                        if i == 5:
                            dve.wait_ge(chunk_out, j * 9 + (39 + 6))
                    else:
                        y = y_sb[:, CH * c:CH * c + CH]
                        V.tensor_tensor(y, y, DN[c][:, 0:CH], ALU.mult).then_inc(chunk_out, 1)
                return step.n

            n0 = step.n
            per = step_b(0, True) - n0
            n1 = step.n
            with dve.Fori(1, KT) as j:
                step.n = j * per + (n1 - per)
                step_b(j, False)
            step.n = n1 + (KT - 1) * per

            for i, (dst, src) in enumerate(((k_out[:, 0, :], bank[0][:, 0:256]), (k_out[0:B8, 1, :], bank[1][0:B8, 0:256]),
                                            (u_out[0:10, 0:512], bank[2][0:10, :]), (u_out[0:10, 512:D], bank[3][0:10, :]))):
                dve.wait_ge(win_psum, i + 1)
                if i == 0:
                    dve.wait_ge(o_stored, 16)
                    dve.wait_ge(a_spilled, 16 * KT)
                V.tensor_copy(dst, src).then_inc(win_copied, 1)
            for t in range(2):
                ins = V.tensor_copy(q_new[:, t, :].rearrange("p (b j) -> p j b", j=4), q_sb[:, 4 * t:4 * t + 4, S:T])
            ins.then_inc(q_new_done, 1)
            dve.wait_ge(sT_psum, 1)
            for x in range(2):
                pick = lambda t: t.rearrange("p (t x c) -> p t x c", t=2, x=2)[:, :, x, :]
                ins = V.tensor_copy(pick(sT[:, :]), pick(bank[4 - 4 * x][:, 0:P]))
            ins.then_inc(sT_copied, 1)
            dve.wait_ge(s_psum, 2)
            step.after(V.tensor_tensor_reduce(pn8[:, :], bank[6][:, 0:B8], tab[:, C_MB:C_MB + 8], 1.0, 0.0, ALU.mult, ALU.add, sc[:, 0:1]))
            step.after(V.tensor_tensor(sc[:, 0:1], sc[:, 0:1], bs8[:, 128:129], ALU.add))
            step.after(V.scalar_tensor_tensor(sc[:, 5:6], sinkc[:, :], 1 / SCALE, sc[:, 0:1], ALU.mult, ALU.max))
            step.after(V.tensor_tensor_reduce(s_rows[:, :], bank[5][:, 0:P], bs8[:, 0:P], 1.0, sc[:, 5:6], ALU.add, ALU.max, sc[:, 6:7]))
            V.tensor_scalar(sc[:, 1:2], sc[:, 6:7], -SCALE, None, ALU.mult).then_inc(s_max, 1)
            dve.wait_ge(s_exp, 1)
            step.after(V.tensor_tensor(sc[:, 7:8], sc[:, 2:3], sc[:, 3:4], ALU.add))
            step.after(V.tensor_tensor(sc[:, 7:8], sc[:, 7:8], sc[:, 4:5], ALU.add))
            step.after(V.reciprocal(sc[:, 7:8], sc[:, 7:8]))
            V.tensor_scalar(s_rows[:, :], s_rows[:, :], sc[:, 7:8], None, ALU.mult)
            V.tensor_scalar(pn8[:, :], tab[:, C_MB:C_MB + 8], sc[:, 3:4], sc[:, 7:8], ALU.mult, ALU.mult).then_inc(s_normed, 1)
            dve.wait_ge(pT_psum, 1)
            V.tensor_copy(pT[:, :], bank[7][:, 0:P])
            V.tensor_copy(pn8T[0:B8, :], bank[7][0:B8, P:2 * P]).then_inc(pT_copied, 1)
            dve.wait_ge(so_psum, 1)
            for x in range(2):
                src = bank[4][64 * x:64 * x + 64, 0:P].rearrange("p (g b t x) -> p g t b x", g=KV, b=B8, t=2)[:, :, :, :, x]
                dst = q_sb[64 * x:64 * x + 64, :, S:T].rearrange("p (g t) b -> p g t b", g=KV)
                ins = V.tensor_copy(dst, src)
            ins.then_inc(so_stored, 1)

            for k in range(KT):
                dve.wait_ge(o_hi_done, k + 1)
                V.tensor_tensor(o_lo[:, k, :], q_sb[:, k, :], o_hi[:, k, :].bitcast(F32), ALU.subtract).then_inc(o_lo_done, 1)

            def step_c(jj, more, conv):
                split_lo(jj * 2 + (U_C + 1), 1)
                if more:
                    split_lo(jj * 2 + (U_C + 2), 0)
                for c in range(3):
                    cols = slice(CH * c, CH * c + CH)
                    dve.wait_ge(chunk_done, jj * 6 + (111 + 3 + c + 1))
                    m = mix[:, bass.ds(jj - KT if conv else jj, 1), cols].rearrange("p a t -> p (a t)")
                    if not conv:
                        V.tensor_tensor(m, gate[:, cols], DN[c][:, 0:CH], ALU.mult).then_inc(chunk_out, 1)
                    else:
                        step.after(V.tensor_tensor(gate[:, cols], gate[:, cols], DN[c][:, 0:CH], ALU.mult))
                        V.tensor_tensor(m, m, gate[:, cols], ALU.add).then_inc(chunk_out, 1)

            dve.wait_ge(states_out, 16 * 7)
            with dve.Fori(0, KT) as jj:
                step_c(jj, True, False)
            for k in range(KT):
                dve.wait_ge(a_hi_done, k + 1)
                V.tensor_tensor(a_lo[:, k, :], a_raw[:, k, :], a_hi[:, k, :].bitcast(F32), ALU.subtract).then_inc(a_lo_done, 1)
            n0 = step.n
            with dve.Fori(KT, 2 * KT - 1) as jj:
                step.n = jj * 3 + (n0 - 3 * KT)
                step_c(jj, True, True)
            step.n = n0 + 3 * (KT - 1)
            step_c(2 * KT - 1, False, True)

            V.memset(lg[:, NG:8], -3e38)
            V.memset(seen[:, :], 0.0)
            V.memset(gl[:, :, :], 0.0)
            V.memset(tv[:, :, :], 0.0)
            V.tensor_copy(tok_u[:, :], tab[:, C_TOK:C_TOK + 2 * NT]).then_inc(seen_done, 1)
            for i in range(4):
                dve.wait_ge(wo_hi_done, i + 1)
                V.tensor_tensor(wo_lo[:, 2 * i:2 * i + 2, :], wo_raw[:, 2 * i:2 * i + 2, :], wo_hi[:, 2 * i:2 * i + 2, :].bitcast(F32),
                                ALU.subtract).then_inc(wo_lo_done, 1)

            def mix_split(n, par, rows):
                dve.wait_ge(mix_hi_done, n + 1)
                V.tensor_tensor(mix_lo[:, par, :, 0:rows], mix[:, :, bass.ds(n * P, rows)], mix_hi[:, par, :, 0:rows].bitcast(F32),
                                ALU.subtract).then_inc(mix_lo_done, 1)

            def residual(n, par, rows, uses):
                dve.wait_ge(proj_done, n + 1)
                dve.wait_ge(x_again[par], uses)
                dst = x2[0:rows, bass.ds(n, 1), :].rearrange("p a d -> p (a d)")
                for x in range(2):
                    half = slice(512 * x, 512 * x + 512)
                    ins = V.tensor_tensor(dst[:, half], bank[2 * par + x][0:rows, :], x_in[0:rows, par, half], ALU.add)
                ins.then_inc(x2_done, 1)

            def second_norm(n, rows, first=False):
                dve.wait_ge(root2_done, n + 1)
                step.after(V.reciprocal(rms[0:rows, 1:2], rms[0:rows, 0:1]))
                if not first:
                    dve.wait_ge(xn_written, n * 16)
                    dve.wait_ge(xnT_psum, n)
                src = x2[0:rows, bass.ds(n, 1), :].rearrange("p a d -> p (a d)")
                V.scalar_tensor_tensor(xn[0:rows, :], src, rms[0:rows, 1:2], g2b[0:rows, :], ALU.mult, ALU.mult).then_inc(xn_done, 1)

            def carry():
                V.memset(carrier[:, :], 0.0)

            def choose(n, par, r):
                dve.wait_ge(logits_done, n + 1)
                V.tensor_tensor(lg[0:r, 0:NG], bank[6][0:r, 0:NG], rb[0:r, 0:NG], ALU.add)
                step.after(V.tensor_tensor(lg[0:r, 8:40], bank[6][0:r, NG:36], rb[0:r, NG:36], ALU.add))
                carry()
                step.after(V.max(top_g[0:r, :], lg[0:r, 0:8]))
                carry()
                step.after(V.max_index(idx_g[0:r, :], top_g[0:r, :], lg[0:r, 0:8]))
                V.tensor_scalar(gl[0:r, bass.ds(n, 1), :].rearrange("p a g -> p (a g)"), lg[0:r, 0:NG], top_g[0:r, 0:1], None, ALU.subtract)
                step.after(V.tensor_copy(grp[0:r, 0:1], idx_g[0:r, 0:1]))
                V.tensor_scalar(grp[0:r, 1:2], grp[0:r, 0:1], float(EG), None, ALU.mult)
                step.after(V.tensor_scalar(oh4[0:r, :], tab[0:r, C_IO:C_IO + NG], grp[0:r, 0:1], None, ALU.is_equal))
                step.after(V.tensor_tensor(prod[0:r, :, :], lg[0:r, 8:40].rearrange("p (g e) -> p e g", g=NG),
                                           oh4[0:r, :].unsqueeze(1).to_broadcast([r, EG, NG]), ALU.mult))
                step.after(V.tensor_reduce(e8[0:r, :], prod[0:r, :, :], AX.X, ALU.add))
                carry()
                step.after(V.max(top_e[0:r, :], e8[0:r, :]))
                V.tensor_copy(tv[0:r, bass.ds(n, 1), :], top_e[0:r, 0:2].unsqueeze(1))
                step.after(V.max_index(idx_e[0:r, :], top_e[0:r, :], e8[0:r, :]))
                step.after(V.tensor_copy(idx_f[0:r, :], idx_e[0:r, 0:2]))
                step.after(V.tensor_scalar(picked[0:r, par, :], idx_f[0:r, :], grp[0:r, 1:2], None, ALU.add))
                for k in range(2):
                    ins = V.tensor_scalar(hots[0:r, par, k, :], tab[0:r, C_IO:C_IO + NE], picked[0:r, par, k:k + 1], None, ALU.is_equal)
                step.after(ins)
                V.tensor_tensor(picks[0:r, par, :], hots[0:r, par, 0, :], hots[0:r, par, 1, :], ALU.add).then_inc(picks_done, 1)

            def address(n, par, r):
                dve.wait_ge(rank_done, n + 1)
                carry()
                for k in range(2):
                    ins = V.tensor_tensor_reduce(prod[0:r, :, :].rearrange("p a b -> p (a b)"), hots[0:r, par, k, :], bank[7][0:r, 0:NE],
                                                 1.0, 0.0, ALU.mult, ALU.add, rank2[0:r, k:k + 1])
                    step.after(ins)
                step.after(V.scalar_tensor_tensor(adr_f[0:r, :], rank2[0:r, :], float(NE), picked[0:r, par, :], ALU.mult, ALU.add))
                V.tensor_copy(adr[0:r, bass.ds(n * 2, 2)], adr_f[0:r, :]).then_inc(adr_done, 1)
                V.tensor_tensor(seen[0:r, :], seen[0:r, :], picks[0:r, par, :], ALU.add).then_inc(seen_done, 1)

            mix_split(0, 0, P)
            mix_split(1, 1, P)
            dve.wait_ge(router_loaded, 80)
            residual(0, 0, P, 16)
            second_norm(0, P, True)
            mix_split(2, 0, P)
            choose(0, 0, P)
            residual(1, 1, P, 16)
            second_norm(1, P)
            n0 = step.n

            def pair_d(i, rows):
                mix_split(i * 2 + 1, 1, P)
                address(i * 2 - 2, 0, P)
                choose(i * 2 - 1, 1, P)
                residual(i * 2, 0, P, i * 16 + 16)
                second_norm(i * 2, P)
                mix_split(i * 2 + 2, 0, rows)
                address(i * 2 - 1, 1, P)
                choose(i * 2, 0, P)
                residual(i * 2 + 1, 1, P, i * 16 + 16)
                second_norm(i * 2 + 1, P)

            pair_steps = 32
            with dve.Fori(1, 3) as i:
                step.n = i * pair_steps + (n0 - pair_steps)
                pair_d(i, P)
            step.n = n0 + 2 * pair_steps
            pair_d(3, B8)
            assert step.n == n0 + 3 * pair_steps
            address(6, 0, P)
            choose(7, 1, P)
            residual(8, 0, B8, 80)
            second_norm(8, B8)
            address(7, 1, P)
            choose(8, 0, B8)
            address(8, 0, B8)

            dve.wait_ge(ov_psum, 1)
            step.after(V.tensor_copy(cnt[0:NE, 0:1], bank[6][0:NE, 0:1]))
            V.tensor_scalar(ov_a[0:NE, 0, 0:8], tab[0:NE, C_B128:C_B128 + 8], cnt[0:NE, 0:1], 0.0, ALU.is_lt, ALU.add,
                            accum_out=cnt[0:NE, 1:2]).then_inc(ov_sbuf, 1)
            dve.wait_ge(ov_psum, 2)
            step.after(V.tensor_copy(cnt[0:NE, 2:3], bank[7][0:NE, 0:1]))
            step.after(V.tensor_tensor(cnt[0:NE, 3:4], cnt[0:NE, 2:3], cnt[0:NE, 1:2], ALU.add))
            i16 = tab[0:NE, C_I16:C_I16 + OVF]
            V.tensor_scalar(ov_a[0:NE, 2, :], i16, cnt[0:NE, 2:3], 1.0, ALU.subtract, ALU.add)
            step.after(V.tensor_scalar(ov_a[0:NE, 1, :], i16, cnt[0:NE, 3:4], None, ALU.is_lt))
            step.after(V.scalar_tensor_tensor(ov_a[0:NE, 0, :], i16, cnt[0:NE, 2:3], ov_a[0:NE, 1, :], ALU.is_ge, ALU.mult))
            V.tensor_scalar(ov_b[0:NE, 0:OVF], ov_a[0:NE, 0, :], tab[0:NE, C_PIX:C_PIX + 1], None, ALU.mult)
            V.tensor_tensor(ov_b[0:NE, OVF:2 * OVF], ov_a[0:NE, 0, :], ov_a[0:NE, 2, :], ALU.mult)
            V.tensor_copy(ov_b[0:NE, 2 * OVF:2 * OVF + 1], cnt[0:NE, 1:2]).then_inc(ov_sbuf, 1)
            dve.wait_ge(ov_psum, 3)
            V.tensor_copy(ov_t[0:1, :], bank[6][0:1, 0:2 * OVF + 1]).then_inc(ov_sbuf, 1)

            def source_rows(dst, src, f, g):
                step.after(V.tensor_copy(f, src))
                step.after(V.tensor_scalar(g, f, float(T), -float(T), ALU.is_ge, ALU.mult))
                step.after(V.tensor_tensor(f, f, g, ALU.add))
                return V.tensor_scalar(dst, f, float(T - 1), None, ALU.min)

            dve.wait_ge(list_loaded, 16)
            source_rows(gidx[:, :], lst[:, :], lst_f[:, :], lst_g[:, :]).then_inc(gidx_done, 1)
            step.after(V.tensor_tensor(wts[:, :, 1], tv[:, :, 1], tv[:, :, 0], ALU.subtract))
            V.memset(carrier[:, :], 0.0).then_inc(wsum_done, 1)
            dve.wait_ge(wexp_done, 1)
            step.after(V.tensor_reduce(wsum[:, :], gl[:, :, :], AX.X, ALU.add))
            step.after(V.scalar_tensor_tensor(wsum[:, :], wts[:, :, 1], 1.0, wsum[:, :], ALU.add, ALU.mult))
            step.after(V.reciprocal(wts[:, :, 0], wsum[:, :]))
            step.after(V.tensor_tensor(wts[:, :, 1], wts[:, :, 1], wts[:, :, 0], ALU.mult))

            def e_split(s, slot):
                dve.wait_ge(e_hi_done, s + 1)
                V.tensor_tensor(e_lo[slot][:, :], e_raw[slot][:, :], e_hi[:, slot % 4, :].bitcast(F32), ALU.subtract).then_inc(e_lo_done, 1)

            def x_split(e, par):
                dve.wait_ge(xT_hi_done, e + 1)
                for x in range(2):
                    ins = V.tensor_tensor(xT_lo[:, par, 4 * x:4 * x + 4, :], bank[4 + x][:, :].rearrange("p (k t) -> p k t", k=4),
                                          xT_hi[:, par, 4 * x:4 * x + 4, :].bitcast(F32), ALU.subtract)
                ins.then_inc(xT_lo_done, 1)

            def a_split(e):
                dve.wait_ge(aT_hi_done, e + 1)
                V.tensor_tensor(aT_lo[:, :, :], bank[6][:, :].rearrange("p (k t) -> p k t", k=4), aT_hi[:, :, :].bitcast(F32),
                                ALU.subtract).then_inc(aT_lo_done, 1)

            def activate(e, s):
                dve.wait_ge(e_used, s)
                dve.wait_ge(silu_done, e + 1)
                if not isinstance(e, int) or e > 0:
                    dve.wait_ge(aT_psum, e)
                V.tensor_tensor(act_sb[:, :], sg[:, :], bank[1][:, :], ALU.mult).then_inc(act_done, 1)

            def step_e(e, par, s, base):
                sp_ = lambda c: e_split(s + c, (base + c) % 12)
                sp_(3)
                sp_(4)
                a_split(e - 1)
                sp_(5)
                sp_(6)
                activate(e, s + 4)
                sp_(7)
                if isinstance(e, int) and e == NE - 1:
                    return
                x_split(e + 1, 1 - par)
                sp_(8)

            e_split(0, 0)
            x_split(0, 0)
            for c in range(1, 6):
                e_split(c, c)
            activate(0, 4)
            x_split(1, 1)
            e_split(6, 6)
            with dve.Fori(0, 15) as i:
                step_e(i * 2 + 1, 1, i * 12 + 4, 4)
                step_e(i * 2 + 2, 0, i * 12 + 10, 10)
            step_e(31, 1, 184, 4)
            a_split(31)

            n_ov = dve.value_load(ov_t[0:1, 2 * OVF:2 * OVF + 1], min_val=0, max_val=OVF)
            n0 = step.n
            with dve.Fori(0, OVF) as i:
                with dve.If(i < n_ov):
                    step.n = i * 3 + n0
                    dve.wait_ge(v_col, i * 16 + 16)
                    source_rows(gcol[:, 0:1], scol[:, 0:1], lst_f[:, 0:1], lst_g[:, 0:1]).then_inc(v_idx, 1)
                    dve.wait_ge(v_xpsum, i + 1)
                    for x in range(2):
                        ins = V.tensor_copy(v_xT[:, 4 * x:4 * x + 4, :], bank[4 + x][:, :].rearrange("p (k t) -> p k t", k=4))
                    ins.then_inc(v_xT_done, 1)
                    dve.wait_ge(v_silu, i + 1)
                    V.tensor_tensor(act_sb[:, :], sg[:, :], bank[1][:, :], ALU.mult).then_inc(v_act, 1)
                    dve.wait_ge(v_apsum, i + 1)
                    V.tensor_copy(v_aT[:, :, :], bank[6][:, :].rearrange("p (k t) -> p k t", k=4)).then_inc(v_aT_done, 1)

            fin_step = Steps(dve, sem("fin_step"))
            dve.wait_ge(gf_loaded, 16)

            def combine(n, par, rows, uses, first=False):
                dve.wait_ge(f_loaded[par], uses)
                if not first:
                    dve.wait_ge(f_stored[par], uses // 2 - 16)
                out, x = f_out[0:rows, par, :], x2[0:rows, bass.ds(n, 1), :].rearrange("p a d -> p (a d)")
                w = [wts[0:rows, bass.ds(n, 1), k] for k in range(2)]
                fin_step.after(V.scalar_tensor_tensor(out, f_y[0][0:rows, par, :], w[0], x, ALU.mult, ALU.add))
                V.scalar_tensor_tensor(out, f_y[1][0:rows, par, :], w[1], out, ALU.mult, ALU.add).then_inc(f_sum, 1)

            def finish(n, par, rows):
                dve.wait_ge(f_root, n + 1)
                fin_step.after(V.reciprocal(rms[0:rows, par + 2:par + 3], rms[0:rows, par:par + 1]))
                out = f_out[0:rows, par, :]
                V.scalar_tensor_tensor(out, out, rms[0:rows, par + 2:par + 3], gfb[0:rows, :], ALU.mult, ALU.mult).then_inc(f_done, 1)

            for n in range(NT):
                combine(n, n % 2, P if n < 8 else B8, 32 * (n // 2 + 1), n < 2)
                if n >= 1:
                    finish(n - 1, (n - 1) % 2, P)
            finish(8, 0, B8)


_INS = ["x_prompt", "x_sample", "cache_conv", "cache_k", "cache_v", "norm1_g", "w_in", "conv_w", "w_conv_out",
        "w_attn_out", "w_o", "sinks", "rel_bias", "norm2_g", "w_router_group", "b_router_group",
        "w_router_expert", "b_router_expert", "w_e_gate", "w_e_up", "w_e_down", "norm_f_g"]
_OUTS = [(1, S, D), (B8, 1, D), (1, 1, 2, D), (1, 1, WIN, KV, HD), (1, 1, WIN, KV, HD),
         (1, B8, 2, D), (1, B8, WIN, KV, HD), (1, B8, WIN, KV, HD)]


def kernel(**inputs):
    import numpy as _np
    import concourse.bacc as _bacc
    from concourse import mybir as _mybir
    from concourse.bass_utils import run_bass_kernel_spmd as _run

    nc = _bacc.Bacc("TRN2", target_bir_lowering=False, num_devices=1)
    table, onehot = constants()
    arrays, args = {}, []
    for name in _INS + ["table", "onehot"]:
        a = table if name == "table" else onehot if name == "onehot" else _np.ascontiguousarray(inputs[name])
        arrays[f"in_{name}_dram"] = a
        args.append(nc.dram_tensor(f"in_{name}_dram", a.shape, _mybir.dt.from_np(a.dtype), kind="ExternalInput").ap())
    for i, shape in enumerate(_OUTS):
        args.append(nc.dram_tensor(f"out_{i}_dram", shape, _mybir.dt.float32, kind="ExternalOutput").ap())
    program(nc, *args)
    r = _run(nc, [arrays], core_ids=[0])
    return tuple(r.results[0][f"out_{i}_dram"] for i in range(len(_OUTS)))
```

```python
from contextlib import ExitStack

import numpy as np
import concourse.bass as bass
from concourse import mybir

F32 = mybir.dt.float32
F32R = mybir.dt.float32r
U32 = mybir.dt.uint32
ALU = mybir.AluOpType
ACT = mybir.ActivationFunctionType
AX = mybir.AxisListType

P = 128
D = 1024
KT = D // P
S = 1024
B8 = 8
T = S + B8
NT = 9
CH = T // 3
HEADS, KV, HD, WIN = 16, 4, 64, 128
NBUCKET, MAXD = 32, 128
NE, NG, EG, FE = 32, 4, 8, 512
EPS = 1e-6
SCALE = HD ** -0.5
MASKED = -1e30
COL_CB, COL_CC, COL_CH, COL_Q, COL_K, COL_V, COL_GA, COL_GB = 0, 1024, 2048, 3072, 4096, 4352, 4608, 5632
SKEW = 384
NBUF = 383
UNITS_A, UNITS_V, UNITS_B, UNITS_C = 10, 2, 24, 32
AHEAD = 4
LISTROWS = 9 * P
OVF = 16
NOROW = 4096
C_ID, C_SLT, C_ONE, C_MB, C_HM, C_IO, C_TOK, C_I16, C_B128, C_PIX, C_END = (
    0, 128, 256, 257, 265, 281, 313, 331, 347, 355, 356)


def bucket(n):
    if n < NBUCKET // 2:
        return n
    big = 16 + int(np.float32(np.log(np.float32(n) / np.float32(16))) / np.float32(np.log(8.0)) * np.float32(16))
    return min(big, NBUCKET - 1)


def constants():
    c = np.zeros((P, C_END), np.float32)
    p = np.arange(P)
    c[:, C_ID:C_ID + P] = np.eye(P)
    c[:, C_SLT:C_SLT + P] = p[:, None] < p[None, :]
    c[:, C_ONE] = 1
    c[:, C_MB:C_MB + 8] = (p[:, None] // 4) % 8 == np.arange(8)
    c[:, C_HM:C_HM + 16] = (p[:, None] // 32) * 4 + p[:, None] % 4 == np.arange(16)
    c[:, C_IO:C_IO + 32] = np.arange(32)
    for t in range(NT):
        for k in range(2):
            c[:, C_TOK + 2 * t + k] = k * T + P * t + p
    c[:, C_I16:C_I16 + OVF] = np.arange(OVF)
    c[:, C_B128:C_B128 + 8] = P * np.arange(1, 9)
    c[:, C_PIX] = p
    hot = np.zeros((NBUCKET + 1, 512 + 1), np.float32)
    for u in range(NBUF):
        d = 255 - u
        if 0 <= d <= WIN:
            hot[bucket(d), u] = 1 / SCALE
        else:
            hot[NBUCKET, u] = MASKED
    for j in range(129):
        hot[bucket(128 - j), SKEW + j] = 1 / SCALE
    return c, hot


class Steps:

    def __init__(self, engine, sem):
        self.engine, self.sem, self.n = engine, sem, 0

    def after(self, instruction):
        instruction.then_inc(self.sem, 1)
        self.n = self.n + 1
        self.engine.wait_ge(self.sem, self.n)


def program(nc, x_prompt, x_sample, cache_conv, cache_k, cache_v, norm1_g, w_in, conv_w, w_conv_out,
            w_attn_out, w_o, sinks, rel_bias, norm2_g, w_router_group, b_router_group,
            w_router_expert, b_router_expert, w_e_gate, w_e_up, w_e_down, norm_f_g, table, onehot,
            y_prompt, y_sample, conv_state_prompt, k_win_prompt, v_win_prompt,
            conv_state_sample, k_win_sample, v_win_sample):
    a_dram = nc.dram_tensor("a_spill", (P, KT, T), F32).ap()
    skew = nc.dram_tensor("bias_skew", (HEADS, P * SKEW), F32).ap()
    xn_dram = nc.dram_tensor("normed_rows", (T, D), F32).ap()
    y_dram = nc.dram_tensor("expert_rows", (2 * T, D), F32).ap()
    list_dram = nc.dram_tensor("token_lists", (LISTROWS * NE, 1), U32).ap()

    with ExitStack() as ctx:
        base = 16512

        def at(name, offset, shape, dt=F32):
            return nc.alloc_sbuf_tensor_at(name, [P] + shape if shape[0] != "rows" else shape[1:], dt, offset=base + offset)

        def sem(name):
            return ctx.enter_context(nc.semaphore(name))

        W8 = KT * T * 4
        R3, R4, R5, RING, SMALL = 2 * W8, 3 * W8, 3 * W8 + 33856, 4 * W8 + 33856, 4 * W8 + 33856 + 36864
        h_hi = at("h_hi", 0, [KT, T], F32R)
        h_lo = at("h_lo", W8, [KT, T], F32R)
        q_sb = at("q_sb", R3, [KT, T])
        o_lo = at("o_lo", R3, [KT, T], F32R)
        o_hi = at("o_hi", R4, [KT, T], F32R)
        a_raw = at("a_raw", R3, [KT, T])
        a_lo = at("a_lo", R3, [KT, T], F32R)
        a_hi = at("a_hi", R4, [KT, T], F32R)
        x_tok = at("x_tok", R3, [NT, D])
        k_sb = at("k_sb", R4, [2, T])
        v_sb = at("v_sb", R4 + 8256, [NT, 256])
        bias_sb = at("bias_sb", R4 + 8256 + 9216, [HEADS, 256])
        mix = at("mix", R5, [KT, T])
        junk = at("junk", R5, [D])
        bias_row = at("bias_row", R5 + 4096, [HEADS, SKEW])
        q_stage = at("q_stage", R5, [KT, P])
        k_stage = at("k_stage", R5 + 4096, [2, 2 * P])
        probs = at("probs", R5 + 6144, [2, 2, 256])
        probsT_hi = at("probsT_hi", R5 + 10240, [2, 2, 2, P], F32R)
        probsT_lo = at("probsT_lo", R5 + 14336, [2, 2, 2, P], F32R)
        v_hi = at("v_hi", R5 + 26720, [2, 256], F32R)
        v_lo = at("v_lo", R5 + 28768, [2, 256], F32R)
        u_sb = at("u_sb", R5 + 18432, [T + 2])
        y_sb = at("y_sb", R5 + 22592, [T])
        kc = at("kc", R4 + 8256 + 9216, [B8, 256])
        vc = at("vc", R4 + 8256 + 9216 + 8192, [B8, 256])
        S5 = R5 + 4 * 4 * T
        kcT = at("kcT", S5, [B8, 2, P])
        q_of = at("q_of", R4 + 8256 + 9216, [2, B8, 32])
        s_rows = at("s_rows", S5 + 8704, [P])
        pT = at("pT", S5 + 9216, [P])
        k_out = at("k_out", S5 + 9728, [2, 256])
        u_out = at("u_out", S5 + 11776, [D])
        pn8 = at("pn8", S5 + 15872, [8])
        pn8T = at("pn8T", S5 + 15904, [P])

        w_raw = [at(f"w_raw{i}", RING + 4096 * i, [KT, P]) for i in range(3)]
        w_hi = at("w_hi", RING + 12288, [3, KT, P], F32R)
        w_lo = at("w_lo", RING + 24576, [3, KT, P], F32R)
        gate_b = [at(f"gate_b{c}", RING + (8192, 8192 + 4 * CH, 12288 + 8192)[c], [CH]) for c in range(3)]
        cur = [SMALL]

        def small(name, shape, dt=F32):
            n = 4
            for s in shape:
                n *= s
            cur[0] += -cur[0] % 32
            t = at(name, cur[0], shape, dt)
            cur[0] += n
            return t

        tab = small("tab", [C_END])
        cols32 = small("cols32", [32])
        g1 = cols32[:, 0:KT]
        carrier = small("carrier", [1])
        ssq = small("ssq", [NT])
        rms = small("rms", [NT])
        eps = small("eps", [1])
        GATE = cur[0] + -cur[0] % 32
        gate = small("gate", [T])
        SHARED = cur[0]
        sinkb = small("sinkb", [HEADS])
        sinkp, sink8 = small("sinkp", [HEADS]), small("sink8", [HEADS])
        sinkc = small("sinkc", [1])
        relb = small("relb", [HEADS])
        relb_hi, relb_lo = small("relb_hi", [HEADS], F32R), small("relb_lo", [HEADS], F32R)
        bs8 = small("bs8", [129])
        histT = small("histT", [KT, 2, B8])
        ustate = small("ustate", [KT, 10])
        maxs = small("maxs", [HEADS])
        negm = small("negm", [HEADS])
        sinkd = small("sinkd", [HEADS])
        den = small("den", [HEADS])
        esink = small("esink", [HEADS])
        rden = small("rden", [HEADS])
        sc = small("sc", [16])
        tmp8 = small("tmp8", [KT, B8])
        relc = at("relc", R5 + 32000, [P])
        hot = at("hot", R5 + 28672, [513])
        hist_rows = at("hist_rows", R4 + 8256, [D])
        rows32 = at("rows32", R4 + 12352, [P])
        hot_r = at("hot_r", R4 + 12864, [SKEW], F32R)
        q_new = small("q_new", [2, 32])
        wo_raw = at("wo_raw", 0, [KT, D])
        wo_lo = at("wo_lo", 0, [KT, D], F32R)
        wo_hi = at("wo_hi", W8, [KT, D], F32R)
        mix_hi = at("mix_hi", R3, [2, KT, P], F32R)
        mix_lo = at("mix_lo", R3 + 8192, [2, KT, P], F32R)
        x2 = at("x2", R3 + 16384, [NT, D])
        x_in = at("x_in", R3 + 53248, [2, D])
        h2T = at("h2T", R3 + 61440, [KT, P])
        xn = at("xn", RING + 32768, [D])
        g2b = at("g2b", GATE, [D])
        list_init = at("list_init", GATE, [LISTROWS * NE // P], U32)
        wr = at("wr", R3 + 65536, [KT, 36])
        cur[0] = SHARED
        rb = small("rb", [36])
        lg = small("lg", [40])
        top_g = small("top_g", [8])
        idx_g = small("idx_g", [8], U32)
        grp = small("grp", [2])
        oh4 = small("oh4", [4])
        prod = small("prod", [8, 4])
        e8 = small("e8", [8])
        top_e = small("top_e", [8])
        idx_e = small("idx_e", [8], U32)
        idx_f = small("idx_f", [2])
        picked = small("picked", [2, 2])
        hots = small("hots", [2, 2, NE])
        picks = small("picks", [2, NE])
        seen = small("seen", [NE])
        rank2 = small("rank2", [2])
        adr_f = small("adr_f", [2])
        adr = small("adr", [2 * NT], U32)
        tok_u = small("tok_u", [2 * NT], U32)
        gl = small("gl", [NT, 4])
        tv = small("tv", [NT, 2])
        wts = small("wts", [NT, 2])
        wsum = small("wsum", [NT])
        cnt = small("cnt", [4])
        ov_a = small("ov_a", [3, OVF])
        ov_b = small("ov_b", [2 * OVF + 1])
        ov_t = small("ov_t", [2 * OVF + 1], U32)
        lst = small("lst", [NE], U32)
        lst_f = small("lst_f", [NE])
        lst_g = small("lst_g", [NE])
        gidx = small("gidx", [NE], U32)
        gcol = small("gcol", [2], U32)
        idle_in, idle_out = small("idle_in", [1]), small("idle_out", [2])
        scol = small("scol", [1], U32)
        e_raw = [at(f"e_raw{i}", RING + 8192 * i if i < 4 else 8192 * (i - 4), [2048]) for i in range(12)]
        e_lo = [at(f"e_lo{i}", RING + 8192 * i if i < 4 else 8192 * (i - 4), [2048], F32R) for i in range(12)]
        e_hi = at("e_hi", R5, [4, 2048], F32R)
        xT_hi = at("xT_hi", R3, [2, KT, P], F32R)
        xT_lo = at("xT_lo", R3 + 8192, [2, KT, P], F32R)
        xg = at("xg", R3 + 53248, [2, D])
        sg = at("sg", R3 + 61440, [FE])
        act_sb = at("act_sb", R3 + 63488, [FE])
        aT_hi = at("aT_hi", RING + 32768, [4, P], F32R)
        aT_lo = at("aT_lo", RING + 34816, [4, P], F32R)
        y_out = at("y_out", GATE, [D])
        v_gate = at("v_gate", 0, [KT, FE])
        v_up = at("v_up", 16384, [KT, FE])
        v_down = at("v_down", 32768, [4, D])
        v_xT = at("v_xT", R3, [KT, P])
        v_aT = at("v_aT", R3 + 4096, [4, P])
        f_y = [at(f"f_y{k}", 36864 * k, [NT, D]) for k in range(2)]
        f_out = at("f_out", R5, [NT, D])
        gfb = at("gfb", RING + 8192, [D])
        f_junk = at("f_junk", RING + 12288, [D])
        assert base + cur[0] <= 229344, cur[0]

        bank = [ctx.enter_context(nc.psum_tensor(f"bank{i}", [P, 512], F32)) for i in range(8)]
        DN, SCB, PTB, OB = bank[0:3], bank[3:5], bank[5], bank[6:8]
        KCB = [bank[3], bank[4], bank[5], bank[7]]
        gates2 = [[gate[:, CH * c:CH * c + CH] for c in range(3)], [gate_b[c][:, :] for c in range(3)]]
        ident = tab[:, C_ID:C_ID + P]

        relb_ones = sem("relb_ones")
        consts_loaded = sem("consts_loaded")
        tab_loaded, cols_loaded, relb_split = sem("tab_loaded"), sem("cols_loaded"), sem("relb_split")
        x_loaded = [sem(f"x_loaded{g}") for g in range(5)]
        sqrt_done, x_scaled = sem("sqrt_done"), sem("x_scaled")
        xT_ready, h_hi_done, h_lo_done = sem("xT_ready"), sem("h_hi_done"), sem("h_lo_done")
        bias_psum, bias_row_done, skew_written, bias_loaded = sem("bias_psum"), sem("bias_row_done"), sem("skew_written"), sem("bias_loaded")
        start_psum, start_copied = sem("start_psum"), sem("start_copied")
        raw_loaded = [sem(f"raw_loaded{i}") for i in range(3)]
        ao_loaded = [sem(f"ao_loaded{i}") for i in range(2)]
        hi_ready, lo_ready = sem("hi_ready"), sem("lo_ready")
        chunk_done, chunk_out, gate_out = sem("chunk_done"), sem("chunk_out"), sem("gate_out")
        staged, scores_ready, max_ready, probs_ready = sem("staged"), sem("scores_ready"), sem("max_ready"), sem("probs_ready")
        probs_turned, probsT_hi_done, probsT_lo_done, pv_done = sem("probs_turned"), sem("probsT_hi_done"), sem("probsT_lo_done"), sem("pv_done")
        sums_inverted, probs_normed, v_hi_done, v_lo_done, o_stored = (sem("sums_inverted"), sem("probs_normed"), sem("v_hi_done"),
                                                                       sem("v_lo_done"), sem("o_stored"))
        a_spilled = sem("a_spilled")
        dve_step, act_step = sem("dve_step"), sem("act_step")
        cache_loaded, states_out, v_out = sem("cache_loaded"), sem("states_out"), sem("v_out")
        kcT_psum, kcT_copied, q_of_done = sem("kcT_psum"), sem("kcT_copied"), sem("q_of_done")
        s_psum, s_max, s_exp, s_normed = sem("s_psum"), sem("s_max"), sem("s_exp"), sem("s_normed")
        pT_psum, pT_copied, so_psum, so_stored = sem("pT_psum"), sem("pT_copied"), sem("so_psum"), sem("so_stored")
        win_psum, win_copied, q_new_done = sem("win_psum"), sem("win_copied"), sem("q_new_done")
        o_hi_done, o_lo_done, a_loaded, a_hi_done, a_lo_done = sem("o_hi_done"), sem("o_lo_done"), [sem(f"a_loaded{x}") for x in range(2)], sem("a_hi_done"), sem("a_lo_done")

        wo_loaded = [sem(f"wo_loaded{i}") for i in range(4)]
        wo_hi_done, wo_lo_done = sem("wo_hi_done"), sem("wo_lo_done")
        router_loaded, list_filled, list_blank = sem("router_loaded"), sem("list_filled"), sem("list_blank")
        x_again = [sem(f"x_again{i}") for i in range(2)]
        mix_hi_done, mix_lo_done, proj_done, x2_done = sem("mix_hi_done"), sem("mix_lo_done"), sem("proj_done"), sem("x2_done")
        sq2_done, root2_done, xn_done, xn_written = sem("sq2_done"), sem("root2_done"), sem("xn_done"), sem("xn_written")
        xnT_psum, h2T_done, logits_done, picks_done = sem("xnT_psum"), sem("h2T_done"), sem("logits_done"), sem("picks_done")
        rank_done, seen_done, adr_done, listed = sem("rank_done"), sem("seen_done"), sem("adr_done"), sem("listed")
        ov_psum, ov_sbuf, list_loaded, gidx_done = sem("ov_psum"), sem("ov_sbuf"), sem("list_loaded"), sem("gidx_done")
        wexp_done, wsum_done = sem("wexp_done"), sem("wsum_done")
        e_loaded = [sem(f"e_loaded{i}") for i in range(12)]
        e_hi_done, e_lo_done, e_used = sem("e_hi_done"), sem("e_lo_done"), sem("e_used")
        silu_done, act_done = sem("silu_done"), sem("act_done")
        aT_psum, aT_hi_done, aT_lo_done = sem("aT_psum"), sem("aT_hi_done"), sem("aT_lo_done")
        xT_psum, xT_hi_done, xT_lo_done = sem("xT_psum"), sem("xT_hi_done"), sem("xT_lo_done")
        final_step, y_stored, col_done, scattered = sem("final_step"), sem("y_stored"), sem("col_done"), sem("scattered")
        idle_ready, idled, v_free = sem("idle_ready"), sem("idled"), sem("v_free")
        gathered = [sem(f"gathered{i}") for i in range(2)]
        v_loaded, v_col, v_idx, v_gathered, v_xpsum, v_xT_done = (sem("v_loaded"), sem("v_col"), sem("v_idx"), sem("v_gathered"),
                                                                  sem("v_xpsum"), sem("v_xT_done"))
        v_gu, v_silu, v_act, v_apsum, v_aT_done, v_ypsum, v_y, v_scattered = (
            sem("v_gu"), sem("v_silu"), sem("v_act"), sem("v_apsum"), sem("v_aT_done"), sem("v_ypsum"), sem("v_y"), sem("v_scattered"))
        rows_written, gf_loaded, f_sum, f_sq, f_root, f_done, f_stored = (
            sem("rows_written"), sem("gf_loaded"), sem("f_sum"), sem("f_sq"), sem("f_root"), sem("f_done"),
            sem("f_stored"))
        f_loaded, F_FROM = e_loaded[0:NT], 16 * 16

        block = ctx.enter_context(nc.Block())

        def e_chunk(s):
            c, e = s
            if c < 4:
                w = (w_e_gate if c < 2 else w_e_up)[0].rearrange("e (k p) f -> e p k f", p=P)
                return w, e, slice(4 * (c % 2), 4 * (c % 2) + 4)
            return w_e_down[0].rearrange("e (k p) f -> e p k f", p=P), e - 1, slice(2 * (c % 2), 2 * (c % 2) + 2)
        w_in_t = w_in[0].rearrange("(k p) f -> p k f", p=P)
        w_ao_h = w_attn_out[0].rearrange("(t h j d) (n f) -> h d t j n f", t=2, h=2, j=4, f=P)
        w_co_t = w_conv_out[0].rearrange("(k p) f -> p k f", p=P)
        N_CONSTS = 4
        U_V, U_B, U_C = UNITS_A, UNITS_A + UNITS_V, UNITS_A + UNITS_V + UNITS_B

        @block.sync
        def _(sp):
            def load(slot, parts):
                for dst, src in parts:
                    sp.dma_start(dst, src).then_inc(raw_loaded[slot], 32 // len(parts))

            def cols(slot, w, col, wait=None):
                if wait is not None:
                    sp.wait_ge(lo_ready, wait)
                w = w.rearrange("p k (n f) -> p k n f", f=P)
                load(slot, [(w_raw[slot][:, 4 * h:4 * h + 4, :], w[:, 4 * h:4 * h + 4, bass.ds(col, 1), :].rearrange("p k n f -> p k (n f)")) for h in range(2)])

            sp.dma_start(tab[:, :], table).then_inc(tab_loaded, 16)
            for g in range(4):
                sp.dma_start(x_tok[:, 2 * g:2 * g + 2, :],
                             x_prompt[0, 256 * g:256 * g + 256, :].rearrange("(t p) d -> p t d", p=P)).then_inc(x_loaded[g], 16)
            sp.dma_start(x_tok[0:B8, 8, :], x_sample[:, 0, :]).then_inc(x_loaded[4], 16)
            def q_unit(t, j, slot, wait):
                col = [COL_Q + t * 512 + j * 64 + 256 * h for h in range(2)]
                col = [x if isinstance(x, int) else sp.snap(x) for x in col]
                if wait is not None:
                    sp.wait_ge(lo_ready, wait)
                load(slot, [(w_raw[slot][:, :, 64 * h:64 * h + 64],
                             w_in_t[:, :, bass.ds(col[h], 64)]) for h in range(2)])

            def a_units(t, first):
                u = t * 5
                for j in range(4):
                    q_unit(t, j, j % 3, None if first and j < 3 else u + j - 1)
                cols(1, w_in_t, COL_K // P + t, u + 3)

            a_units(0, True)
            a_units(1, False)
            for v in range(2):
                cols(v, w_in_t, COL_V // P + v, U_V + v - 1)
            with sp.Fori(0, KT) as j:
                for s, col in enumerate((COL_CC, COL_CH, COL_CB)):
                    cols(s, w_in_t, j + col // P, j * 3 + (U_B + s - 1))
            def out_cols(slot, col, wait):
                sp.wait_ge(lo_ready, wait)
                for t, loaded in enumerate((raw_loaded[slot], ao_loaded[slot])):
                    for h in range(2):
                        sp.dma_start(w_raw[slot][64 * h:64 * h + 64, 4 * t:4 * t + 4, :],
                                     w_ao_h[h, :, t, :, bass.ds(col, 1), :].rearrange("d j n f -> d j (n f)")).then_inc(loaded, 16)

            for n in range(AHEAD):
                cols(n % 2, w_in_t, n + COL_GB // P, U_C + n - 1)
            for n in range(AHEAD, 2 * AHEAD):
                out_cols(n % 2, n - AHEAD, U_C + n - 1)
            with sp.Fori(AHEAD, KT) as j:
                cols(0, w_in_t, j + COL_GB // P, j * 2 + (U_C - 1))
                out_cols(1, j, j * 2 + U_C)
            for n in range(2):
                cols(n, w_in_t, COL_GA // P + n, U_C + 15 + n)
            sp.wait_ge(chunk_done, 111 + 48)
            for x in range(2):
                sp.dma_start(a_raw[:, 4 * x:4 * x + 4, :], a_dram[:, 4 * x:4 * x + 4, :]).then_inc(a_loaded[x], 16)
            with sp.Fori(0, KT - 2) as j:
                cols(0, w_co_t, j, j * 2 + (U_C + 17))
                cols(1, w_in_t, j + (COL_GA // P + 2), j * 2 + (U_C + 18))
            for n in range(2):
                cols(n, w_co_t, KT - 2 + n, U_C + 29 + n)
            sp.wait_ge(chunk_done, 111 + 3 * 30)
            wo_t = w_o[0].rearrange("(k p) f -> p k f", p=P)
            for i in range(4):
                sp.dma_start(wo_raw[:, 2 * i:2 * i + 2, :], wo_t[:, 2 * i:2 * i + 2, :]).then_inc(wo_loaded[i], 16)
            sp.wait_ge(chunk_done, 111 + 96)

            def load_x(n, slot, first):
                if not first:
                    sp.wait_ge(sq2_done, n - 1)
                sp.dma_start(x_in[:, slot, :], x_prompt[0, bass.ds(n * P, P), :]).then_inc(x_again[slot], 16)

            def load_chunk(slot, c, e, wait):
                if wait is not None:
                    sp.wait_ge(e_used, wait)
                w, ex, ks = e_chunk((c, e))
                n = ks.stop - ks.start
                sp.dma_start(e_raw[slot][:, :].rearrange("p (k f) -> p k f", k=n),
                             w[bass.ds(ex, 1), :, ks, :].rearrange("e p k f -> p (e k) f")).then_inc(e_loaded[slot], 16)

            load_x(0, 0, True)
            load_x(1, 1, True)
            sp.wait_ge(chunk_out, 159)
            sp.wait_ge(router_loaded, 80)
            for s in range(4):
                load_chunk(s, s, 0, None)
            with sp.Fori(1, 4) as i:
                for b in range(2):
                    load_x(i * 2 + b, b, False)
            sp.wait_ge(sq2_done, 7)
            sp.dma_start(x_in[0:B8, 0, :], x_sample[:, 0, :]).then_inc(x_again[0], 16)
            sp.wait_ge(proj_done, NT)
            for s in range(4, 12):
                if s == 9:
                    for par in range(2):
                        sp.wait_ge(gathered[par], 16)
                load_chunk(s, (s - 4) % 6, 1 + (s - 4) // 6, None)

            def load_round(i, final):
                for c in range(12):
                    s = 8 + c
                    cc, de = s % 6, s // 6
                    if final and c >= 10:
                        cc, de = cc + 4, de
                    load_chunk(c, cc, i * 2 + (1 + de), i * 12 + (1 + c))

            with sp.Fori(0, 14) as i:
                load_round(i, False)
            load_round(14, True)

            sp.wait_ge(e_used, 192)
            sp.dma_start(gfb[:, :], norm_f_g.partition_broadcast(P)).then_inc(gf_loaded, 16)
            sp.wait_ge(ov_sbuf, 3)
            n_ov = sp.value_load(ov_t[0:1, 2 * OVF:2 * OVF + 1], min_val=0, max_val=OVF)
            with sp.If(n_ov > 0):
                with sp.Fori(0, OVF) as i:
                    with sp.If(i < n_ov):
                        ex = sp.value_load(ov_t[0:1, bass.ds(i, 1)], min_val=0, max_val=NE - 1)
                        sp.wait_ge(v_free, i + 1)
                        for dst, w in ((v_gate, w_e_gate), (v_up, w_e_up), (v_down, w_e_down)):
                            sp.dma_start(dst[:, :, :], w[0][bass.ds(ex, 1)].rearrange("e (k p) f -> p (e k) f", p=P)).then_inc(v_loaded, 16)

            sp.wait_ge(rows_written, 1)
            for n in range(NT):
                rows = P if n < 8 else B8
                for k in range(2):
                    sp.dma_start(f_y[k][0:rows, n, :], y_dram[n * P + k * T:n * P + k * T + rows, :]).then_inc(f_loaded[n], 16)
            with sp.Fori(0, 8) as n:
                sp.wait_ge(f_done, n + 1)
                sp.dma_start(y_prompt[0, bass.ds(n * P, P), :], f_out[:, bass.ds(n, 1), :].rearrange("p a d -> p (a d)")).then_inc(f_stored, 16)
            sp.wait_ge(f_done, 9)
            sp.dma_start(y_sample[:, 0, :], f_out[0:B8, 8, :]).then_inc(f_stored, 16)
            sp.wait_ge(f_stored, 16 * NT)
            sp.wait_ge(states_out, 16 * 7)

        @block.gpsimd
        def _(pool):
            pool.dma_start(rows32[0:8, :], norm1_g[0].rearrange("(k p) -> k p", p=P)).then_inc(cols_loaded, 16)
            pool.dma_start(rows32[8:32, :], conv_w[0].rearrange("j (k p) -> (j k) p", p=P)).then_inc(cols_loaded, 16)
            pool.dma_start(hot[0:33, :], onehot).then_inc(consts_loaded, 16)
            pool.dma_start(sinkb[:, :], sinks[0].partition_broadcast(P)).then_inc(consts_loaded, 16)
            pool.dma_start(hist_rows[0:16, :], cache_conv[0].rearrange("b r d -> (b r) d")).then_inc(consts_loaded, 16)
            pool.wait_ge(relb_ones, 1)
            pool.dma_start(relb[0:32, :], rel_bias).then_inc(consts_loaded, 16)
            pool.wait_ge(list_filled, 1)
            pool.dma_start(list_dram.rearrange("(p q) o -> p (q o)", p=P), list_init[:, :]).then_inc(list_blank, 16)
            for h in range(HEADS):
                pool.wait_ge(bias_row_done, h + 1)
                pool.dma_start(skew[h].rearrange("(p q) -> p q", q=SKEW), bias_row[:, h, :]).then_inc(skew_written, 16)
            pool.wait_ge(skew_written, 16 * HEADS)
            pool.dma_start(bias_sb[:, :, :], skew[:, 127:127 + P * NBUF].rearrange("h (p q) -> p h q", q=NBUF)[:, :, 0:256]).then_inc(bias_loaded, 16)

            def stage(b, first):
                if not first:
                    pool.wait_ge(scores_ready, b * 8)
                if first:
                    pool.tensor_copy(k_stage[:, :, P:2 * P], k_sb[:, :, 0:P]).then_inc(staged, 1)
                else:
                    pool.tensor_copy(k_stage[:, :, :], k_sb[:, :, bass.ds(b * P - P, 2 * P)]).then_inc(staged, 1)
                pool.tensor_copy(q_stage[:, :, :], q_sb[:, :, bass.ds(b * P, P)]).then_inc(staged, 1)

            def spill(j):
                pool.wait_ge(chunk_out, j * 9 + 48)
                pool.dma_start(a_dram[:, bass.ds(j, 1), :], y_sb[:, :].unsqueeze(1)).then_inc(a_spilled, 16)

            pool.wait_ge(chunk_out, 3 * UNITS_A)
            pool.wait_ge(bias_loaded, 16)
            stage(0, True)
            flat = lambda x: x.rearrange("b s g d -> b s (g d)")
            pool.dma_start(flat(k_win_sample[0])[:, 0:WIN - 1, :], flat(cache_k[0])[:, 1:WIN, :]).then_inc(states_out, 16)
            pool.dma_start(flat(v_win_sample[0])[:, 0:WIN - 1, :], flat(cache_v[0])[:, 1:WIN, :]).then_inc(states_out, 16)
            pool.dma_start(conv_state_sample[0, :, 0, :], cache_conv[0, :, 1, :]).then_inc(states_out, 16)
            pool.wait_ge(chunk_out, 39)
            pool.dma_start(flat(v_win_prompt[0])[0], v_sb[:, 7, :]).then_inc(v_out, 16)
            pool.dma_start(flat(v_win_sample[0])[:, WIN - 1, :], v_sb[0:B8, 8, :]).then_inc(v_out, 16)
            with pool.Fori(0, KT - 1) as j:
                stage(j + 1, False)
                spill(j)
            pool.wait_ge(max_ready, 64)
            pool.dma_start(kc[:, :, :], cache_k[0].rearrange("b s g d -> s b (g d)")).then_inc(cache_loaded, 16)
            pool.dma_start(vc[:, :, :], cache_v[0].rearrange("b s g d -> s b (g d)")).then_inc(cache_loaded, 16)
            spill(KT - 1)
            pool.wait_ge(win_copied, 4)
            pool.dma_start(flat(k_win_prompt[0])[0], k_out[:, 0, :]).then_inc(states_out, 16)
            pool.dma_start(flat(k_win_sample[0])[:, WIN - 1, :], k_out[0:B8, 1, :]).then_inc(states_out, 16)
            pool.dma_start(conv_state_prompt[0, 0], u_out[0:2, :]).then_inc(states_out, 16)
            pool.dma_start(conv_state_sample[0, :, 1, :], u_out[2:10, :]).then_inc(states_out, 16)
            pool.wait_ge(states_out, 16 * 7)
            pool.wait_ge(v_out, 32)
            pool.wait_ge(chunk_out, 159)
            pool.dma_start(g2b[:, :], norm2_g[0].partition_broadcast(P)).then_inc(router_loaded, 16)
            pool.dma_start(wr[:, :, 0:NG], w_router_group[0].rearrange("(k p) g -> p k g", p=P)).then_inc(router_loaded, 16)
            pool.dma_start(wr[:, :, NG:NG + NE], w_router_expert[0].rearrange("(k p) g -> p k g", p=P)).then_inc(router_loaded, 16)
            pool.dma_start(rb[:, 0:NG], b_router_group[0].partition_broadcast(P)).then_inc(router_loaded, 16)
            pool.dma_start(rb[:, NG:NG + NE], b_router_expert[0].partition_broadcast(P)).then_inc(router_loaded, 16)
            pool.wait_ge(list_blank, 16)

            def write_xn(n, rows):
                pool.wait_ge(xn_done, n + 1)
                pool.dma_start(xn_dram[P * n:P * n + rows, :], xn[0:rows, :]).then_inc(xn_written, 16)

            def enter_lists(n, rows):
                pool.wait_ge(adr_done, n + 1)
                for k in range(2):
                    pool.indirect_dma_start(out=list_dram, out_offset=bass.IndirectOffsetOnAxis(ap=adr[0:rows, 2 * n + k:2 * n + k + 1], axis=0),
                                            in_=tok_u[0:rows, 2 * n + k:2 * n + k + 1], in_offset=None,
                                            bounds_check=LISTROWS * NE - 1, oob_is_err=False).then_inc(listed, 16)

            for n in range(NT + 2):
                if n == NT:
                    pool.wait_ge(sq2_done, NT)
                    pool.memset(xg[:, :, :], 0.0).then_inc(idle_ready, 1)
                if n >= 2:
                    enter_lists(n - 2, P if n < 10 else B8)
                if n < NT:
                    write_xn(n, P if n < 8 else B8)
            pool.wait_ge(listed, 32 * NT)
            pool.wait_ge(xn_written, 16 * NT)
            pool.dma_start(lst[:, :], list_dram[0:P * NE, :].rearrange("(r e) o -> r (e o)", e=NE)).then_inc(list_loaded, 16)
            pool.wait_ge(gidx_done, 1)

            pool.memset(idle_in[:, :], 0.0).then_inc(idle_ready, 1)
            pool.wait_ge(idle_ready, 2)

            def gather(e, par, first):
                if not first:
                    pool.wait_ge(xT_psum, e - 1)
                pool.tensor_copy(gcol[:, par:par + 1], gidx[:, bass.ds(e, 1)]).then_inc(col_done, 1)
                return par

            def carry(k=0):
                return pool.tensor_tensor(idle_out[:, k:k + 1], idle_in[:, :], idle_in[:, :], ALU.add)

            def gather_rows(par):
                pool.indirect_dma_start(out=xg[:, par, :], out_offset=None, in_=xn_dram,
                                        in_offset=bass.IndirectOffsetOnAxis(ap=gcol[:, par:par + 1], axis=0),
                                        bounds_check=T - 1, oob_is_err=False).then_inc(gathered[par], 16)

            def scatter_rows():
                pool.indirect_dma_start(out=y_dram, out_offset=bass.IndirectOffsetOnAxis(ap=scol[:, 0:1], axis=0),
                                        in_=y_out[:, :], in_offset=None, bounds_check=2 * T - 1, oob_is_err=False).then_inc(scattered, 16)

            for e in range(2):
                gather(e, e, True)
                pool.wait_ge(col_done, e + 1)
                gather_rows(e)

            def step_e(e, par, more):
                if more:
                    gather(e + 2, par, False)
                    pool.wait_ge(col_done, e * 2 + 3)
                    carry()
                    gather_rows(par)
                    pool.wait_ge(y_stored, e + 1)
                    pool.tensor_copy(scol[:, 0:1], lst[:, bass.ds(e, 1)]).then_inc(col_done, 1)
                    pool.wait_ge(col_done, e * 2 + 4)
                    carry()
                else:
                    pool.wait_ge(y_stored, e + 1)
                    pool.tensor_copy(scol[:, 0:1], lst[:, bass.ds(e, 1)]).then_inc(col_done, 1)
                    pool.wait_ge(col_done, e + 33)
                scatter_rows()

            with pool.Fori(0, 15) as i:
                for b in range(2):
                    step_e(i * 2 + b, b, True)
            step_e(30, 0, False)
            step_e(31, 1, False)
            pool.wait_ge(scattered, 16 * NE)

            pool.wait_ge(ov_sbuf, 3)
            pool.sem_inc(v_free, 1)
            n_ov = pool.value_load(ov_t[0:1, 2 * OVF:2 * OVF + 1], min_val=0, max_val=OVF)
            with pool.If(n_ov > 0):
                with pool.Fori(0, OVF) as i:
                    with pool.If(i < n_ov):
                        ex = pool.value_load(ov_t[0:1, bass.ds(i, 1)], min_val=0, max_val=NE - 1)
                        bk = pool.value_load(ov_t[0:1, bass.ds(i + OVF, 1)], min_val=1, max_val=8)
                        pool.dma_start(scol[:, 0:1], list_dram[bass.ds(bk * (P * NE), P * NE), :].rearrange("(r e) o -> r (e o)", e=NE)[:, bass.ds(ex, 1)],
                                       allow_slow_non_contiguous=True).then_inc(v_col, 16)
                        pool.wait_ge(v_idx, i + 1)
                        carry().then_inc(idled, 1)
                        pool.indirect_dma_start(out=xg[:, 0, :], out_offset=None, in_=xn_dram,
                                                in_offset=bass.IndirectOffsetOnAxis(ap=gcol[:, 0:1], axis=0),
                                                bounds_check=T - 1, oob_is_err=False).then_inc(v_gathered, 16)
                        pool.wait_ge(v_y, i + 1)
                        carry(1).then_inc(idled, 1)
                        pool.indirect_dma_start(out=y_dram, out_offset=bass.IndirectOffsetOnAxis(ap=scol[:, 0:1], axis=0),
                                                in_=y_out[:, :], in_offset=None, bounds_check=2 * T - 1, oob_is_err=False).then_inc(v_scattered, 16)
                        pool.wait_ge(idled, i * 2 + 2)
                        pool.wait_ge(v_scattered, i * 16 + 16)
                        pool.sem_inc(v_free, 1)
            pool.drain().then_inc(rows_written, 1)

        @block.tensor
        def _(pe):
            def split_product(out, pairs, ready=None):
                for i, ((xh, xl), (wh, wl)) in enumerate(pairs):
                    if ready is not None:
                        pe.wait_ge(ready, i + 1)
                    pe.matmul(out, wh, xh, start=i == 0, stop=False)
                    pe.matmul(out, wh, xl, start=False, stop=False)
                    mm = pe.matmul(out, wl, xh, start=False, stop=i == len(pairs) - 1)
                return mm

            def unit_chunk(slot, xh, xl, c, ready=None):
                cols = slice(CH * c, CH * c + CH)
                split_product(DN[c][:, 0:CH], [((xh[:, k, cols], xl[:, k, cols]), (w_hi[:, slot, k, :], w_lo[:, slot, k, :]))
                                               for k in range(KT)], ready).then_inc(chunk_done, 1)

            pe.wait_ge(tab_loaded, 16)
            pe.wait_ge(cols_loaded, 32)
            pe.transpose(bank[7][:, 0:32], rows32[0:32, :], ident[0:32, 0:32]).then_inc(start_psum, 1)
            pe.wait_ge(start_copied, 1)
            for g in range(2):
                pe.wait_ge(x_scaled, 4 * g + 4)
                for k in range(KT):
                    if g:
                        pe.wait_ge(h_lo_done, k + 1)
                    for i in range(4):
                        mm = pe.transpose(bank[k][:, P * i:P * i + P], x_tok[:, 4 * g + i, P * k:P * k + P], ident)
                    mm.then_inc(xT_ready, 1)

            def turn_new():
                pe.wait_ge(x_scaled, 9)
                pe.wait_ge(h_lo_done, 12)
                for k in range(KT):
                    mm = pe.transpose(bank[3][:, B8 * k:B8 * k + B8], x_tok[0:B8, 8, P * k:P * k + P], ident[0:B8, 0:B8])
                mm.then_inc(xT_ready, 1)

            pe.wait_ge(h_lo_done, 9)

            def bias_head(h):
                if h >= 4:
                    pe.wait_ge(bias_row_done, h - 3)
                for rb_part in (relb_hi, relb_lo):
                    mm = pe.matmul(bank[3 + h % 4][:, 0:SKEW], rb_part[0:33, h:h + 1].to_broadcast([33, P]), hot_r[0:33, :],
                                   start=rb_part is relb_hi, stop=rb_part is relb_lo)
                mm.then_inc(bias_psum, 1)

            def units_a(t, first):
                for i in range(5):
                    u = t * 5 + i
                    pe.wait_ge(lo_ready, u + 1)
                    for c in range(3):
                        if not (first and i == 0):
                            pe.wait_ge(chunk_out, u * 3 + (c - 2))
                        if first and i == 0 and c:
                            pe.wait_ge(h_lo_done, 15 + c)
                        unit_chunk((0, 1, 2, 0, 1)[i], h_hi, h_lo, c)
                        if first and i == 0 and c == 0:
                            turn_new()
                        if first and (i or c):
                            if i == 0 and c == 1:
                                pe.wait_ge(relb_split, 1)
                            bias_head(3 * i + c - 1)

            units_a(0, True)
            bias_head(14)
            bias_head(15)
            pe.matmul(bank[7][:, 0:129], relc[0:33, :], hot[0:33, SKEW:SKEW + 129], start=True, stop=True)
            for k in range(KT):
                mm = pe.transpose(bank[7][:, 256 + 16 * k:256 + 16 * k + 16], hist_rows[0:16, P * k:P * k + P], ident[0:16, 0:16])
            mm.then_inc(start_psum, 1)
            with pe.Fori(1, 2) as t:
                units_a(t, False)
            pe.wait_ge(lo_ready, U_V + 2)
            for n in range(NT):
                rows = P if n < 8 else B8
                pe.wait_ge(chunk_out, 30 + n - 2)
                out = DN[n % 3][0:rows, 0:256].rearrange("p (a f) -> p a f", a=2)
                for k in range(KT):
                    xh, xl = h_hi[:, k, P * n:P * n + rows], h_lo[:, k, P * n:P * n + rows]
                    pe.matmul(out, xh, w_hi[:, 0:2, k, :], start=k == 0, stop=False)
                    pe.matmul(out, xh, w_lo[:, 0:2, k, :], start=False, stop=False)
                    mm = pe.matmul(out, xl, w_hi[:, 0:2, k, :], start=False, stop=k == KT - 1)
                mm.then_inc(chunk_done, 1)

            def scores(st, b, first):
                t, off = st // 4, P if first else 0
                place = 256 * (st % 2)
                if st == 0:
                    pe.wait_ge(staged, b * 2 + 2)
                if not (first and st == 0):
                    pe.wait_ge(max_ready, b * 8 + st)
                for h in range(2):
                    mm = pe.matmul(SCB[h][:, place + off:place + 256], q_stage[64 * h:64 * h + 64, st, :],
                                   k_stage[64 * h:64 * h + 64, t, off:256], start=True, stop=True)
                mm.then_inc(scores_ready, 1)

            def turn_probs(st, b, first):
                pe.wait_ge(probs_normed, b * 8 + (st + 1))
                if not (first and st == 0):
                    pe.wait_ge(probsT_lo_done, b * 8 + st)
                for h in range(2):
                    for kt in range(1 if first else 0, 2):
                        mm = pe.transpose(PTB[:, P * (2 * h + kt):P * (2 * h + kt) + P],
                                          probs[:, st % 2, h, P * kt:P * kt + P], ident)
                mm.then_inc(probs_turned, 1)

            def values(st, b, first):
                pe.wait_ge(probsT_lo_done, b * 8 + (st + 1))
                if st == 1:
                    pe.wait_ge(v_lo_done, b + 1)
                t, pair = st // 4, st // 2 % 2
                if pair == 0 and not (first and t == 0):
                    pe.wait_ge(o_stored, b * 2 + t)
                for h in range(2):
                    kts = (1,) if first else (0, 1)
                    out = OB[h][:, 256 * pair:256 * pair + 256].rearrange("p (j s) -> p j s", j=2)
                    for kt in kts:
                        vh, vl = v_hi[:, kt, P * t:P * t + P], v_lo[:, kt, P * t:P * t + P]
                        ph, pl = probsT_hi[:, h, kt, :, :], probsT_lo[:, h, kt, :, :]
                        pe.matmul(out, vh, ph, start=kt == kts[0], stop=False)
                        pe.matmul(out, vh, pl, start=False, stop=False)
                        mm = pe.matmul(out, vl, ph, start=False, stop=kt == 1)
                mm.then_inc(pv_done, 1)

            def step_b(j, first, after_first=False):
                for i in range(9):
                    s, c = i // 3, i % 3
                    if i < 8:
                        scores(i, j, first)
                    if c == 0:
                        pe.wait_ge(lo_ready, j * 3 + (U_B + s + 1))
                    pe.wait_ge(chunk_out, j * 9 + (39 + i - 2))
                    cols = slice(CH * c, CH * c + CH)
                    for k in range(KT):
                        if k == 2 and i in (3, 5, 7):
                            values(i - 2, j, first)
                        if k == 5 and i == 0 and not first:
                            values(7, j - 1, after_first)
                        if k == 5 and i > 0:
                            turn_probs(i - 1, j, first)
                        pe.matmul(DN[c][:, 0:CH], w_hi[:, s, k, :], h_hi[:, k, cols], start=k == 0, stop=False)
                        pe.matmul(DN[c][:, 0:CH], w_hi[:, s, k, :], h_lo[:, k, cols], start=False, stop=False)
                        mm = pe.matmul(DN[c][:, 0:CH], w_lo[:, s, k, :], h_hi[:, k, cols], start=False, stop=k == KT - 1)
                    mm.then_inc(chunk_done, 1)

            step_b(0, True)
            step_b(1, False, after_first=True)
            with pe.Fori(2, KT) as j:
                step_b(j, False)
            values(7, KT - 1, False)

            def unit_c(n, slot, xh, xl, gates, projections, between=None, ready=None):
                pe.wait_ge(lo_ready, n + (U_C + 1))
                for c in range(3):
                    if gates is not None:
                        pe.wait_ge(gate_out, gates * 3 + (c - 2))
                    else:
                        pe.wait_ge(chunk_out, projections * 3 + (109 + c))
                    unit_chunk(slot, xh, xl, c, ready if c == 0 else None)
                    if between is not None:
                        between(3 * n + c)

            def caches(c):
                if c == 0:
                    pe.wait_ge(max_ready, 64)
                    for t in range(2):
                        mm = pe.transpose(bank[3][:, P * t:P * t + P], k_sb[:, t, S - P:S], ident)
                    mm.then_inc(win_psum, 1)
                    for t in range(2):
                        mm = pe.transpose(bank[4][0:B8, P * t:P * t + P], k_sb[:, t, S:T], ident)
                    mm.then_inc(win_psum, 1)
                    pe.wait_ge(probsT_lo_done, 64)
                    pe.wait_ge(o_stored, 16)
                    for half in range(2):
                        for k in range(4):
                            mm = pe.transpose(bank[5 + 2 * half][0:10, P * k:P * k + P], ustate[:, 4 * half + k, :], ident)
                        mm.then_inc(win_psum, 1)
                if c == 1:
                    pe.wait_ge(q_new_done, 1)
                    for g in range(KV):
                        half, t = 64 * (g % 2), g // 2
                        mm = pe.matmul(bank[6][32 * g:32 * g + 32, 0:B8], q_new[half:half + 64, t, :], k_sb[half:half + 64, t, S:T], start=True, stop=True)
                    mm.then_inc(s_psum, 1)
                if c == 3:
                    pe.wait_ge(cache_loaded, 32)
                    pe.wait_ge(win_copied, 4)
                    for i in range(4):
                        for b in range(2):
                            for t in range(2):
                                mm = pe.transpose(KCB[i][:, P * (2 * b + t):P * (2 * b + t) + P], kc[:, 2 * i + b, P * t:P * t + P], ident)
                        mm.then_inc(kcT_psum, 1)
                if c == 4:
                    pe.wait_ge(kcT_copied, 4)
                    pe.wait_ge(q_of_done, 1)
                    for g in range(KV):
                        half, t = 64 * (g % 2), g // 2
                        for b in range(B8):
                            mm = pe.matmul(bank[4 - g % 2][32 * g:32 * g + 32, 0:P], q_of[half:half + 64, t, b, :],
                                           kcT[half:half + 64, b, t, :], start=b == 0, stop=b == B8 - 1)
                    mm.then_inc(s_psum, 1)
                if c == 6:
                    pe.wait_ge(s_normed, 1)
                    pe.transpose(bank[7][:, 0:P], s_rows[:, :], ident)
                    pe.transpose(bank[7][0:B8, P:2 * P], pn8[:, :], ident).then_inc(pT_psum, 1)
                if c == 7:
                    pe.wait_ge(pT_copied, 1)
                    for g in range(KV):
                        rows = slice(64 * (g % 2), 64 * (g % 2) + 64)
                        pe.matmul(bank[4][rows, 32 * g:32 * g + 32], v_sb[0:B8, 8, HD * g:HD * g + HD],
                                  pn8T[0:B8, 32 * g:32 * g + 32], start=True, stop=False)
                        for b in range(B8):
                            mm = pe.matmul(bank[4][rows, 32 * g + 4 * b:32 * g + 4 * b + 4], vc[:, b, HD * g:HD * g + HD],
                                           pT[:, 32 * g + 4 * b:32 * g + 4 * b + 4], start=False, stop=b == B8 - 1)
                    mm.then_inc(so_psum, 1)

            for n in range(AHEAD):
                unit_c(n, n % 2, h_hi, h_lo, n if n else None, 0, caches)
            for n in range(AHEAD, 2 * AHEAD):
                unit_c(n, n % 2, o_hi, o_lo, AHEAD if n == AHEAD else None, n - AHEAD, ready=o_lo_done if n == AHEAD else None)
            with pe.Fori(AHEAD, KT) as j:
                unit_c(j * 2, 0, h_hi, h_lo, None, j)
                unit_c(j * 2 + 1, 1, o_hi, o_lo, j + 1, None)
            unit_c(2 * KT, 0, h_hi, h_lo, None, KT)
            unit_c(2 * KT + 1, 1, h_hi, h_lo, KT + 1, None)
            unit_c(2 * KT + 2, 0, a_hi, a_lo, KT + 2, None, ready=a_lo_done)
            unit_c(2 * KT + 3, 1, h_hi, h_lo, None, KT + 1)
            with pe.Fori(1, KT - 2) as j:
                unit_c(j * 2 + (2 * KT + 2), 0, a_hi, a_lo, j + (KT + 2), None)
                unit_c(j * 2 + (2 * KT + 3), 1, h_hi, h_lo, None, j + (KT + 1))
            unit_c(4 * KT - 2, 0, a_hi, a_lo, 2 * KT, None)
            unit_c(4 * KT - 1, 1, a_hi, a_lo, None, 2 * KT - 1)

            def rank(n, par, rows):
                pe.wait_ge(picks_done, n + 1)
                pe.wait_ge(seen_done, n + 1)
                pe.matmul(bank[7][0:rows, 0:NE], tab[0:rows, C_SLT:C_SLT + rows], picks[0:rows, par, :], start=True, stop=False)
                pe.matmul(bank[7][0:rows, 0:NE], tab[:, C_ONE:C_ONE + 1].to_broadcast([P, rows]), seen[:, :],
                          start=False, stop=True).then_inc(rank_done, 1)

            def turn_xn(n, rows):
                pe.wait_ge(xn_done, n + 1)
                for k in range(KT):
                    mm = pe.transpose(bank[4 + k // 4][:, P * (k % 4):P * (k % 4) + rows], xn[0:rows, P * k:P * k + P], ident[0:rows, 0:rows])
                mm.then_inc(xnT_psum, 1)

            def route(n, rows):
                pe.wait_ge(h2T_done, n + 1)
                for k in range(KT):
                    mm = pe.matmul(bank[6][0:rows, 0:36], h2T[:, k, 0:rows], wr[:, k, :], start=k == 0, stop=k == KT - 1)
                mm.then_inc(logits_done, 1)

            def step_d(n, par, rows, before=True, ranked=True):
                pe.wait_ge(mix_lo_done, n + 1)
                for k in range(KT):
                    if not before and k % 2 == 0:
                        pe.wait_ge(wo_lo_done, k // 2 + 1)
                    if k == 6 and ranked:
                        rank(n - 2, par, P)
                    if k == 6 and before:
                        turn_xn(n - 1, P)
                    out = [bank[2 * par + x][0:rows, :] for x in range(2)]
                    half = [slice(0, 512), slice(512, D)]
                    for x in range(2):
                        pe.matmul(out[x], mix_hi[:, par, k, 0:rows], wo_hi[:, k, half[x]], start=k == 0, stop=False)
                    for x in range(2):
                        pe.matmul(out[x], mix_hi[:, par, k, 0:rows], wo_lo[:, k, half[x]], start=False, stop=False)
                    for x in range(2):
                        mm = pe.matmul(out[x], mix_lo[:, par, k, 0:rows], wo_hi[:, k, half[x]], start=False, stop=k == KT - 1)
                mm.then_inc(proj_done, 1)
                if before:
                    route(n - 1, P)

            pe.wait_ge(chunk_out, 159)
            step_d(0, 0, P, False, False)
            pe.wait_ge(router_loaded, 80)
            step_d(1, 1, P, True, False)
            with pe.Fori(1, 4) as i:
                for b in range(2):
                    step_d(i * 2 + b, b, P)
            step_d(8, 0, B8)
            rank(7, 1, P)
            turn_xn(8, B8)
            route(8, B8)
            rank(8, 0, B8)
            pe.wait_ge(seen_done, NT + 1)
            pe.matmul(bank[6][0:NE, 0:1], seen[:, :], tab[:, C_ONE:C_ONE + 1], start=True, stop=True).then_inc(ov_psum, 1)
            pe.wait_ge(ov_sbuf, 1)
            pe.matmul(bank[7][0:NE, 0:1], tab[0:NE, C_SLT:C_SLT + NE], cnt[0:NE, 1:2], start=True, stop=True).then_inc(ov_psum, 1)
            pe.wait_ge(ov_sbuf, 2)
            pe.matmul(bank[6][0:1, 0:2 * OVF + 1], tab[0:NE, C_ONE:C_ONE + 1], ov_b[0:NE, :], start=True, stop=True).then_inc(ov_psum, 1)

            def turn_x(par, e):
                pe.wait_ge(gathered[par], (e - par) * 8 + 16 if isinstance(e, int) else e * 8 + (16 - 8 * par))
                for k in range(KT):
                    mm = pe.transpose(bank[4 + k // 4][:, P * (k % 4):P * (k % 4) + P], xg[:, par, P * k:P * k + P], ident)
                mm.then_inc(xT_psum, 1)

            def chunk_gu(s, slot, c, par, out):
                pe.wait_ge(e_lo_done, s + 1)
                for k in range(4):
                    kk = 4 * (c % 2) + k
                    wh, wl = e_hi[:, slot % 4, 512 * k:512 * k + 512], e_lo[slot][:, 512 * k:512 * k + 512]
                    pe.matmul(out, xT_hi[:, par, kk, :], wh, start=kk == 0, stop=False)
                    pe.matmul(out, xT_hi[:, par, kk, :], wl, start=False, stop=False)
                    mm = pe.matmul(out, xT_lo[:, par, kk, :], wh, start=False, stop=kk == KT - 1)
                mm.then_inc(e_used, 1)

            def chunk_d(s, slot, c):
                pe.wait_ge(e_lo_done, s + 1)
                for k in range(2):
                    kk = 2 * (c % 2) + k
                    w_h, w_l = e_hi[:, slot % 4, :], e_lo[slot][:, :]
                    for a, w, st in ((aT_hi, w_h, kk == 0), (aT_hi, w_l, False), (aT_lo, w_h, False)):
                        for x in range(2):
                            mm = pe.matmul(bank[2 + x][:, :], a[:, kk, :], w[:, 1024 * k + 512 * x:1024 * k + 512 * x + 512],
                                           start=st, stop=kk == 3 and a is aT_lo)
                mm.then_inc(e_used, 1)

            def turn_act(e):
                pe.wait_ge(act_done, e + 1)
                if not isinstance(e, int) or e > 0:
                    pe.wait_ge(aT_lo_done, e)
                for k in range(4):
                    mm = pe.transpose(bank[6][:, P * k:P * k + P], act_sb[:, P * k:P * k + P], ident)
                mm.then_inc(aT_psum, 1)

            def step_e(e, par, s, slot, down, more):
                pe.wait_ge(xT_lo_done, e + 1)
                if down:
                    pe.wait_ge(silu_done, e)
                chunk_gu(s, slot, 0, par, bank[0][:, :])
                chunk_gu(s + 1, (slot + 1) % 12, 1, par, bank[0][:, :])
                if down:
                    turn_act(e - 1)
                chunk_gu(s + 2, (slot + 2) % 12, 2, par, bank[1][:, :])
                chunk_gu(s + 3, (slot + 3) % 12, 3, par, bank[1][:, :])
                if more:
                    turn_x(1 - par, e + 1)
                if down:
                    down_e(e - 1, s + 4, (slot + 4) % 12)

            def down_e(e, s, slot):
                pe.wait_ge(aT_lo_done, e + 1)
                if not isinstance(e, int) or e > 0:
                    pe.wait_ge(y_stored, e)
                chunk_d(s, slot, 0)
                chunk_d(s + 1, slot + 1, 1)

            turn_x(0, 0)
            step_e(0, 0, 0, 0, False, True)
            step_e(1, 1, 4, 4, True, True)
            with pe.Fori(1, 15) as i:
                for b in range(2):
                    step_e(i * 2 + b, b, i * 12 + (6 * b - 2), (6 * b - 2) % 12, True, True)
            step_e(30, 0, 178, 10, True, True)
            step_e(31, 1, 184, 4, True, False)
            turn_act(31)
            down_e(31, 190, 10)

            n_ov = pe.value_load(ov_t[0:1, 2 * OVF:2 * OVF + 1], min_val=0, max_val=OVF)
            with pe.If(n_ov > 0):
                with pe.Fori(0, OVF) as i:
                    with pe.If(i < n_ov):
                        pe.wait_ge(v_gathered, i * 16 + 16)
                        for k in range(KT):
                            mm = pe.transpose(bank[4 + k // 4][:, P * (k % 4):P * (k % 4) + P], xg[:, 0, P * k:P * k + P], ident)
                        mm.then_inc(v_xpsum, 1)
                        pe.wait_ge(v_xT_done, i + 1)
                        pe.wait_ge(v_loaded, i * 48 + 48)
                        for x, w in enumerate((v_gate, v_up)):
                            for k in range(KT):
                                mm = pe.matmul(bank[x][:, :], v_xT[:, k, :], w[:, k, :], start=k == 0, stop=k == KT - 1)
                        mm.then_inc(v_gu, 1)
                        pe.wait_ge(v_act, i + 1)
                        for k in range(4):
                            mm = pe.transpose(bank[6][:, P * k:P * k + P], act_sb[:, P * k:P * k + P], ident)
                        mm.then_inc(v_apsum, 1)
                        pe.wait_ge(v_aT_done, i + 1)
                        for k in range(4):
                            for x in range(2):
                                mm = pe.matmul(bank[2 + x][:, :], v_aT[:, k, :], v_down[:, k, 512 * x:512 * x + 512], start=k == 0, stop=k == 3)
                        mm.then_inc(v_ypsum, 1)

        @block.scalar
        def _(act):
            A = nc.scalar
            step = Steps(act, act_step)

            def split_hi(u, slot, uses, freed):
                act.wait_ge(raw_loaded[slot], uses * 32)
                if freed is not None:
                    act.wait_ge(chunk_done, freed)
                A.activation(w_hi[:, slot, :, :], w_raw[slot][:, :, :], ACT.Copy).then_inc(hi_ready, 1)

            act.wait_ge(relb_ones, 1)
            for g in range(3):
                for n in range(4 * g, min(4 * g + 4, NT)):
                    rows = P if n < 8 else B8
                    act.wait_ge(x_loaded[n // 2], 16)
                    step.after(A.activation(junk[0:rows, :], x_tok[0:rows, n, :], ACT.Square, accum_out=ssq[0:rows, n:n + 1]))
                rows, w = (P, 4) if g < 2 else (B8, 1)
                A.activation(rms[0:rows, 4 * g:4 * g + w], ssq[0:rows, 4 * g:4 * g + w], ACT.Sqrt, bias=eps[0:rows, 0:1],
                             scale=1.0 / D).then_inc(sqrt_done, 1)
            act.wait_ge(start_copied, 1)
            for g in range(2):
                for k in range(KT):
                    act.wait_ge(xT_ready, KT * g + k + 1)
                    A.activation(h_hi[:, k, 512 * g:512 * g + 512], bank[k][:, :], ACT.Copy, scale=g1[:, k:k + 1]).then_inc(h_hi_done, 1)
                if g == 0:
                    split_hi(0, 0, 1, None)

            def splits_a(t):
                split_hi(t * 5 + 1, 1, t * 2 + 1, None if isinstance(t, int) and t == 0 else t * 15)
                split_hi(t * 5 + 2, 2, t + 1, t * 15 + 3)
                split_hi(t * 5 + 3, 0, t * 2 + 2, t * 15 + 6)
                split_hi(t * 5 + 4, 1, t * 2 + 2, t * 15 + 9)
                split_hi(t * 5 + 5, 0, t * 2 + 3, t * 15 + 12)

            splits_a(0)
            with act.Fori(1, 2) as t:
                splits_a(t)
            split_hi(U_V + 1, 1, 5, 30)
            split_hi(U_B, 0, 6, 39)

            def store_o(t, b):
                act.wait_ge(pv_done, b * 4 + (2 * t + 2))
                for h in range(2):
                    rows = slice(64 * h, 64 * h + 64)
                    ins = A.activation(q_sb[rows, 4 * t:4 * t + 4, bass.ds(b * P, P)], OB[h][rows, :].rearrange("p (k t) -> p k t", k=4), ACT.Copy)
                ins.then_inc(o_stored, 1)

            def step_b(j, first):
                off = P if first else 0
                for i in range(9):
                    if i == 1:
                        if not first:
                            act.wait_ge(pv_done, j * 4)
                            store_o(1, j - 1)
                            A.activation(v_hi[:, :, :], v_sb[:, bass.ds(j - 1, 2), :], ACT.Copy).then_inc(v_hi_done, 1)
                        else:
                            A.activation(v_hi[:, 1, :], v_sb[:, 0, :], ACT.Copy).then_inc(v_hi_done, 1)
                    if i < 8:
                        act.wait_ge(max_ready, j * 8 + (i + 1))
                        for h in range(2):
                            n = 2 * i + h
                            pr = probs[:, i % 2, h, off:256]
                            A.activation(pr, pr, ACT.Exp, bias=negm[:, n:n + 1], scale=SCALE, accum_out=den[:, n:n + 1])
                        A.activation(esink[:, 2 * i:2 * i + 2], sinkd[:, 2 * i:2 * i + 2], ACT.Exp).then_inc(probs_ready, 1)
                    if i > 0:
                        st = i - 1
                        act.wait_ge(probs_turned, j * 8 + (st + 1))
                        if st % 2 == 0 and not (first and st == 0):
                            act.wait_ge(pv_done, j * 4 + st // 2)
                        turned = PTB[:, :].rearrange("p (h k t) -> p h k t", h=2, k=2)
                        kts = slice(1 if first else 0, 2)
                        A.activation(probsT_hi[:, :, kts, st % 2, :], turned[:, :, kts, :], ACT.Copy).then_inc(probsT_hi_done, 1)
                    if i == 6:
                        store_o(0, j)
                    if i < 8:
                        act.wait_ge(sums_inverted, j * 8 + (i + 1))
                        for h in range(2):
                            pr = probs[:, i % 2, h, off:256]
                            ins = A.activation(pr, pr, ACT.Copy, scale=rden[:, 2 * i + h:2 * i + h + 1])
                        ins.then_inc(probs_normed, 1)
                    if i == 0:
                        split_hi(j * 3 + (U_B + 1), 1, j + 6, j * 9 + 39)
                    if i == 3:
                        split_hi(j * 3 + (U_B + 2), 2, j + 3, j * 9 + 42)
                    if i == 6:
                        split_hi(j * 3 + (U_B + 3), 0, j + 7, j * 9 + 45)

            act.wait_ge(skew_written, 16 * HEADS)
            step_b(0, True)
            with act.Fori(1, KT) as j:
                step_b(j, False)
            store_o(1, KT - 1)

            def gate_chunk(c, n, dst):
                act.wait_ge(chunk_done, n * 3 + (111 + c + 1))
                A.activation(dst, DN[c][:, 0:CH], ACT.Sigmoid).then_inc(gate_out, 1)

            def mix_of(j):
                return mix[:, bass.ds(j, 1), :].rearrange("p a t -> p (a t)")

            for n in range(AHEAD):
                if AHEAD <= n + 1 < 2 * AHEAD:
                    act.wait_ge(ao_loaded[(n + 1) % 2], 32 * ((n + 1 - AHEAD) // 2 + 1))
                split_hi(U_C + n + 1, (n + 1) % 2, (n + 1) // 2 + 14, 3 * n + 111)
                for c in range(3):
                    gate_chunk(c, n, mix_of(n)[:, CH * c:CH * c + CH])
                    if 3 * n + c == 3:
                        for i in range(4):
                            act.wait_ge(kcT_psum, i + 1)
                            A.activation(kcT[:, 2 * i:2 * i + 2, :, :], KCB[i][:, :].rearrange("p (b t s) -> p b t s", b=2, t=2), ACT.Copy).then_inc(kcT_copied, 1)
                    if 3 * n + c == 4:
                        act.wait_ge(s_max, 1)
                        A.activation(s_rows[:, :], s_rows[:, :], ACT.Exp, bias=sc[:, 1:2], scale=SCALE, accum_out=sc[:, 2:3])
                        A.activation(sc[:, 3:4], sc[:, 0:1], ACT.Exp, bias=sc[:, 1:2], scale=SCALE)
                        A.activation(sc[:, 4:5], sinkc[:, :], ACT.Exp, bias=sc[:, 1:2]).then_inc(s_exp, 1)
                    k0 = 3 * n + c - 8
                    if k0 >= 0:
                        if k0 == 0:
                            act.wait_ge(so_stored, 1)
                            act.wait_ge(v_out, 32)
                        for k in range(2 * k0, 2 * k0 + 2):
                            A.activation(o_hi[:, k, :], q_sb[:, k, :], ACT.Copy).then_inc(o_hi_done, 1)
            for n in range(AHEAD, 2 * AHEAD):
                if AHEAD <= n + 1 < 2 * AHEAD:
                    act.wait_ge(ao_loaded[(n + 1) % 2], 32 * ((n + 1 - AHEAD) // 2 + 1))
                split_hi(U_C + n + 1, (n + 1) % 2, (n + 1) // 2 + 14, 3 * n + 111)

            def split_c(n, slot, uses):
                split_hi(n + U_C, slot, uses, n * 3 + 108)

            act.wait_ge(states_out, 16 * 7)
            with act.Fori(AHEAD, KT) as jj:
                act.wait_ge(ao_loaded[1], jj * 32 - 32)
                split_c(jj * 2 + 1, 1, jj + 14)
                for c in range(3):
                    gate_chunk(c, jj * 2, mix_of(jj)[:, CH * c:CH * c + CH])
                split_c(jj * 2 + 2, 0, jj + 15)

            def conv_gate(n, par):
                for c in range(3):
                    gate_chunk(c, n, gates2[par][c])

            split_c(17, 1, 22)
            conv_gate(16, 0)
            split_c(18, 0, 23)

            def a_split(first, end):
                act.wait_ge(a_loaded[first // 4], 16)
                for k in range(first, end):
                    A.activation(a_hi[:, k, :], a_raw[:, k, :], ACT.Copy).then_inc(a_hi_done, 1)

            a_split(0, 4)
            gate_chunk(0, 17, gates2[1][0])
            a_split(4, 6)
            gate_chunk(1, 17, gates2[1][1])
            a_split(6, 8)
            gate_chunk(2, 17, gates2[1][2])
            with act.Fori(0, (KT - 2) // 2) as i:
                for b in range(2):
                    split_c(i * 4 + (19 + 2 * b), 1, i * 2 + (23 + b))
                    split_c(i * 4 + (20 + 2 * b), 0, i * 2 + (24 + b))
                    act.wait_ge(chunk_out, i * 6 + (138 + 3 * b))
                    conv_gate(i * 4 + (19 + 2 * b), b)
            split_c(31, 1, 29)

            for i in range(4):
                act.wait_ge(wo_loaded[i], 16)
                A.activation(wo_hi[:, 2 * i:2 * i + 2, :], wo_raw[:, 2 * i:2 * i + 2, :], ACT.Copy).then_inc(wo_hi_done, 1)
            act.wait_ge(chunk_out, 159)

            def mix_split(n, par, rows, first=False):
                if not first:
                    act.wait_ge(proj_done, n - 1)
                A.activation(mix_hi[:, par, :, 0:rows], mix[:, :, bass.ds(n * P, rows)], ACT.Copy).then_inc(mix_hi_done, 1)

            def turned(n, rows):
                act.wait_ge(xnT_psum, n + 1)
                for x in range(2):
                    ins = A.activation(h2T[:, 4 * x:4 * x + 4, 0:rows], bank[4 + x][:, :].rearrange("p (k t) -> p k t", k=4)[:, :, 0:rows], ACT.Copy)
                ins.then_inc(h2T_done, 1)

            def norm2(n, par, rows):
                act.wait_ge(x2_done, n + 1)
                src = x2[0:rows, bass.ds(n, 1), :].rearrange("p a d -> p (a d)")
                A.activation(x_in[0:rows, par, :], src, ACT.Square, accum_out=ssq[0:rows, 0:1]).then_inc(sq2_done, 1)
                act.wait_ge(sq2_done, n + 1)
                A.activation(rms[0:rows, 0:1], ssq[0:rows, 0:1], ACT.Sqrt, bias=eps[0:rows, 0:1], scale=1.0 / D).then_inc(root2_done, 1)

            mix_split(0, 0, P, True)
            mix_split(1, 1, P, True)
            norm2(0, 0, P)
            mix_split(2, 0, P)
            turned(0, P)
            norm2(1, 1, P)

            def pair_d(i, rows):
                mix_split(i * 2 + 1, 1, P)
                turned(i * 2 - 1, P)
                norm2(i * 2, 0, P)
                mix_split(i * 2 + 2, 0, rows)
                turned(i * 2, P)
                norm2(i * 2 + 1, 1, P)

            with act.Fori(1, 3) as i:
                pair_d(i, P)
            pair_d(3, B8)
            turned(7, P)
            norm2(8, 0, B8)
            turned(8, B8)

            def e_split(s, slot, uses):
                act.wait_ge(e_loaded[slot], uses)
                if not isinstance(s, int) or s >= 4:
                    act.wait_ge(e_used, s - 3)
                A.activation(e_hi[:, slot % 4, :], e_raw[slot][:, :], ACT.Copy).then_inc(e_hi_done, 1)

            def x_split(e, par):
                act.wait_ge(xT_psum, e + 1)
                for x in range(2):
                    ins = A.activation(xT_hi[:, par, 4 * x:4 * x + 4, :], bank[4 + x][:, :].rearrange("p (k t) -> p k t", k=4), ACT.Copy)
                ins.then_inc(xT_hi_done, 1)

            def a_split(e):
                act.wait_ge(aT_psum, e + 1)
                A.activation(aT_hi[:, :, :], bank[6][:, :].rearrange("p (k t) -> p k t", k=4), ACT.Copy).then_inc(aT_hi_done, 1)

            def store_rows(e, s_end, first=False):
                act.wait_ge(e_used, s_end)
                if not first:
                    act.wait_ge(scattered, e * 16)
                for x in range(2):
                    ins = A.activation(y_out[:, 512 * x:512 * x + 512], bank[2 + x][:, :], ACT.Copy)
                ins.then_inc(y_stored, 1)

            def step_e(e, par, s, base, uses, first=False):
                sp_ = lambda c: e_split(s + c, (base + c) % 12, uses + 16 * ((base + c) // 12 + 1))
                if not first:
                    store_rows(e - 2, s, first=isinstance(e, int) and e == 2)
                sp_(3)
                sp_(4)
                silu_e(e, s + 2)
                a_split(e - 1)
                sp_(5)
                sp_(6)
                sp_(7)
                if isinstance(e, int) and e == NE - 1:
                    return
                x_split(e + 1, 1 - par)
                sp_(8)

            def silu_e(e, s):
                act.wait_ge(e_used, s)
                if not isinstance(e, int) or e > 0:
                    act.wait_ge(act_done, e)
                A.activation(sg[:, :], bank[0][:, :], ACT.Silu).then_inc(silu_done, 1)

            act.wait_ge(wsum_done, 1)
            A.activation(gl[:, :, :], gl[:, :, :], ACT.Exp)
            A.activation(wts[:, :, 1], wts[:, :, 1], ACT.Exp).then_inc(wexp_done, 1)
            act.wait_ge(proj_done, NT)
            e_split(0, 0, 16)
            x_split(0, 0)
            for c in range(1, 5):
                e_split(c, c, 16)
            silu_e(0, 2)
            e_split(5, 5, 16)
            x_split(1, 1)
            e_split(6, 6, 16)
            step_e(1, 1, 4, 4, 0, first=True)
            step_e(2, 0, 10, 10, 0)
            with act.Fori(1, 15) as i:
                step_e(i * 2 + 1, 1, i * 12 + 4, 4, i * 16)
                step_e(i * 2 + 2, 0, i * 12 + 10, 10, i * 16)
            step_e(31, 1, 184, 4, 240)
            store_rows(30, 190)
            a_split(31)
            store_rows(31, 192)

            n_ov = act.value_load(ov_t[0:1, 2 * OVF:2 * OVF + 1], min_val=0, max_val=OVF)
            with act.If(n_ov > 0):
                with act.Fori(0, OVF) as i:
                    with act.If(i < n_ov):
                        act.wait_ge(v_gu, i + 1)
                        A.activation(sg[:, :], bank[0][:, :], ACT.Silu).then_inc(v_silu, 1)
                        act.wait_ge(v_ypsum, i + 1)
                        act.wait_ge(v_free, i + 1)
                        for x in range(2):
                            ins = A.activation(y_out[:, 512 * x:512 * x + 512], bank[2 + x][:, :], ACT.Copy)
                        ins.then_inc(v_y, 1)

            act.wait_ge(rows_written, 1)
            for n in range(NT):
                rows = P if n < 8 else B8
                act.wait_ge(f_sum, n + 1)
                A.activation(f_junk[0:rows, :], f_out[0:rows, n, :], ACT.Square, accum_out=ssq[0:rows, n:n + 1]).then_inc(f_sq, 1)
                act.wait_ge(f_sq, n + 1)
                A.activation(rms[0:rows, n:n + 1], ssq[0:rows, n:n + 1], ACT.Sqrt, bias=eps[0:rows, 0:1], scale=1.0 / D).then_inc(f_root, 1)

        @block.vector
        def _(dve):
            V = nc.vector
            step = Steps(dve, dve_step)

            def split_lo(u, slot):
                dve.wait_ge(hi_ready, u + 1)
                V.tensor_tensor(w_lo[:, slot, :, :], w_raw[slot][:, :, :], w_hi[:, slot, :, :].bitcast(F32), ALU.subtract).then_inc(lo_ready, 1)

            step.after(V.memset(relb[:, :], 1.0))
            V.memset(list_init[:, :], NOROW).then_inc(list_filled, 1)
            V.memset(eps[:, :], EPS)
            V.memset(ssq[:, :], 1.0).then_inc(relb_ones, 1)
            dve.wait_ge(start_psum, 1)
            V.tensor_copy(cols32[:, :], bank[7][:, 0:32]).then_inc(start_copied, 1)
            for g in range(3):
                rows, w = (P, 4) if g < 2 else (B8, 1)
                dve.wait_ge(sqrt_done, g + 1)
                r = rms[0:rows, 4 * g:4 * g + w]
                step.after(V.reciprocal(r, r))
                for n in range(4 * g, 4 * g + w):
                    V.tensor_scalar(x_tok[0:rows, n, :], x_tok[0:rows, n, :], rms[0:rows, n:n + 1], None, ALU.mult).then_inc(x_scaled, 1)
            for g in range(2):
                for k in range(KT):
                    dve.wait_ge(h_hi_done, KT * g + k + 1)
                    cols = slice(512 * g, 512 * g + 512)
                    V.scalar_tensor_tensor(h_lo[:, k, cols], bank[k][:, :], g1[:, k:k + 1], h_hi[:, k, cols].bitcast(F32),
                                           ALU.mult, ALU.subtract).then_inc(h_lo_done, 1)
                if g == 0:
                    split_lo(0, 0)
            dve.wait_ge(xT_ready, 17)
            step.after(V.tensor_tensor(tmp8[:, :, :], bank[3][:, 0:64].rearrange("p (k b) -> p k b", k=KT),
                                       g1[:, :].unsqueeze(2).to_broadcast([P, KT, B8]), ALU.mult))
            step.after(V.tensor_copy(h_hi[:, :, S:T], tmp8[:, :, :]))
            V.tensor_tensor(h_lo[:, :, S:T], tmp8[:, :, :], h_hi[:, :, S:T].bitcast(F32), ALU.subtract).then_inc(h_lo_done, 1)
            dve.wait_ge(consts_loaded, 16 * N_CONSTS)
            V.tensor_copy(hot_r[0:33, :], hot[0:33, 0:SKEW])
            step.after(V.tensor_copy(relb_hi[0:33, :], relb[0:33, :]))
            V.tensor_tensor(relb_lo[0:33, :], relb[0:33, :], relb_hi[0:33, :].bitcast(F32), ALU.subtract)
            relc_v = relc[0:33, :].rearrange("p (g b j) -> p g b j", g=4, b=8)
            for b in range(B8):
                ins = V.tensor_copy(relc_v[:, :, b, :], relb[0:33, :].rearrange("p (g j) -> p g j", g=4))
            ins.then_inc(relb_split, 1)
            step.after(V.tensor_copy(sinkp[:, :].rearrange("p (t j h) -> p t h j", t=2, j=4), sinkb[:, :].rearrange("p (t h j) -> p t h j", t=2, h=2)))
            step.after(V.tensor_scalar(sink8[:, :], sinkp[:, :], 1 / SCALE, None, ALU.mult))
            step.after(V.tensor_tensor_reduce(tmp8[:, 0:2, :].rearrange("p a b -> p (a b)"), sinkb[:, :], tab[:, C_HM:C_HM + 16], 1.0, 0.0, ALU.mult, ALU.add, sinkc[:, :]))

            def units_a(t, first):
                for i in range(5):
                    split_lo(t * 5 + (i + 1), (1, 2, 0, 1, 0)[i])
                    for c in range(3):
                        dve.wait_ge(chunk_done, t * 15 + (3 * i + c + 1))
                        dst = q_sb[:, bass.ds(t * 4 + i, 1), CH * c:CH * c + CH] if i < 4 else k_sb[:, bass.ds(t, 1), CH * c:CH * c + CH]
                        V.tensor_copy(dst, DN[c][:, 0:CH].unsqueeze(1)).then_inc(chunk_out, 1)
                        if first and (i or c):
                            keep_bias(3 * i + c - 1)

            def keep_bias(h):
                dve.wait_ge(bias_psum, h + 1)
                V.tensor_copy(bias_row[:, h, :], bank[3 + h % 4][:, 0:SKEW]).then_inc(bias_row_done, 1)

            units_a(0, True)
            keep_bias(14)
            keep_bias(15)
            dve.wait_ge(start_psum, 2)
            V.tensor_copy(bs8[:, :], bank[7][:, 0:129])
            V.tensor_copy(histT[:, :, :, :], bank[7][:, 256:256 + P].rearrange("p (k b r) -> p k r b", k=KT, b=B8))
            with dve.Fori(1, 2) as t:
                units_a(t, False)
            split_lo(U_V + 1, 1)
            for n in range(NT):
                rows = P if n < 8 else B8
                dve.wait_ge(chunk_done, 31 + n)
                V.tensor_copy(v_sb[0:rows, n, :], DN[n % 3][0:rows, 0:256]).then_inc(chunk_out, 1)
            split_lo(U_B, 0)
            dve.wait_ge(bias_loaded, 16)
            step.after(V.memset(u_sb[:, 0:2], 0.0))

            def invert_sums(i, b):
                dve.wait_ge(probs_ready, b * 8 + (i + 1))
                pair = slice(2 * i, 2 * i + 2)
                step.after(V.tensor_tensor(rden[:, pair], den[:, pair], esink[:, pair], ALU.add))
                V.reciprocal(rden[:, pair], rden[:, pair]).then_inc(sums_inverted, 1)

            def step_b(j, first):
                off = P if first else 0
                w = [cols32[:, bass.ds(j + (8 + 8 * i), 1)] for i in range(3)]

                def leave(i):
                    cols = slice(2 + CH * (i % 3), 2 + CH * (i % 3) + CH)
                    dve.wait_ge(chunk_done, j * 9 + (39 + i + 1))
                    if i < 3:
                        V.tensor_copy(u_sb[:, cols], DN[i % 3][:, 0:CH]).then_inc(chunk_out, 1)
                    elif i < 6:
                        dve.wait_ge(chunk_out, j * 9 + (39 + i - 2))
                        V.tensor_tensor(u_sb[:, cols], u_sb[:, cols], DN[i % 3][:, 0:CH], ALU.mult).then_inc(chunk_out, 1)
                        if i == 5:
                            dve.wait_ge(chunk_out, j * 9 + (39 + 6))
                    else:
                        y = y_sb[:, CH * (i % 3):CH * (i % 3) + CH]
                        V.tensor_tensor(y, y, DN[i % 3][:, 0:CH], ALU.mult).then_inc(chunk_out, 1)

                for i in range(9):
                    if i < 8:
                        dve.wait_ge(scores_ready, j * 8 + (i + 1))
                        if not (first and i < 2):
                            dve.wait_ge(probs_turned, j * 8 + (i - 1))
                        V.memset(carrier[:, :], 0.0)
                        for h in range(2):
                            n = 2 * i + h
                            ins = V.tensor_tensor_reduce(probs[:, i % 2, h, off:256], SCB[h][:, 256 * (i % 2) + off:256 * (i % 2) + 256],
                                                         bias_sb[:, 8 * (i // 4) + i % 4 + 4 * h, off:256], 1.0, sink8[:, n:n + 1],
                                                         ALU.add, ALU.max, maxs[:, n:n + 1])
                        step.after(ins)
                        pair = slice(2 * i, 2 * i + 2)
                        step.after(V.tensor_scalar(negm[:, pair], maxs[:, pair], -SCALE, None, ALU.mult))
                        V.tensor_tensor(sinkd[:, pair], sinkp[:, pair], negm[:, pair], ALU.add).then_inc(max_ready, 1)
                    if i == 1:
                        dve.wait_ge(v_hi_done, j + 1)
                        if first:
                            V.tensor_tensor(v_lo[:, 1, :], v_sb[:, 0, :], v_hi[:, 1, :].bitcast(F32), ALU.subtract).then_inc(v_lo_done, 1)
                        else:
                            V.tensor_tensor(v_lo[:, :, :], v_sb[:, bass.ds(j - 1, 2), :], v_hi[:, :, :].bitcast(F32), ALU.subtract).then_inc(v_lo_done, 1)
                    if i < 8:
                        invert_sums(i, j)
                    if i > 0:
                        st = i - 1
                        dve.wait_ge(probsT_hi_done, j * 8 + (st + 1))
                        turned = PTB[:, :].rearrange("p (h k t) -> p h k t", h=2, k=2)
                        kts = slice(1 if first else 0, 2)
                        V.tensor_tensor(probsT_lo[:, :, kts, st % 2, :], turned[:, :, kts, :], probsT_hi[:, :, kts, st % 2, :].bitcast(F32),
                                        ALU.subtract).then_inc(probsT_lo_done, 1)
                    hist = [histT[:, bass.ds(j, 1), r, :].rearrange("p a b -> p (a b)") for r in range(2)]
                    if i == 6:
                        if not first:
                            dve.wait_ge(a_spilled, j * 16)
                        V.tensor_copy(ustate[:, bass.ds(j, 1), :], u_sb[:, S:S + 10].unsqueeze(1))
                        V.tensor_scalar(y_sb[:, 0:S], u_sb[:, 0:S], w[0], None, ALU.mult)
                        step.after(V.tensor_scalar(y_sb[:, S:T], hist[0], w[0], None, ALU.mult))
                        V.scalar_tensor_tensor(y_sb[:, 0:S], u_sb[:, 1:S + 1], w[1], y_sb[:, 0:S], ALU.mult, ALU.add)
                        step.after(V.scalar_tensor_tensor(y_sb[:, S:T], hist[1], w[1], y_sb[:, S:T], ALU.mult, ALU.add))
                    if i == 7:
                        step.after(V.scalar_tensor_tensor(y_sb[:, :], u_sb[:, 2:T + 2], w[2], y_sb[:, :], ALU.mult, ALU.add))
                        leave(6)
                    if i != 6:
                        leave(i)
                    if i % 3 == 0:
                        split_lo(j * 3 + (U_B + i // 3 + 1), (i // 3 + 1) % 3)
                return step.n

            n0 = step.n
            per = step_b(0, True) - n0
            n1 = step.n
            with dve.Fori(1, KT) as j:
                step.n = j * per + (n1 - per)
                step_b(j, False)
            step.n = n1 + (KT - 1) * per

            split_lo(U_C + 1, 1)
            for i, (dst, src) in enumerate(((k_out[:, 0, :], bank[3][:, 0:256]), (k_out[0:B8, 1, :], bank[4][0:B8, 0:256]),
                                            (u_out[0:10, 0:512], bank[5][0:10, :]), (u_out[0:10, 512:D], bank[7][0:10, :]))):
                dve.wait_ge(win_psum, i + 1)
                if i == 0:
                    dve.wait_ge(a_spilled, 16 * KT)
                V.tensor_copy(dst, src).then_inc(win_copied, 1)
            for t in range(2):
                ins = V.tensor_copy(q_new[:, t, :].rearrange("p (b j) -> p j b", j=4), q_sb[:, 4 * t:4 * t + 4, S:T])
            ins.then_inc(q_new_done, 1)
            split_lo(U_C + 2, 0)
            dve.wait_ge(kcT_psum, 4)
            step.after(V.memset(q_of[:, :, :, :], 0.0))
            for b in range(B8):
                ins = V.tensor_copy(q_of[:, :, b, 4 * b:4 * b + 4], q_new[:, :, 4 * b:4 * b + 4])
            ins.then_inc(q_of_done, 1)
            dve.wait_ge(s_psum, 2)
            step.after(V.tensor_tensor_reduce(pn8[:, :], bank[6][:, 0:B8], tab[:, C_MB:C_MB + 8], 1.0, 0.0, ALU.mult, ALU.add, sc[:, 0:1]))
            step.after(V.tensor_tensor(sc[:, 0:1], sc[:, 0:1], bs8[:, 128:129], ALU.add))
            step.after(V.scalar_tensor_tensor(sc[:, 5:6], sinkc[:, :], 1 / SCALE, sc[:, 0:1], ALU.mult, ALU.max))
            for g in range(KV):
                r = slice(32 * g, 32 * g + 32)
                ins = V.tensor_tensor_reduce(s_rows[r, :], bank[4 - g % 2][r, 0:P], bs8[r, 0:P], 1.0, sc[r, 5:6], ALU.add, ALU.max, sc[r, 6:7])
            step.after(ins)
            V.tensor_scalar(sc[:, 1:2], sc[:, 6:7], -SCALE, None, ALU.mult).then_inc(s_max, 1)
            dve.wait_ge(s_exp, 1)
            step.after(V.tensor_tensor(sc[:, 7:8], sc[:, 2:3], sc[:, 3:4], ALU.add))
            step.after(V.tensor_tensor(sc[:, 7:8], sc[:, 7:8], sc[:, 4:5], ALU.add))
            step.after(V.reciprocal(sc[:, 7:8], sc[:, 7:8]))
            V.tensor_scalar(s_rows[:, :], s_rows[:, :], sc[:, 7:8], None, ALU.mult)
            V.tensor_scalar(pn8[:, :], tab[:, C_MB:C_MB + 8], sc[:, 3:4], sc[:, 7:8], ALU.mult, ALU.mult).then_inc(s_normed, 1)
            split_lo(U_C + 3, 1)
            dve.wait_ge(pT_psum, 1)
            V.tensor_copy(pT[:, :], bank[7][:, 0:P])
            V.tensor_copy(pn8T[0:B8, :], bank[7][0:B8, P:2 * P]).then_inc(pT_copied, 1)
            dve.wait_ge(so_psum, 1)
            for x in range(2):
                src = bank[4][64 * x:64 * x + 64, 0:P].rearrange("p (t x b j) -> p t x j b", t=2, x=2, b=B8)[:, :, x, :, :]
                dst = q_sb[64 * x:64 * x + 64, :, S:T].rearrange("p (t j) b -> p t j b", t=2)
                ins = V.tensor_copy(dst, src)
            ins.then_inc(so_stored, 1)
            split_lo(U_C + 4, 0)
            for k in range(KT):
                dve.wait_ge(o_hi_done, k + 1)
                V.tensor_tensor(o_lo[:, k, :], q_sb[:, k, :], o_hi[:, k, :].bitcast(F32), ALU.subtract).then_inc(o_lo_done, 1)

            def projected(n, j):
                for c in range(3):
                    cols = slice(CH * c, CH * c + CH)
                    dve.wait_ge(chunk_done, n * 3 + (111 + c + 1))
                    m = mix[:, bass.ds(j, 1), cols].rearrange("p a t -> p (a t)")
                    V.tensor_tensor(m, m, DN[c][:, 0:CH], ALU.mult).then_inc(chunk_out, 1)

            for n in range(AHEAD, 2 * AHEAD):
                split_lo(U_C + n + 1, (n + 1) % 2)
                projected(n, n - AHEAD)

            def conv_projected(n, j, par, after=None):
                for c in range(3):
                    g = gates2[par][c]
                    dve.wait_ge(chunk_done, n * 3 + (111 + c + 1))
                    m = mix[:, bass.ds(j, 1), CH * c:CH * c + CH].rearrange("p a t -> p (a t)")
                    step.after(V.tensor_tensor(g, g, DN[c][:, 0:CH], ALU.mult))
                    V.tensor_tensor(m, m, g, ALU.add).then_inc(chunk_out, 1)
                    if after is not None:
                        after(c)

            with dve.Fori(AHEAD, KT) as jj:
                split_lo(jj * 2 + (U_C + 1), 1)
                split_lo(jj * 2 + (U_C + 2), 0)
                projected(jj * 2 + 1, jj)
            split_lo(U_C + 17, 1)
            split_lo(U_C + 18, 0)
            for k in range(KT):
                dve.wait_ge(a_hi_done, k + 1)
                V.tensor_tensor(a_lo[:, k, :], a_raw[:, k, :], a_hi[:, k, :].bitcast(F32), ALU.subtract).then_inc(a_lo_done, 1)
            n0 = step.n
            with dve.Fori(0, (KT - 2) // 2) as i:
                step.n = i * 6 + n0
                for b in range(2):
                    split_lo(i * 4 + (U_C + 19 + 2 * b), 1)
                    conv_projected(i * 4 + (18 + 2 * b), i * 2 + b, b)
                    split_lo(i * 4 + (U_C + 20 + 2 * b), 0)
            step.n = n0 + 3 * (KT - 2)
            split_lo(U_C + 31, 1)

            def wo_split(i):
                dve.wait_ge(wo_hi_done, i + 1)
                V.tensor_tensor(wo_lo[:, 2 * i:2 * i + 2, :], wo_raw[:, 2 * i:2 * i + 2, :], wo_hi[:, 2 * i:2 * i + 2, :].bitcast(F32),
                                ALU.subtract).then_inc(wo_lo_done, 1)

            conv_projected(30, KT - 2, 0, lambda c: wo_split(0) if c == 2 else None)
            conv_projected(31, KT - 1, 1, lambda c: wo_split(c + 1) if c < 2 else None)

            V.memset(lg[:, NG:8], -3e38)
            V.memset(seen[:, :], 0.0)
            V.memset(gl[:, :, :], 0.0)
            V.memset(tv[:, :, :], 0.0)
            V.tensor_copy(tok_u[:, :], tab[:, C_TOK:C_TOK + 2 * NT]).then_inc(seen_done, 1)
            def mix_split(n, par, rows):
                dve.wait_ge(mix_hi_done, n + 1)
                V.tensor_tensor(mix_lo[:, par, :, 0:rows], mix[:, :, bass.ds(n * P, rows)], mix_hi[:, par, :, 0:rows].bitcast(F32),
                                ALU.subtract).then_inc(mix_lo_done, 1)

            def residual(n, par, rows, uses):
                dve.wait_ge(proj_done, n + 1)
                dve.wait_ge(x_again[par], uses)
                dst = x2[0:rows, bass.ds(n, 1), :].rearrange("p a d -> p (a d)")
                for x in range(2):
                    half = slice(512 * x, 512 * x + 512)
                    ins = V.tensor_tensor(dst[:, half], bank[2 * par + x][0:rows, :], x_in[0:rows, par, half], ALU.add)
                ins.then_inc(x2_done, 1)

            def second_norm(n, rows, first=False):
                dve.wait_ge(root2_done, n + 1)
                step.after(V.reciprocal(rms[0:rows, 1:2], rms[0:rows, 0:1]))
                if not first:
                    dve.wait_ge(xn_written, n * 16)
                    dve.wait_ge(xnT_psum, n)
                src = x2[0:rows, bass.ds(n, 1), :].rearrange("p a d -> p (a d)")
                V.scalar_tensor_tensor(xn[0:rows, :], src, rms[0:rows, 1:2], g2b[0:rows, :], ALU.mult, ALU.mult).then_inc(xn_done, 1)

            def carry():
                V.memset(carrier[:, :], 0.0)

            def choose(n, par, r):
                dve.wait_ge(logits_done, n + 1)
                V.tensor_tensor(lg[0:r, 0:NG], bank[6][0:r, 0:NG], rb[0:r, 0:NG], ALU.add)
                step.after(V.tensor_tensor(lg[0:r, 8:40], bank[6][0:r, NG:36], rb[0:r, NG:36], ALU.add))
                carry()
                step.after(V.max(top_g[0:r, :], lg[0:r, 0:8]))
                carry()
                step.after(V.max_index(idx_g[0:r, :], top_g[0:r, :], lg[0:r, 0:8]))
                V.tensor_scalar(gl[0:r, bass.ds(n, 1), :].rearrange("p a g -> p (a g)"), lg[0:r, 0:NG], top_g[0:r, 0:1], None, ALU.subtract)
                step.after(V.tensor_copy(grp[0:r, 0:1], idx_g[0:r, 0:1]))
                V.tensor_scalar(grp[0:r, 1:2], grp[0:r, 0:1], float(EG), None, ALU.mult)
                step.after(V.tensor_scalar(oh4[0:r, :], tab[0:r, C_IO:C_IO + NG], grp[0:r, 0:1], None, ALU.is_equal))
                step.after(V.tensor_tensor(prod[0:r, :, :], lg[0:r, 8:40].rearrange("p (g e) -> p e g", g=NG),
                                           oh4[0:r, :].unsqueeze(1).to_broadcast([r, EG, NG]), ALU.mult))
                step.after(V.tensor_reduce(e8[0:r, :], prod[0:r, :, :], AX.X, ALU.add))
                carry()
                step.after(V.max(top_e[0:r, :], e8[0:r, :]))
                V.tensor_copy(tv[0:r, bass.ds(n, 1), :], top_e[0:r, 0:2].unsqueeze(1))
                step.after(V.max_index(idx_e[0:r, :], top_e[0:r, :], e8[0:r, :]))
                step.after(V.tensor_copy(idx_f[0:r, :], idx_e[0:r, 0:2]))
                step.after(V.tensor_scalar(picked[0:r, par, :], idx_f[0:r, :], grp[0:r, 1:2], None, ALU.add))
                for k in range(2):
                    ins = V.tensor_scalar(hots[0:r, par, k, :], tab[0:r, C_IO:C_IO + NE], picked[0:r, par, k:k + 1], None, ALU.is_equal)
                step.after(ins)
                V.tensor_tensor(picks[0:r, par, :], hots[0:r, par, 0, :], hots[0:r, par, 1, :], ALU.add).then_inc(picks_done, 1)

            def address(n, par, r):
                dve.wait_ge(rank_done, n + 1)
                carry()
                for k in range(2):
                    ins = V.tensor_tensor_reduce(prod[0:r, :, :].rearrange("p a b -> p (a b)"), hots[0:r, par, k, :], bank[7][0:r, 0:NE],
                                                 1.0, 0.0, ALU.mult, ALU.add, rank2[0:r, k:k + 1])
                    step.after(ins)
                step.after(V.scalar_tensor_tensor(adr_f[0:r, :], rank2[0:r, :], float(NE), picked[0:r, par, :], ALU.mult, ALU.add))
                V.tensor_copy(adr[0:r, bass.ds(n * 2, 2)], adr_f[0:r, :]).then_inc(adr_done, 1)
                V.tensor_tensor(seen[0:r, :], seen[0:r, :], picks[0:r, par, :], ALU.add).then_inc(seen_done, 1)

            mix_split(0, 0, P)
            wo_split(3)
            mix_split(1, 1, P)
            dve.wait_ge(router_loaded, 80)
            residual(0, 0, P, 16)
            second_norm(0, P, True)
            mix_split(2, 0, P)
            residual(1, 1, P, 16)
            choose(0, 0, P)
            second_norm(1, P)
            mix_split(3, 1, P)
            address(0, 0, P)
            n0 = step.n

            def pair_d(i, rows):
                residual(i * 2, 0, P, i * 16 + 16)
                choose(i * 2 - 1, 1, P)
                second_norm(i * 2, P)
                mix_split(i * 2 + 2, 0, rows)
                address(i * 2 - 1, 1, P)
                residual(i * 2 + 1, 1, P, i * 16 + 16)
                choose(i * 2, 0, P)
                second_norm(i * 2 + 1, P)
                if rows == P:
                    mix_split(i * 2 + 3, 1, P)
                address(i * 2, 0, P)

            pair_steps = 32
            with dve.Fori(1, 3) as i:
                step.n = i * pair_steps + (n0 - pair_steps)
                pair_d(i, P)
            step.n = n0 + 2 * pair_steps
            pair_d(3, B8)
            assert step.n == n0 + 3 * pair_steps
            residual(8, 0, B8, 80)
            choose(7, 1, P)
            second_norm(8, B8)
            address(7, 1, P)
            choose(8, 0, B8)
            address(8, 0, B8)

            dve.wait_ge(ov_psum, 1)
            step.after(V.tensor_copy(cnt[0:NE, 0:1], bank[6][0:NE, 0:1]))
            V.tensor_scalar(ov_a[0:NE, 0, 0:8], tab[0:NE, C_B128:C_B128 + 8], cnt[0:NE, 0:1], 0.0, ALU.is_lt, ALU.add,
                            accum_out=cnt[0:NE, 1:2]).then_inc(ov_sbuf, 1)
            dve.wait_ge(ov_psum, 2)
            step.after(V.tensor_copy(cnt[0:NE, 2:3], bank[7][0:NE, 0:1]))
            step.after(V.tensor_tensor(cnt[0:NE, 3:4], cnt[0:NE, 2:3], cnt[0:NE, 1:2], ALU.add))
            i16 = tab[0:NE, C_I16:C_I16 + OVF]
            V.tensor_scalar(ov_a[0:NE, 2, :], i16, cnt[0:NE, 2:3], 1.0, ALU.subtract, ALU.add)
            step.after(V.tensor_scalar(ov_a[0:NE, 1, :], i16, cnt[0:NE, 3:4], None, ALU.is_lt))
            step.after(V.scalar_tensor_tensor(ov_a[0:NE, 0, :], i16, cnt[0:NE, 2:3], ov_a[0:NE, 1, :], ALU.is_ge, ALU.mult))
            V.tensor_scalar(ov_b[0:NE, 0:OVF], ov_a[0:NE, 0, :], tab[0:NE, C_PIX:C_PIX + 1], None, ALU.mult)
            V.tensor_tensor(ov_b[0:NE, OVF:2 * OVF], ov_a[0:NE, 0, :], ov_a[0:NE, 2, :], ALU.mult)
            V.tensor_copy(ov_b[0:NE, 2 * OVF:2 * OVF + 1], cnt[0:NE, 1:2]).then_inc(ov_sbuf, 1)
            dve.wait_ge(ov_psum, 3)
            V.tensor_copy(ov_t[0:1, :], bank[6][0:1, 0:2 * OVF + 1]).then_inc(ov_sbuf, 1)

            def source_rows(dst, src, f, g):
                step.after(V.tensor_copy(f, src))
                step.after(V.tensor_scalar(g, f, float(T), -float(T), ALU.is_ge, ALU.mult))
                return V.tensor_tensor(dst, f, g, ALU.add)

            dve.wait_ge(list_loaded, 16)
            source_rows(gidx[:, :], lst[:, :], lst_f[:, :], lst_g[:, :]).then_inc(gidx_done, 1)
            step.after(V.tensor_tensor(wts[:, :, 1], tv[:, :, 1], tv[:, :, 0], ALU.subtract))
            V.memset(carrier[:, :], 0.0).then_inc(wsum_done, 1)
            dve.wait_ge(wexp_done, 1)
            step.after(V.tensor_reduce(wsum[:, :], gl[:, :, :], AX.X, ALU.add))
            step.after(V.scalar_tensor_tensor(wsum[:, :], wts[:, :, 1], 1.0, wsum[:, :], ALU.add, ALU.mult))
            step.after(V.reciprocal(wts[:, :, 0], wsum[:, :]))
            step.after(V.tensor_tensor(wts[:, :, 1], wts[:, :, 1], wts[:, :, 0], ALU.mult))

            def e_split(s, slot):
                dve.wait_ge(e_hi_done, s + 1)
                V.tensor_tensor(e_lo[slot][:, :], e_raw[slot][:, :], e_hi[:, slot % 4, :].bitcast(F32), ALU.subtract).then_inc(e_lo_done, 1)

            def x_split(e, par):
                dve.wait_ge(xT_hi_done, e + 1)
                for x in range(2):
                    ins = V.tensor_tensor(xT_lo[:, par, 4 * x:4 * x + 4, :], bank[4 + x][:, :].rearrange("p (k t) -> p k t", k=4),
                                          xT_hi[:, par, 4 * x:4 * x + 4, :].bitcast(F32), ALU.subtract)
                ins.then_inc(xT_lo_done, 1)

            def a_split(e):
                dve.wait_ge(aT_hi_done, e + 1)
                V.tensor_tensor(aT_lo[:, :, :], bank[6][:, :].rearrange("p (k t) -> p k t", k=4), aT_hi[:, :, :].bitcast(F32),
                                ALU.subtract).then_inc(aT_lo_done, 1)

            def activate(e, s):
                dve.wait_ge(e_used, s)
                dve.wait_ge(silu_done, e + 1)
                if not isinstance(e, int) or e > 0:
                    dve.wait_ge(aT_psum, e)
                V.tensor_tensor(act_sb[:, :], sg[:, :], bank[1][:, :], ALU.mult).then_inc(act_done, 1)

            def step_e(e, par, s, base):
                sp_ = lambda c: e_split(s + c, (base + c) % 12)
                sp_(3)
                sp_(4)
                a_split(e - 1)
                sp_(5)
                sp_(6)
                activate(e, s + 4)
                sp_(7)
                if isinstance(e, int) and e == NE - 1:
                    return
                x_split(e + 1, 1 - par)
                sp_(8)

            e_split(0, 0)
            x_split(0, 0)
            for c in range(1, 6):
                e_split(c, c)
            activate(0, 4)
            x_split(1, 1)
            e_split(6, 6)
            with dve.Fori(0, 15) as i:
                step_e(i * 2 + 1, 1, i * 12 + 4, 4)
                step_e(i * 2 + 2, 0, i * 12 + 10, 10)
            step_e(31, 1, 184, 4)
            a_split(31)

            n_ov = dve.value_load(ov_t[0:1, 2 * OVF:2 * OVF + 1], min_val=0, max_val=OVF)
            n0 = step.n
            with dve.If(n_ov > 0):
                with dve.Fori(0, OVF) as i:
                    with dve.If(i < n_ov):
                        step.n = i * 2 + n0
                        dve.wait_ge(v_col, i * 16 + 16)
                        source_rows(gcol[:, 0:1], scol[:, 0:1], lst_f[:, 0:1], lst_g[:, 0:1]).then_inc(v_idx, 1)
                        dve.wait_ge(v_xpsum, i + 1)
                        for x in range(2):
                            ins = V.tensor_copy(v_xT[:, 4 * x:4 * x + 4, :], bank[4 + x][:, :].rearrange("p (k t) -> p k t", k=4))
                        ins.then_inc(v_xT_done, 1)
                        dve.wait_ge(v_silu, i + 1)
                        V.tensor_tensor(act_sb[:, :], sg[:, :], bank[1][:, :], ALU.mult).then_inc(v_act, 1)
                        dve.wait_ge(v_apsum, i + 1)
                        V.tensor_copy(v_aT[:, :, :], bank[6][:, :].rearrange("p (k t) -> p k t", k=4)).then_inc(v_aT_done, 1)


            dve.wait_ge(gf_loaded, 16)

            final = Steps(dve, final_step)

            def rows_of(n):
                return P if n < 8 else B8

            def combine(n):
                r = rows_of(n)
                dve.wait_ge(f_loaded[n], F_FROM + 32)
                out = f_out[0:r, n, :]
                final.after(V.scalar_tensor_tensor(out, f_y[0][0:r, n, :], wts[0:r, n, 0:1], x2[0:r, n, :], ALU.mult, ALU.add))
                V.scalar_tensor_tensor(out, f_y[1][0:r, n, :], wts[0:r, n, 1:2], out, ALU.mult, ALU.add).then_inc(f_sum, 1)

            def finish(n):
                r = rows_of(n)
                dve.wait_ge(f_root, n + 1)
                final.after(V.reciprocal(rms[0:r, n:n + 1], rms[0:r, n:n + 1]))
                V.scalar_tensor_tensor(f_out[0:r, n, :], f_out[0:r, n, :], rms[0:r, n:n + 1], gfb[0:r, :], ALU.mult, ALU.mult).then_inc(f_done, 1)

            for n in range(NT + 1):
                if n < NT:
                    combine(n)
                if n > 0:
                    finish(n - 1)


_INS = ["x_prompt", "x_sample", "cache_conv", "cache_k", "cache_v", "norm1_g", "w_in", "conv_w", "w_conv_out",
        "w_attn_out", "w_o", "sinks", "rel_bias", "norm2_g", "w_router_group", "b_router_group",
        "w_router_expert", "b_router_expert", "w_e_gate", "w_e_up", "w_e_down", "norm_f_g"]
_OUTS = [(1, S, D), (B8, 1, D), (1, 1, 2, D), (1, 1, WIN, KV, HD), (1, 1, WIN, KV, HD),
         (1, B8, 2, D), (1, B8, WIN, KV, HD), (1, B8, WIN, KV, HD)]


def kernel(**inputs):
    import numpy as _np
    import concourse.bacc as _bacc
    from concourse import mybir as _mybir
    from concourse.bass_utils import run_bass_kernel_spmd as _run

    nc = _bacc.Bacc("TRN2", target_bir_lowering=False, num_devices=1)
    table, onehot = constants()
    arrays, args = {}, []
    for name in _INS + ["table", "onehot"]:
        a = table if name == "table" else onehot if name == "onehot" else _np.ascontiguousarray(inputs[name])
        arrays[f"in_{name}_dram"] = a
        args.append(nc.dram_tensor(f"in_{name}_dram", a.shape, _mybir.dt.from_np(a.dtype), kind="ExternalInput").ap())
    for i, shape in enumerate(_OUTS):
        args.append(nc.dram_tensor(f"out_{i}_dram", shape, _mybir.dt.float32, kind="ExternalOutput").ap())
    program(nc, *args)
    r = _run(nc, [arrays], core_ids=[0])
    return tuple(r.results[0][f"out_{i}_dram"] for i in range(len(_OUTS)))
```
